# Optimizing a Trainium2 kernel written in Bass

```python
import math
import jax, jax.numpy as jnp
from jax import lax
import numpy as np

D_MODEL = 1024
BATCH = 1
SEQ = 1024
DEPTH = 1

N_HEADS_ATTN = 8
N_KV_GROUPS = 2
HEADS_PER_GROUP = N_HEADS_ATTN // N_KV_GROUPS
HEAD_DIM = 64
ATTN_WIDTH = N_HEADS_ATTN * HEAD_DIM
KV_WIDTH = N_KV_GROUPS * HEAD_DIM
CMP_BLOCK = 32
CMP_STRIDE = 16
CMP_HIDDEN = 2 * HEAD_DIM
SEL_BLOCK = 64
N_SEL = 16
WINDOW = 512
SEL_QCHUNK = 32
WIN_QBLOCK = 128
ROPE_THETA = 10000.0
FORCE_SCORE = 1.0e4
MASK_VALUE = -1.0e30

SSM_WIDTH = 256
SSM_GROUP = 16
SSM_GROUPS = SSM_WIDTH // SSM_GROUP
SSM_STATE = 64
DT_MIN = 0.001
DT_MAX = 0.1

NORM_EPS = 1e-6
N_BRANCHES = 2
IN_SPLITS = (ATTN_WIDTH, 6 * KV_WIDTH, 3 * N_HEADS_ATTN, ATTN_WIDTH,
             SSM_WIDTH, SSM_WIDTH, N_BRANCHES * D_MODEL)
IN_WIDTH = sum(IN_SPLITS)
IN_OFFSETS = tuple(int(v) for v in np.cumsum(IN_SPLITS)[:-1])

kernel_name = "hybrid_nsa_s5_gated_block"

def rms_norm(x, gain):
    xf = x.astype(jnp.float32)
    y = xf * lax.rsqrt(jnp.mean(xf * xf, axis=-1, keepdims=True) + NORM_EPS)
    return (y * gain.astype(jnp.float32)).astype(x.dtype)

def rope_tables(seq, dtype):
    half = HEAD_DIM // 2
    inv_freq = ROPE_THETA ** (-jnp.arange(half, dtype=jnp.float32) / half)
    ang = jnp.arange(seq, dtype=jnp.float32)[:, None] * inv_freq[None, :]
    return jnp.cos(ang).astype(dtype), jnp.sin(ang).astype(dtype)

def apply_rope(t, cos, sin):
    t1, t2 = jnp.split(t, 2, axis=-1)
    c = cos[:, None, :]
    s = sin[:, None, :]
    return jnp.concatenate([t1 * c - t2 * s, t2 * c + t1 * s], axis=-1)

def compress_blocks(t, pe, w1, b1, w2):
    b, s, g, dh = t.shape
    nc = (s - CMP_BLOCK) // CMP_STRIDE + 1
    idx = jnp.arange(nc)[:, None] * CMP_STRIDE + jnp.arange(CMP_BLOCK)[None, :]
    blk = t[:, idx] + pe[None, None, :, None, :]
    blk = jnp.moveaxis(blk, 3, 2).reshape(b, nc, g, CMP_BLOCK * dh)
    hid = jax.nn.gelu(blk @ w1 + b1)
    return hid @ w2

def compressed_attention(q, kc, vc, scale):
    s_len = q.shape[1]
    nc = kc.shape[1]
    sc = jnp.einsum('bsghd,bngd->bghsn', q, kc).astype(jnp.float32) * scale
    blk_end = jnp.arange(nc) * CMP_STRIDE + CMP_BLOCK - 1
    valid = blk_end[None, :] <= jnp.arange(s_len)[:, None]
    p = jax.nn.softmax(jnp.where(valid, sc, MASK_VALUE), axis=-1) * valid
    o = jnp.einsum('bghsn,bngd->bsghd', p.astype(vc.dtype), vc)
    return o, p

def select_blocks(p_cmp, s_len):
    nc = p_cmp.shape[-1]
    ns = s_len // SEL_BLOCK
    cs = jnp.arange(nc) * CMP_STRIDE
    ss = jnp.arange(ns) * SEL_BLOCK
    overlap = (jnp.minimum(cs[:, None] + CMP_BLOCK, ss[None, :] + SEL_BLOCK)
               > jnp.maximum(cs[:, None], ss[None, :])).astype(jnp.float32)
    imp = jnp.einsum('bghsn,nj->bgsj', p_cmp, overlap)
    t = jnp.arange(s_len)[:, None]
    blk = jnp.arange(ns)[None, :]
    future = ss[None, :] > t
    forced = (blk == 0) | (blk == t // SEL_BLOCK)
    imp = jnp.where(forced, FORCE_SCORE, jnp.where(future, -1.0, imp))
    _, idx = lax.top_k(imp, min(N_SEL, ns))
    return idx

def selected_attention(q, ks, vs, idx, scale):
    b, s_len, g, hg, dh = q.shape
    ns = s_len // SEL_BLOCK
    k_sel = idx.shape[-1]
    nq = s_len // SEL_QCHUNK
    kb = ks.reshape(b, ns, SEL_BLOCK, g, dh).transpose(0, 3, 1, 2, 4)
    vb = vs.reshape(b, ns, SEL_BLOCK, g, dh).transpose(0, 3, 1, 2, 4)
    qc = q.reshape(b, nq, SEL_QCHUNK, g, hg, dh).transpose(1, 0, 3, 4, 2, 5)
    ic = idx.reshape(b, g, nq, SEL_QCHUNK, k_sel).transpose(2, 0, 1, 3, 4)
    bi = jnp.arange(b)[:, None, None, None]
    gi = jnp.arange(g)[None, :, None, None]

    def chunk(args):
        qi, ii, ci = args
        kg = kb[bi, gi, ii]
        vg = vb[bi, gi, ii]
        sc = jnp.einsum('bghtd,bgtkld->bghtkl', qi, kg).astype(jnp.float32) * scale
        kpos = ii[..., None] * SEL_BLOCK + jnp.arange(SEL_BLOCK)
        qpos = ci * SEL_QCHUNK + jnp.arange(SEL_QCHUNK)
        valid = kpos <= qpos[None, None, :, None, None]
        sc = jnp.where(valid[:, :, None], sc, MASK_VALUE).reshape(b, g, hg, SEL_QCHUNK, k_sel * SEL_BLOCK)
        p = jax.nn.softmax(sc, axis=-1).reshape(b, g, hg, SEL_QCHUNK, k_sel, SEL_BLOCK)
        return jnp.einsum('bghtkl,bgtkld->bghtd', p.astype(vg.dtype), vg)

    o = lax.map(chunk, (qc, ic, jnp.arange(nq)))
    return o.transpose(1, 0, 4, 2, 3, 5).reshape(b, s_len, g, hg, dh)

def window_attention(q, kw, vw, scale):
    b, s_len, g, hg, dh = q.shape
    nb = s_len // WIN_QBLOCK
    span = WINDOW + WIN_QBLOCK
    kp = jnp.pad(kw, ((0, 0), (WINDOW, 0), (0, 0), (0, 0)))
    vp = jnp.pad(vw, ((0, 0), (WINDOW, 0), (0, 0), (0, 0)))
    qb = q.reshape(b, nb, WIN_QBLOCK, g, hg, dh).transpose(1, 0, 3, 4, 2, 5)

    def block(args):
        qi, blk_id = args
        start = blk_id * WIN_QBLOCK
        kk = lax.dynamic_slice_in_dim(kp, start, span, axis=1)
        vv = lax.dynamic_slice_in_dim(vp, start, span, axis=1)
        sc = jnp.einsum('bghtd,bsgd->bghts', qi, kk).astype(jnp.float32) * scale
        qpos = start + jnp.arange(WIN_QBLOCK)
        kpos = start - WINDOW + jnp.arange(span)
        valid = ((kpos[None, :] <= qpos[:, None]) & (kpos[None, :] > qpos[:, None] - WINDOW)
                 & (kpos[None, :] >= 0))
        p = jax.nn.softmax(jnp.where(valid, sc, MASK_VALUE), axis=-1)
        return jnp.einsum('bghts,bsgd->bghtd', p.astype(vv.dtype), vv)

    o = lax.map(block, (qb, jnp.arange(nb)))
    return o.transpose(1, 0, 4, 2, 3, 5).reshape(b, s_len, g, hg, dh)

def _complex_linear_combine(left, right):
    ar1, ai1, br1, bi1 = left
    ar2, ai2, br2, bi2 = right
    ar = ar2 * ar1 - ai2 * ai1
    ai = ar2 * ai1 + ai2 * ar1
    xr = ar2 * br1 - ai2 * bi1 + br2
    xi = ar2 * bi1 + ai2 * br1 + bi2
    return ar, ai, xr, xi

def s5_ssm(u, lam_re, lam_im, log_dt, b_re, b_im, c_re, c_im, d_skip):
    b, s_len, _ = u.shape
    uf = u.astype(jnp.float32).reshape(b, s_len, SSM_GROUPS, SSM_GROUP)
    dt = jnp.exp(log_dt.astype(jnp.float32))[:, None]
    lr = lam_re.astype(jnp.float32)
    li = lam_im.astype(jnp.float32)
    mag = jnp.exp(lr * dt)
    ab_re = mag * jnp.cos(li * dt)
    ab_im = mag * jnp.sin(li * dt)
    nr = ab_re - 1.0
    ni = ab_im
    den = lr * lr + li * li
    cr = ((nr * lr + ni * li) / den)[..., None]
    ci = ((ni * lr - nr * li) / den)[..., None]
    br = b_re.astype(jnp.float32)
    bim = b_im.astype(jnp.float32)
    bb_re = cr * br - ci * bim
    bb_im = cr * bim + ci * br
    bu_re = jnp.einsum('bsgc,gpc->sbgp', uf, bb_re)
    bu_im = jnp.einsum('bsgc,gpc->sbgp', uf, bb_im)
    a_re = jnp.broadcast_to(ab_re, (s_len, 1) + ab_re.shape)
    a_im = jnp.broadcast_to(ab_im, (s_len, 1) + ab_im.shape)
    _, _, x_re, x_im = lax.associative_scan(_complex_linear_combine, (a_re, a_im, bu_re, bu_im), axis=0)
    y = (jnp.einsum('sbgp,gcp->bsgc', x_re, c_re.astype(jnp.float32))
         - jnp.einsum('sbgp,gcp->bsgc', x_im, c_im.astype(jnp.float32)))
    y = y.reshape(b, s_len, SSM_WIDTH) + d_skip.astype(jnp.float32) * uf.reshape(b, s_len, SSM_WIDTH)
    return y.astype(u.dtype)

def setup_inputs(seed: int = 0) -> dict:
    key = jax.random.key(seed)
    ks = jax.random.split(key, 32)
    L = DEPTH
    nrm = jax.random.normal
    f32 = jnp.float32
    lam_im_base = math.pi * jnp.arange(SSM_STATE, dtype=f32)
    return {
        "x": nrm(ks[0], (BATCH, SEQ, D_MODEL), f32),
        "c": nrm(ks[1], (BATCH, D_MODEL), f32),
        "w_ada": nrm(ks[2], (L, D_MODEL, 3 * D_MODEL), f32) * D_MODEL ** -0.5,
        "b_ada": nrm(ks[3], (L, 3 * D_MODEL), f32) * 0.02,
        "norm_gain": 1.0 + 0.05 * nrm(ks[4], (L, D_MODEL), f32),
        "w_in": nrm(ks[5], (L, D_MODEL, IN_WIDTH), f32) * D_MODEL ** -0.5,
        "pe_cmp_k": nrm(ks[6], (L, CMP_BLOCK, HEAD_DIM), f32) * 0.1,
        "w_cmp_k1": nrm(ks[7], (L, CMP_BLOCK * HEAD_DIM, CMP_HIDDEN), f32) * (CMP_BLOCK * HEAD_DIM) ** -0.5,
        "b_cmp_k1": nrm(ks[8], (L, CMP_HIDDEN), f32) * 0.02,
        "w_cmp_k2": nrm(ks[9], (L, CMP_HIDDEN, HEAD_DIM), f32) * CMP_HIDDEN ** -0.5,
        "pe_cmp_v": nrm(ks[10], (L, CMP_BLOCK, HEAD_DIM), f32) * 0.1,
        "w_cmp_v1": nrm(ks[11], (L, CMP_BLOCK * HEAD_DIM, CMP_HIDDEN), f32) * (CMP_BLOCK * HEAD_DIM) ** -0.5,
        "b_cmp_v1": nrm(ks[12], (L, CMP_HIDDEN), f32) * 0.02,
        "w_cmp_v2": nrm(ks[13], (L, CMP_HIDDEN, HEAD_DIM), f32) * CMP_HIDDEN ** -0.5,
        "lam_re": -0.5 + 0.01 * nrm(ks[14], (L, SSM_GROUPS, SSM_STATE), f32),
        "lam_im": lam_im_base + 0.01 * nrm(ks[15], (L, SSM_GROUPS, SSM_STATE), f32),
        "log_dt": jax.random.uniform(ks[16], (L, SSM_GROUPS), f32, math.log(DT_MIN), math.log(DT_MAX)),
        "b_re": nrm(ks[17], (L, SSM_GROUPS, SSM_STATE, SSM_GROUP), f32) * (2 * SSM_GROUP) ** -0.5,
        "b_im": nrm(ks[18], (L, SSM_GROUPS, SSM_STATE, SSM_GROUP), f32) * (2 * SSM_GROUP) ** -0.5,
        "c_re": nrm(ks[19], (L, SSM_GROUPS, SSM_GROUP, SSM_STATE), f32) * (2 * SSM_STATE) ** -0.5,
        "c_im": nrm(ks[20], (L, SSM_GROUPS, SSM_GROUP, SSM_STATE), f32) * (2 * SSM_STATE) ** -0.5,
        "d_skip": nrm(ks[21], (L, SSM_WIDTH), f32) * 0.5,
        "w_glu": nrm(ks[22], (L, SSM_WIDTH, 2 * SSM_WIDTH), f32) * SSM_WIDTH ** -0.5,
        "w_proj_attn": nrm(ks[23], (L, ATTN_WIDTH, D_MODEL), f32) * ATTN_WIDTH ** -0.5,
        "w_proj_ssm": nrm(ks[24], (L, SSM_WIDTH, D_MODEL), f32) * SSM_WIDTH ** -0.5,
        "w_out": nrm(ks[25], (L, D_MODEL, D_MODEL), f32) * D_MODEL ** -0.5,
        "final_gain": 1.0 + 0.05 * nrm(ks[26], (D_MODEL,), f32),
    }

def reference(x, c, w_ada, b_ada, norm_gain, w_in, pe_cmp_k, w_cmp_k1, b_cmp_k1, w_cmp_k2,
              pe_cmp_v, w_cmp_v1, b_cmp_v1, w_cmp_v2, lam_re, lam_im, log_dt, b_re, b_im,
              c_re, c_im, d_skip, w_glu, w_proj_attn, w_proj_ssm, w_out, final_gain):
    b, s_len, _ = x.shape
    scale = HEAD_DIM ** -0.5
    cos, sin = rope_tables(s_len, x.dtype)
    for l in range(DEPTH):
        mod = jax.nn.silu(c) @ w_ada[l] + b_ada[l]
        shift, mscale, gate = jnp.split(mod[:, None, :], 3, axis=-1)
        h = rms_norm(x, norm_gain[l]) * (1.0 + mscale) + shift

        proj = h @ w_in[l]
        q, kv, nsa_gl, z_attn, u, z_ssm, merge_gl = jnp.split(proj, IN_OFFSETS, axis=-1)

        q = apply_rope(q.reshape(b, s_len, N_HEADS_ATTN, HEAD_DIM), cos, sin)
        q = q.reshape(b, s_len, N_KV_GROUPS, HEADS_PER_GROUP, HEAD_DIM)
        k_c, v_c, k_s, v_s, k_w, v_w = [t.reshape(b, s_len, N_KV_GROUPS, HEAD_DIM)
                                        for t in jnp.split(kv, 6, axis=-1)]
        k_c = apply_rope(k_c, cos, sin)
        k_s = apply_rope(k_s, cos, sin)
        k_w = apply_rope(k_w, cos, sin)
        kc = compress_blocks(k_c, pe_cmp_k[l], w_cmp_k1[l], b_cmp_k1[l], w_cmp_k2[l])
        vc = compress_blocks(v_c, pe_cmp_v[l], w_cmp_v1[l], b_cmp_v1[l], w_cmp_v2[l])
        o_cmp, p_cmp = compressed_attention(q, kc, vc, scale)
        sel_idx = select_blocks(p_cmp, s_len)
        o_slc = selected_attention(q, k_s, v_s, sel_idx, scale)
        o_win = window_attention(q, k_w, v_w, scale)
        g3 = jax.nn.sigmoid(nsa_gl.reshape(b, s_len, N_KV_GROUPS, HEADS_PER_GROUP, 3))
        o_attn = (g3[..., 0:1] * o_cmp + g3[..., 1:2] * o_slc + g3[..., 2:3] * o_win)
        o_attn = o_attn.reshape(b, s_len, ATTN_WIDTH) * jax.nn.silu(z_attn)

        y = jax.nn.gelu(s5_ssm(u, lam_re[l], lam_im[l], log_dt[l], b_re[l], b_im[l],
                               c_re[l], c_im[l], d_skip[l]))
        ya, yb = jnp.split(y @ w_glu[l], 2, axis=-1)
        o_ssm = ya * jax.nn.sigmoid(yb) * jax.nn.silu(z_ssm)

        m_a, m_s = jnp.split(merge_gl, 2, axis=-1)
        merged = (jax.nn.sigmoid(m_a) * (o_attn @ w_proj_attn[l])
                  + jax.nn.sigmoid(m_s) * (o_ssm @ w_proj_ssm[l]))
        x = x + gate * (merged @ w_out[l])
    return rms_norm(x, final_gain)


_drawn_inputs = setup_inputs


def setup_inputs(seed=0):
    import zlib

    import numpy as np

    out = dict(_drawn_inputs(seed))
    spreads = {}
    factors = {'b_ada': 5.241,
     'norm_gain': 4.256,
     'pe_cmp_k': 8.0,
     'b_cmp_k1': 8.0,
     'pe_cmp_v': 7.123,
     'b_cmp_v1': 34.646,
     'lam_re': 64.0,
     'lam_im': 45.296,
     'log_dt': 59.112,
     'b_re': 55.928,
     'b_im': 64.0,
     'c_re': 47.64,
     'c_im': 61.008}
    for name, (base, spread) in spreads.items():
        noise = np.random.default_rng([zlib.crc32(name.encode()), seed]).standard_normal(out[name].shape)
        drawn = base * np.exp(spread * noise) if base else spread * noise
        out[name] = __import__('jax').numpy.asarray(drawn.astype(out[name].dtype))
    for name, factor in factors.items():
        out[name] = (out[name] * factor).astype(out[name].dtype)
    return out
```

```python
import math
import numpy as np
import concourse.bass as bass
from concourse import mybir

P = 128
SEQ = 1024
D_MODEL = 1024
KT = D_MODEL // P
ST = SEQ // P
HALF = 512
NC_HALF = SEQ // HALF
HEADS, GROUPS, HD = 8, 2, 64
HPG = HEADS // GROUPS
CMP_BLOCK, CMP_STRIDE = 32, 16
NCMP = (SEQ - CMP_BLOCK) // CMP_STRIDE + 1
PAIRS = CMP_BLOCK // 2
CMP_HIDDEN = 2 * HD
WIN_TILES = 512 // P
EPS = 1e-6
MASK = -1.0e30
MAX_FLOOR = -1.0e29
TINY = 1.0e-30
SG, SC, SS = 16, 16, 64
SW = SG * SC
SSM_T = SG // 2
CH = 8
NCH = SEQ // CH
IN_W = 4376
COL_Q, COL_KV, COL_GATE, COL_U, COL_ZS, COL_MA, COL_MS = 0, 512, 1280, 1816, 2072, 2328, 3352
NGATE = 3 * HEADS
ROUND = 1.5 * 2.0 ** 23
TWO_PI_1, TWO_PI_2, TWO_PI_3 = 6.28125, 0.0019350051879882812, 3.019915981956753e-07
SIN_2PI = 6.2831845
VW = HD + 2

CHUNKS = [(COL_U, 256), (COL_ZS, 256), (COL_Q, 256), (COL_Q + 256, 256), (COL_KV, 256),
          (COL_GATE, 280), (COL_GATE + 280, 256), (COL_KV + 256, 256), (COL_KV + 512, 256)]
U_, ZS_, Q0_, Q1_, KC_, Z0_, Z1_, KS_, KW_ = range(9)
CW = 280

R_H = 16544
R_K = R_H + 65536
R_V = R_K + 32768
R_Q = R_V + 8448
R_Z = R_Q + 16384
R_O = R_Z + 16384
R_W = R_O + 8192
R_C = R_W + 5 * CW * 4 * KT


def shape_tables():
    f32 = np.float32
    half = HD // 2
    inv = (f32(10000.0) ** (-np.arange(half, dtype=f32) / f32(half))).astype(f32)
    ang = (np.arange(SEQ, dtype=f32)[:, None] * inv[None, :]).astype(f32)
    cos, sin = np.cos(ang).astype(f32), np.sin(ang).astype(f32)
    rope = np.concatenate([cos, cos, -sin, sin], axis=1)
    ident = np.eye(P, dtype=f32)
    p, f = np.arange(P)[:, None], np.arange(P)[None, :]
    causal = np.where(f <= p, 0.0, MASK).astype(f32)
    band = np.where(f > p, 0.0, MASK).astype(f32)
    q, n = np.arange(SEQ)[:, None], np.arange(64)[None, :]
    cmp_q = np.where((CMP_STRIDE * n + CMP_BLOCK - 1 <= q) & (n < NCMP), 0.0, MASK).astype(f32)
    ramp = np.zeros((1, 160), f32)
    ramp[0, 0:NCH] = np.arange(NCH) - 1
    ramp[0, NCH:NCH + 16] = np.arange(16)
    aug = np.zeros((P, 4), f32)
    for b in range(3):
        aug[HD + 2 * b:HD + 2 * b + 2, b] = 1.0
    return {"t_rope": rope, "t_ident": ident, "t_masks": np.concatenate([causal, band], 1),
            "t_cmpq": cmp_q, "t_cmpt": np.ascontiguousarray(cmp_q.T), "t_ramp": ramp, "t_aug": aug}


class Chain:

    def __init__(self, eng, sem):
        self.eng, self.sem, self.n = eng, sem, 0

    def mark(self, ins):
        self.n += 1
        ins.then_inc(self.sem, 1)

    def wait(self):
        self.eng.wait_ge(self.sem, self.n)

    def link(self, ins):
        self.mark(ins)
        self.wait()


def head_units():
    units = []
    for c in range(NC_HALF):
        units.append((0, c, 0, c * HALF, (c + 1) * HALF, False, False))
    for c in range(NC_HALF):
        for j in range(4 * c + 4):
            q0 = max(P * j, HALF * c)
            units.append((1, c, j, q0, HALF * (c + 1), P * j >= HALF * c, False))
    for c in range(NC_HALF):
        order = range(4) if c == 0 else (3, 0, 1, 2, 4, 5, 6, 7)
        for j in order:
            q0, q1 = max(P * j, HALF * c), min(P * (j + WIN_TILES + 1), HALF * (c + 1))
            last = j + WIN_TILES
            units.append((2, c, j, q0, q1, P * j >= HALF * c, HALF * c <= P * last < HALF * (c + 1)))
    return units


def attention_plan():
    units = head_units()
    nu = len(units)
    LAG = 2
    plan = [("MQ", 0)] + [("MX", 0, i) for i in range(ST)] + [("MM", 0)]
    last_of = {}
    for u, t in enumerate(units):
        last_of[(t[0], t[1])] = u
    closes = {u: k for k, u in enumerate(sorted(last_of.values()))}
    pending = []
    for e in range(HEADS * nu + LAG + 3):
        h, u = divmod(e, nu)
        if e < HEADS * nu:
            plan.append(("S", e))
        v = e - LAG
        if 0 <= v < HEADS * nu:
            plan.append(("V", v))
            if v % nu in closes:
                pending.append((e + 2, 6 * (v // nu) + closes[v % nu]))
        while pending and (pending[0][0] <= e or e == HEADS * nu + LAG + 2):
            plan.append(("N", pending.pop(0)[1]))
        if h + 1 < HEADS and e < HEADS * nu:
            if u == 1:
                plan.append(("MQ", h + 1))
            if u >= 3 and (u - 3) % 2 == 0 and (u - 3) // 2 < ST:
                plan.append(("MX", h + 1, (u - 3) // 2))
            if u == 21:
                plan.append(("MM", h + 1))
    assert not pending
    b7_after, n = {}, 0
    for step in plan:
        n += {"MQ": 2, "MM": 2, "N": 1}.get(step[0], 0)
        b7_after[step] = n
    return units, plan, b7_after


def build(nc, x, c, w_ada, b_ada, norm_gain, w_in, pe_cmp_k, w_cmp_k1, b_cmp_k1, w_cmp_k2,
          pe_cmp_v, w_cmp_v1, b_cmp_v1, w_cmp_v2, lam_re, lam_im, log_dt, b_re, b_im,
          c_re, c_im, d_skip, w_glu, w_proj_attn, w_proj_ssm, w_out, final_gain,
          t_rope, t_ident, t_masks, t_cmpq, t_cmpt, t_ramp, t_aug, out, stop_after=None):
    F, R, B = mybir.dt.float32, mybir.dt.float32r, mybir.dt.bfloat16
    ALU, ACT, AX = mybir.AluOpType, mybir.ActivationFunctionType, mybir.AxisListType

    def at(name, shape, dt, offset):
        return nc.alloc_sbuf_tensor_at(name, shape, dt, offset=offset)

    def f(ap):
        return ap.bitcast(F)

    ada = at("ada", [P, KT, 2048], F, R_H)
    ht_hi = at("ht_hi", [P, KT, SEQ], R, R_H)
    ht_lo = at("ht_lo", [P, KT, SEQ], R, R_H + 32768)
    xs = at("xs", [P, ST, D_MODEL], F, R_K)
    xt = at("xt", [P, KT, SEQ], F, R_Q)
    k1 = [at(f"k1_{b}", [P, GROUPS, SEQ], R, R_K + 16384 * (b - 1)) for b in (1, 2)]
    k2 = [at(f"k2_{b}", [P, GROUPS, SEQ], R, R_K + 16384 * (b - 1) + 8192) for b in (1, 2)]
    vv = [at(f"vv_{b}", [P, ST, GROUPS, VW], F, R_V + 4224 * (b - 1)) for b in (1, 2)]
    qa = at("qa", [P, 4, ST, P], F, R_Q)
    zs = at("zs", [P, ST, 512], F, R_Z)
    so = at("so", [P, 2, SEQ], F, R_O)
    wraw = at("wraw", [P, KT, CW], F, R_W)
    whi = [at(f"whi{s}", [P, KT, CW], R, R_W + KT * CW * 4 * (1 + s)) for s in range(2)]
    wlo = [at(f"wlo{s}", [P, KT, CW], R, R_W + KT * CW * 4 * (3 + s)) for s in range(2)]
    junk = at("junk", [P, D_MODEL], F, R_W + KT * CW * 4 * 4)
    mrow = at("mrow", [1, 2 * D_MODEL], F, R_W + KT * CW * 4 * 2)

    top = [R_C]

    def const(name, shape, dt, size=4):
        n = size * int(np.prod(shape[1:]))
        t = at(name, shape, dt, top[0])
        top[0] += (n + 31) // 32 * 32
        return t

    ident = const("ident", [P, P], F)
    identb = const("identb", [P, P], B, 2)
    maskb = const("maskb", [P, 2, P], B, 2)
    cmpq = const("cmpq", [P, ST, 64], B, 2)
    cmpt = const("cmpt", [64, SEQ], B, 2)
    rope = const("rope", [P, ST, 2, HD], F)
    gates = const("gates", [P, ST, NGATE], F)
    aug = const("aug", [P, 4], F)
    k1c = const("k1c", [P, GROUPS, 64], R)
    k2c = const("k2c", [P, GROUPS, 64], R)
    vc = const("vc", [64, GROUPS, VW], F)
    rt1 = const("rt1", [P, 256], F)
    rt2 = const("rt2", [P, 256], F)
    kcat = [const(f"kcat{s}", [P, GROUPS, 2, HD], R) for s in range(2)]
    ccol = const("ccol", [P, KT], F)
    scol = const("scol", [P, KT], F)
    bcol = const("bcol", [P, 2 * KT], F)
    modc = const("modc", [P, 2 * KT], F)
    gcol = const("gcol", [P, KT], F)
    g1 = const("g1", [P, KT], F)
    ss = const("ss", [P, ST], F)
    rs = const("rs", [P, ST], F)
    mx = [const(f"mx{s}", [P, ST, 3], F) for s in range(2)]
    mneg = const("mneg", [P, ST, 3], F)
    mneg_hi = const("mneg_hi", [P, ST, 3], R)
    one11 = const("one11", [1, 1], F)
    onesq = const("onesq", [P, P], F)
    lsum = const("lsum", [P, 4], F)
    wrow = const("wrow", [P, 4], F)
    lr = const("lr", [P, SSM_T], F)
    li = const("li", [P, SSM_T], F)
    dt_ = const("dt_", [P, SSM_T], F)
    sm = const("sm", [P, 12, SSM_T], F)
    ramp = const("ramp", [P, 160], F)
    dcol = const("dcol", [SC, SG], F)
    assert top[0] <= nc.sbuf_usable_end, top[0]
    mload = at("mload", [P, 2, P], F, R_O)
    cqload = at("cqload", [P, ST, 64], F, R_O + 1024)
    ctload = at("ctload", [64, SEQ], F, R_O + 3072)

    cld = [at(f"cld{r}", [P, P], F, R_V + 512 * r) for r in range(2)]
    ct = [at(f"ct{r}", [P, SSM_T, SC], F, R_V + 1024 + 512 * r) for r in range(2)]
    bb = [at(f"bb{r}", [P, SSM_T, SC], F, R_V + 2048 + 512 * r) for r in range(2)]
    bbar = [at(f"bbar{r}", [P, SSM_T, SC], F, R_V + 3072 + 512 * r) for r in range(2)]
    pw = at("pw", [P, 6, SSM_T, 9], F, R_V + 4096)
    cp = [at(f"cp{r}", [P, SSM_T, 9, SC], F, R_K + 4608 * r) for r in range(2)]
    gt = [at(f"gt{r}", [P, SSM_T, P], F, R_K + 9216 + 4096 * r) for r in range(2)]
    toep = at("toep", [P, SG, P], F, R_K + 17408)
    b_r = at("b_r", [P, SSM_T, NCH], F, R_K + 25600)
    gs = [at(f"gs{r}", [P, SSM_T, CH, SC], F, R_Z + 4096 * r) for r in range(2)]
    klag = at("klag", [SC, SG, CH * SC], F, R_Z + 8192)
    b_i = at("b_i", [P, SSM_T, NCH], F, R_Z)
    zi = at("zi", [P, SSM_T, NCH], F, R_Z + 4096)
    zr = at("zr", [P, SSM_T, NCH], F, R_K + 9216)
    utok = at("utok", [P, SG, CH, SC], F, R_Q)
    ut = at("ut", [P, SG, NCH], F, R_Z + 8192)
    ecos = at("ecos", [P, SSM_T, NCH], F, R_V)
    esin = at("esin", [P, SSM_T, NCH], F, R_V + 4096)
    etmp = at("etmp", [P, SSM_T, NCH], F, R_Q + 8192)
    etmp2 = at("etmp2", [P, SSM_T, NCH], F, R_Q + 12288)
    ytok = at("ytok", [P, CH, SW], F, R_V)
    yt = at("yt", [P, 2, SEQ], F, R_Z)
    wglu = at("wglu", [P, 2, 512], F, R_K + 13312)
    sg = at("sg", [P, HALF], F, R_K + 29696)
    catc = [at(f"catc{s}", [P, 2, GROUPS, 2, HD], F, R_V + 2048 * s) for s in range(4)]
    t2 = at("t2", [P, 2, GROUPS, SEQ], F, R_K)
    w1 = [at(f"w1_{r}", [P, PAIRS, CMP_HIDDEN], F, R_K + 16384 + 8192 * r) for r in range(2)]
    hid = [at(f"hid{r}", [P, GROUPS * NCMP], F, R_V + 512 * r) for r in range(2)]
    w2 = [at(f"w2_{r}", [P, HD], F, R_V + 1024 + 256 * r) for r in range(2)]
    w2d = at("w2d", [P, 2, HD], F, R_V + 1536)
    pec = [at(f"pec{r}", [P, PAIRS], F, R_V + 2048 + 64 * r) for r in range(2)]
    b1c = [at(f"b1c{r}", [P, 1], F, R_V + 2176 + 32 * r) for r in range(2)]
    hb = at("hb", [P, 2], F, R_V + 2240)
    kch = at("kch", [P, GROUPS * NCMP], R, R_V + 2304)

    q1 = [at(f"q1_{s}", [P, SEQ], R, R_W + 4096 * s) for s in range(2)]
    q2 = [at(f"q2_{s}", [P, SEQ], R, R_W + 8192 + 4096 * s) for s in range(2)]
    qc1 = at("qc1", [P, ST, 2, HD], R, R_W + 16384)
    qc2 = at("qc2", [P, ST, P], F, R_W + 20480)
    NPT = 6
    pt = [at(f"pt{s}", [P, HALF], F, R_W + 24576 + 2048 * s) for s in range(NPT)]
    osb = [at(f"osb{s}", [HD + 1, HALF], F, R_W + 36864 + 2048 * s) for s in range(2)]
    otmp = at("otmp", [P, 4, HD], F, R_W + 40960)

    NW = 12
    mt = at("mt", [P, KT, SEQ], F, R_K)
    at_hi = at("at_hi", [P, 4, SEQ], R, R_Z)
    at_lo = at("at_lo", [P, 4, SEQ], R, R_Q)
    so_hi = at("so_hi", [P, 2, SEQ], R, R_V)
    so_lo = at("so_lo", [P, 2, SEQ], R, R_O)
    draw = [at(f"draw{s}", [P, NW, P], F, R_W + NW * 512 * s) for s in range(2)]
    dhi = [at(f"dhi{s}", [P, NW, P], R, R_W + NW * 512 * (2 + s)) for s in range(2)]
    dlo = [at(f"dlo{s}", [P, NW, P], R, R_W + NW * 512 * (4 + s)) for s in range(2)]
    dsig = at("dsig", [P, HALF], F, R_W + NW * 512 * 6)
    dtm = at("dtm", [P, HALF], F, R_W + NW * 512 * 6 + 2048)
    gstage = at("gstage", [P, HALF], F, R_W + NW * 512 * 6 + 4096)
    gacc = at("gacc", [P, D_MODEL], F, R_C + 512 + 256 + 512)

    ohi = at("ohi", [P, KT, D_MODEL], R, R_H)
    olo = at("olo", [P, KT, D_MODEL], R, R_H + 32768)
    oraw = at("oraw", [P, KT, D_MODEL], F, R_Q)
    mhi = [at(f"mhi{s}", [P, KT, P], R, R_W + 4096 * s) for s in range(2)]
    mlo = [at(f"mlo{s}", [P, KT, P], R, R_W + 8192 + 4096 * s) for s in range(2)]
    xr = [at(f"xr{s}", [P, D_MODEL], F, R_W + 16384 + 4096 * s) for s in range(2)]
    yr = [at(f"yr{s}", [P, D_MODEL], F, R_W + 24576 + 4096 * s) for s in range(2)]
    gateb = at("gateb", [P, D_MODEL], F, R_W + 32768)
    fgb = at("fgb", [P, D_MODEL], F, R_W + 36864)
    gbias = at("gbias", [P, D_MODEL], F, R_V)
    oss = at("oss", [P, 3, ST], F, R_W + 40960)
    ojunk = at("ojunk", [P, D_MODEL], F, R_O)

    bank = [nc.alloc_psum_tensor(f"bank{i}", [P, HALF], F) for i in range(2)]
    slc_max = nc.alloc_psum_tensor("slc_max", [P, SEQ], F)
    win_max = nc.alloc_psum_tensor("win_max", [P, SEQ], F)
    bank += [slc_max[:, 0:HALF], slc_max[:, HALF:SEQ], win_max[:, 0:HALF], win_max[:, HALF:SEQ]]
    bank += [nc.alloc_psum_tensor(f"bank{i}", [P, HALF], F) for i in (6, 7)]
    bank = [b[:, :] for b in bank]

    names = {}

    def sem(name):
        names[name] = nc.alloc_semaphore(name)
        return names[name]

    units, plan, b7_after = attention_plan()
    NU = len(units)

    s_small, s_c = sem("s_small"), sem("s_c")
    s_ssmp = sem("s_ssmp")
    s_x = [sem(f"s_x{i}") for i in range(ST)]
    s_ada = [sem(f"s_ada{k}") for k in range(KT)]
    s_raw = sem("s_raw")
    s_silu, s_sq, s_var, s_sd, s_rs, s_xn = (sem(n) for n in
        ("s_silu", "s_sq", "s_var", "s_sd", "s_rs", "s_xn"))
    s_xtr, s_xt, s_mod, s_mrow, s_mcol, s_g1 = (sem(n) for n in
        ("s_xtr", "s_xt", "s_mod", "s_mrow", "s_mcol", "s_g1"))
    s_h32, s_hhi, s_hlo = sem("s_h32"), sem("s_hhi"), sem("s_hlo")
    s_whi, s_wlo = sem("s_whi"), sem("s_wlo")
    s_unit = sem("s_unit")
    s_evd, s_eva = sem("s_evd"), sem("s_eva")
    s_tr, s_trf = sem("s_tr"), sem("s_trf")
    s_ch_d, s_ch_a, s_ch_p = sem("s_ch_d"), sem("s_ch_a"), sem("s_ch_p")
    s_masks = sem("s_masks")
    s_one = {}

    def once(name):
        if name not in s_one:
            s_one[name] = sem("s_" + name)
        return s_one[name]

    unit_list = [(w, i) for w in range(9) for i in range(4 if w == ZS_ else ST)]
    unit_no = {u: n for n, u in enumerate(unit_list)}
    reads_d = {U_: False, ZS_: False, Q0_: True, Q1_: True, KC_: True, Z0_: True, Z1_: False,
               KS_: True, KW_: True}
    reads_a = {U_: True, ZS_: True, Q0_: False, Q1_: False, KC_: True, Z0_: True, Z1_: True,
               KS_: True, KW_: True}

    def read_count(table, n):
        return sum(1 for w, _ in unit_list[:n] if table[w])

    def unit_bank(n):
        w, i = unit_list[n]
        if w == U_:
            return bank[i // 2][:, (i % 2) * 256:(i % 2) * 256 + 256]
        return bank[4 + (n - ST) % 4]

    FILLS = (["gt"] * 4 + ["klag"] * 4 + ["ut"] * 4 + ["bu"] * 4 + ["y"] * 4 + ["yt"] * 4
             + ["kc"] * 8 + ["ks"] * 8 + ["kw"] * 8)
    first = {}
    for n, name in enumerate(FILLS):
        first.setdefault(name, n)

    C_RE, C_IM = c_re[0], c_im[0]

    with nc.Block() as block:

        @block.sync
        def _(sp):
            def load_ada(k):
                sp.dma_start(ada[:, k, :], w_ada[0, P * k:P * k + P, 0:2048]).then_inc(s_ada[k], 16)
            load_ada(0)
            load_ada(1)
            for i in range(ST):
                sp.dma_start(xs[:, i, :], x[0, P * i:P * i + P, :]).then_inc(s_x[i], 16)
            for k in range(2, KT):
                load_ada(k)
            w_view = w_in[0].rearrange("(k p) n -> p k n", p=P)
            for w, (c0, n) in enumerate(CHUNKS):
                if w >= 1:
                    sp.wait_ge(s_whi, w)
                    sp.wait_ge(s_wlo, w)
                sp.dma_start(wraw[:, :, 0:n], w_view[:, :, c0:c0 + n]).then_inc(s_raw, 16)
                if w == Q1_:
                    sp.wait_ge(s_tr, first["bu"] + 4)
                    sp.dma_start(wglu[:, :, :], w_glu[0].rearrange("(k p) n -> p k n", p=P))\
                      .then_inc(once("wglu"), 16)
                if w == Z1_:
                    sp.wait_ge(once("gluo"), 4)
                    for r, (a, b, pe) in enumerate(((w_cmp_k1, w_cmp_k2, pe_cmp_k),
                                                    (w_cmp_v1, w_cmp_v2, pe_cmp_v))):
                        sp.dma_start(w1[r][:, :, :], a[0].rearrange("(m p) n -> p m n", p=P))\
                          .then_inc(once("cmpw"), 16)
                    sp.wait_ge(s_tr, first["kc"] + 8)
                    for r, (b, pe, b1) in enumerate(((w_cmp_k2, pe_cmp_k, b_cmp_k1),
                                                     (w_cmp_v2, pe_cmp_v, b_cmp_v1))):
                        sp.dma_start(w2[r][:, :], b[0]).then_inc(once("cmpw"), 16)
                        sp.dma_start(pec[r][:, :], pe[0].rearrange("(m l) d -> (l d) m", l=2),
                                     allow_slow_non_contiguous=True).then_inc(once("cmpw"), 16)
                        sp.dma_start(b1c[r][:, :], b1[0].rearrange("(p a) -> p a", a=1),
                                     allow_slow_non_contiguous=True).then_inc(once("cmpw"), 16)

            def slot_parts(n):
                nb, kind = divmod(n, 2)
                gate = COL_MA if kind == 0 else COL_MS
                proj = w_proj_attn if kind == 0 else w_proj_ssm
                kp = 4 if kind == 0 else 2
                return nb, gate, proj, kp
            for n in range(2 * KT):
                nb, gate, proj, kp = slot_parts(n)
                if n < 2:
                    sp.wait_ge(once("norm"), 4 * HEADS)
                else:
                    sp.wait_ge(once("dhi"), n - 1)
                    sp.wait_ge(once("dlo"), n - 1)
                sp.dma_start(draw[n % 2][:, 0:KT, :], w_view[:, :, gate + P * nb:gate + P * nb + P])\
                  .then_inc(once(f"draw{n % 2}"), 16)
                sp.dma_start(draw[n % 2][:, KT:KT + kp, :],
                             proj[0].rearrange("(k p) n -> p k n", p=P)[:, :, P * nb:P * nb + P])\
                  .then_inc(once(f"draw{n % 2}"), 16)
            sp.wait_ge(once("dproj"), 4 * (KT - 1) + 2)
            for k in range(KT):
                sp.dma_start(oraw[:, k, :], w_out[0, P * k:P * k + P, :]).then_inc(once(f"oraw{k}"), 16)
            sp.wait_ge(once("merged"), 2 * KT)
            sp.wait_ge(once("dgate"), 4 * KT)
            sp.dma_start(gbias[:, :], b_ada[0:1, 2048:3072].to_broadcast([P, D_MODEL])).then_inc(once("gbias"), 16)
            sp.dma_start(fgb[:, :], final_gain.rearrange("(a n) -> a n", a=1).to_broadcast([P, D_MODEL]))\
              .then_inc(once("fgb"), 16)
            for i in range(ST):
                if i >= 2:
                    sp.wait_ge(once("res"), i - 1)
                sp.dma_start(xr[i % 2][:, :], x[0, P * i:P * i + P, :]).then_inc(once(f"xr{i % 2}"), 16)
                if i >= 1:
                    sp.wait_ge(once("y"), i)
                    sp.dma_start(out[0, P * (i - 1):P * i, :], yr[(i - 1) % 2][:, :])\
                      .then_inc(once(f"out{(i - 1) % 2}"), 16)
            sp.wait_ge(once("y"), ST)
            sp.dma_start(out[0, P * (ST - 1):P * ST, :], yr[(ST - 1) % 2][:, :]).then_inc(once("out1"), 16)
            sp.wait_ge(once("out0"), 16 * (ST // 2))
            sp.wait_ge(once("out1"), 16 * (ST // 2))

        @block.gpsimd
        def _(pool):
            ch = Chain(pool, s_ch_p)

            def tt(o, a, b, op):
                return nc.gpsimd.tensor_tensor(o, a, b, op)

            nc.gpsimd.memset(onesq[:, :], 1.0).then_inc(once("vc0"), 1)
            nc.gpsimd.memset(vc[:, :, :], 0.0).then_inc(once("vc0"), 1)
            z_re, ph, fr, ta, tb, nr, cr, ci, den, tc = (sm[:, i, :] for i in range(10))
            pool.wait_ge(s_ssmp, 16 * 12)
            pool.wait_ge(once("dt"), 1)
            ch.link(tt(z_re, lr[:, :], dt_[:, :], ALU.mult))
            ch.link(tt(ph, li[:, :], dt_[:, :], ALU.mult))
            ch.link(nc.gpsimd.tensor_scalar(ta, ph, 1.0 / (2 * math.pi), ROUND, ALU.mult, ALU.add))
            ch.link(nc.gpsimd.tensor_scalar(ta, ta, -ROUND, None, ALU.add))
            for part in (TWO_PI_1, TWO_PI_2, TWO_PI_3):
                ch.link(nc.gpsimd.tensor_scalar(tb, ta, part, None, ALU.mult))
                ch.link(tt(ph, ph, tb, ALU.subtract))
            ch.link(nc.gpsimd.tensor_scalar(fr, ph, 1.0 / (2 * math.pi), None, ALU.mult))
            J = [P, SSM_T, 9]
            turns, mag, cs, sn, pr, pi = (pw[:, i, :, :] for i in range(6))
            jr = ramp[:, NCH:NCH + 9].unsqueeze(1).to_broadcast(J)
            ch.link(tt(turns, fr.unsqueeze(2).to_broadcast(J), jr, ALU.mult))
            ch.link(nc.gpsimd.tensor_scalar(cs, turns, ROUND, -ROUND, ALU.add, ALU.add))
            ch.link(tt(turns, turns, cs, ALU.subtract))
            tt(mag, z_re.unsqueeze(2).to_broadcast(J), jr, ALU.mult).then_inc(once("pw_arg"), 1)
            pool.wait_ge(once("pw_fn"), 3)
            ch.link(tt(cs, cs, cs, ALU.mult))
            ch.link(nc.gpsimd.tensor_scalar(cs, cs, -2.0, 1.0, ALU.mult, ALU.add))
            ch.link(tt(pr, mag, cs, ALU.mult))
            ch.link(tt(pi, mag, sn, ALU.mult))
            ar, ai = pw[:, 4, :, 1], pw[:, 5, :, 1]
            ch.link(nc.gpsimd.tensor_scalar(nr, ar, -1.0, None, ALU.add))
            ch.link(tt(den, lr[:, :], lr[:, :], ALU.mult))
            ch.link(tt(ta, li[:, :], li[:, :], ALU.mult))
            ch.link(tt(den, den, ta, ALU.add))
            ch.link(tt(cr, nr, lr[:, :], ALU.mult))
            ch.link(tt(ta, ai, li[:, :], ALU.mult))
            ch.link(tt(cr, cr, ta, ALU.add))
            ch.link(tt(ci, ai, lr[:, :], ALU.mult))
            ch.link(tt(ta, nr, li[:, :], ALU.mult))
            tt(ci, ci, ta, ALU.subtract).then_inc(once("den"), 1)
            pool.wait_ge(once("rden"), 1)
            ch.link(tt(cr, cr, tc, ALU.mult))
            ch.link(tt(ci, ci, tc, ALU.mult))
            S3 = [P, SSM_T, SC]
            crb, cib = cr.unsqueeze(2).to_broadcast(S3), ci.unsqueeze(2).to_broadcast(S3)
            tmp3 = zi[:, 0, :].rearrange("p (t c) -> p t c", t=SSM_T)
            pool.wait_ge(s_hlo, KT)
            for r, (a, b, op) in enumerate(((0, 1, ALU.subtract), (1, 0, ALU.add))):
                ch.link(tt(bbar[r][:, :, :], crb, bb[a][:, :, :], ALU.mult))
                ch.link(tt(tmp3, cib, bb[b][:, :, :], ALU.mult))
                ch.link(tt(bbar[r][:, :, :], bbar[r][:, :, :], tmp3, op))
            G4 = [P, SSM_T, CH, SC]

            def pw_rev(q):
                return pw[:, q, :, 7::-1].unsqueeze(3).to_broadcast(G4)

            def bb4(q):
                return bbar[q][:, :, :].unsqueeze(2).to_broadcast(G4)
            gtmp = etmp[:, :, :].rearrange("p t (j c) -> p t j c", c=SC)
            for r, (a, b, op) in enumerate(((0, 1, ALU.subtract), (1, 0, ALU.add))):
                ch.link(tt(gs[r][:, :, :, :], pw_rev(4), bb4(a), ALU.mult))
                ch.link(tt(gtmp, pw_rev(5), bb4(b), ALU.mult))
                tt(gs[r][:, :, :, :], gs[r][:, :, :, :], gtmp, op).then_inc(once("gs"), 1)
                pool.wait_ge(once("gs"), r + 1)
            pool.wait_ge(once("ctev"), 2)
            C4 = [P, SSM_T, 9, SC]
            ctmp = at("ctmp", [P, SSM_T, 9, SC], F, R_Q + 8192)

            def pw9(q):
                return pw[:, q, :, :].unsqueeze(3).to_broadcast(C4)

            def ct4(q):
                return ct[q][:, :, :].unsqueeze(2).to_broadcast(C4)
            ch.link(tt(cp[0][:, :, :, :], pw9(4), ct4(0), ALU.mult))
            ch.link(tt(ctmp[:, :, :, :], pw9(5), ct4(1), ALU.mult))
            ch.link(tt(cp[0][:, :, :, :], cp[0][:, :, :, :], ctmp[:, :, :, :], ALU.subtract))
            ch.link(tt(cp[1][:, :, :, :], pw9(5), ct4(0), ALU.mult))
            ch.link(tt(ctmp[:, :, :, :], pw9(4), ct4(1), ALU.mult))
            ch.link(tt(cp[1][:, :, :, :], cp[1][:, :, :, :], ctmp[:, :, :, :], ALU.add))
            nc.gpsimd.tensor_scalar(cp[1][:, :, :, :], cp[1][:, :, :, :], -1.0, None, ALU.mult)\
                .then_inc(once("cp"), 1)
            ch.link(nc.gpsimd.memset(toep[:, :, :], 0.0))
            ch.link(nc.gpsimd.tensor_copy(tb, pw[:, 1, :, 8]))
            ch.link(nc.gpsimd.tensor_copy(ta, pw[:, 0, :, 8]))
            pool.wait_ge(s_trf, first["klag"] + 4)
            dtmp = at("dtmp", [SC, SG, SC], F, R_Q + 8192)
            ch.link(tt(dtmp[:, :, :], ident[0:SC, 0:SC].unsqueeze(1).to_broadcast([SC, SG, SC]),
                       dcol[:, :].unsqueeze(2).to_broadcast([SC, SG, SC]), ALU.mult))
            ch.link(tt(klag[:, :, 0:SC], klag[:, :, 0:SC], dtmp[:, :, :], ALU.add))
            for i in range(CH):
                pool.dma_start(toep[SC * i:SC * i + SC, :, SC * i:CH * SC], klag[:, :, 0:(CH - i) * SC])\
                    .then_inc(once("toep"), 16)
            E3 = [P, SSM_T, NCH]
            ch.link(tt(etmp[:, :, :], ta.unsqueeze(2).to_broadcast(E3),
                       ramp[:, 0:NCH].unsqueeze(1).to_broadcast(E3), ALU.mult))
            ch.link(nc.gpsimd.tensor_scalar(etmp2[:, :, :], etmp[:, :, :], ROUND, -ROUND, ALU.add, ALU.add))
            tt(etmp[:, :, :], etmp[:, :, :], etmp2[:, :, :], ALU.subtract).then_inc(once("eang"), 1)
            pool.wait_ge(once("efn"), 2)
            ch.link(tt(ecos[:, :, :], ecos[:, :, :], ecos[:, :, :], ALU.mult))
            nc.gpsimd.tensor_scalar(ecos[:, :, :], ecos[:, :, :], -2.0, 1.0, ALU.mult, ALU.add)\
                .then_inc(once("ecos"), 1)
            for n in range(4):
                nb, cc = divmod(n, 2)
                pool.wait_ge(once("glusig"), n + 1)
                v = so[:, nb, cc * HALF:(cc + 1) * HALF]
                tt(v, v, sg[:, :], ALU.mult).then_inc(once("glugate"), 1)
            for h in range(HEADS):
                pool.wait_ge(once("qhi"), h + 1)
                nc.gpsimd.tensor_copy(qc1[:, :, 1, :], f(qc1[:, :, 0, :])).then_inc(once("qdup"), 1)
            for b in range(4):
                pool.wait_ge(once("norm"), 8 * (b + 1))
                v = qa[:, b, :, :]
                tt(v, v, zs[:, :, P * b:P * b + P], ALU.mult).then_inc(once("az"), 1)
            for n in range(2 * KT):
                k, hf = divmod(n, 2)
                dst = gacc[:, HALF * hf:HALF * hf + HALF]
                if n > 0:
                    ch.wait()
                pool.dma_start(gstage[:, :], w_ada[0, P * k:P * k + P, 2048 + HALF * hf:2560 + HALF * hf])\
                    .then_inc(once("gst"), 16)
                pool.wait_ge(once("gst"), 16 * (n + 1))
                if k == 0:
                    ch.mark(nc.gpsimd.tensor_scalar(dst, gstage[:, :], scol[:, k:k + 1], None, ALU.mult))
                else:
                    ch.link(nc.gpsimd.tensor_scalar(gstage[:, :], gstage[:, :], scol[:, k:k + 1], None,
                                                    ALU.mult))
                    ins = tt(dst, dst, gstage[:, :], ALU.add)
                    if n < 2 * KT - 1:
                        ch.mark(ins)
            ins.then_inc(once("gacc"), 1)

        @block.scalar
        def _(act):
            ch = Chain(act, s_ch_a)

            def a(o, i, fn=ACT.Copy, **kw):
                return nc.scalar.activation(o, i, fn, **kw)

            sl = dict(allow_slow_non_contiguous=True)
            act.dma_start(ccol[:, :], c[0].rearrange("(k p) -> p k", p=P), **sl).then_inc(s_c, 16)
            act.dma_start(ident[:, :], t_ident).then_inc(s_small, 16)
            act.dma_start(bcol[:, :], b_ada[0, 0:2048].rearrange("(k p) -> p k", p=P), **sl).then_inc(s_small, 16)
            act.dma_start(gcol[:, :], norm_gain[0].rearrange("(k p) -> p k", p=P), **sl).then_inc(s_small, 16)
            act.dma_start(mload[:, :, :], t_masks.rearrange("p (a f) -> p a f", a=2)).then_inc(s_small, 16)
            act.dma_start(cqload[:, :, :], t_cmpq.rearrange("(i p) n -> p i n", p=P)).then_inc(s_small, 16)
            act.dma_start(ctload[:, :], t_cmpt).then_inc(s_small, 16)
            act.dma_start(rope[:, :, :, :], t_rope.rearrange("(i p) (a d) -> p i a d", p=P, a=2)).then_inc(s_small, 16)
            act.dma_start(aug[:, :], t_aug).then_inc(s_small, 16)
            SMALL = 16 * 8
            for gp in range(2):
                half = slice(SS * gp, SS * gp + SS)
                for dst, src in ((lr, lam_re), (li, lam_im)):
                    act.dma_start(dst[half, :], src[0].rearrange("(t g) s -> g s t", g=2)[gp], **sl)\
                        .then_inc(s_ssmp, 16)
                act.dma_start(dt_[half, :], log_dt[0].rearrange("(t g) -> g t", g=2)[gp:gp + 1, :]
                              .to_broadcast([SS, SSM_T]), **sl).then_inc(s_ssmp, 16)
                for dst, src in ((bb[0], b_re), (bb[1], b_im)):
                    act.dma_start(dst[half, :, :], src[0].rearrange("(t g) s c -> g s t c", g=2)[gp], **sl)\
                        .then_inc(s_ssmp, 16)
            act.dma_start(ramp[:, :], t_ramp.to_broadcast([P, 160])).then_inc(s_ssmp, 16)
            act.dma_start(dcol[:, :], d_skip[0].rearrange("(g c) -> c g", g=SG), **sl).then_inc(s_ssmp, 16)
            for r, src in enumerate((C_RE, C_IM)):
                for t in range(SSM_T):
                    act.dma_start(cld[r][SC * t:SC * t + SC, :].rearrange("c (g s) -> c g s", g=2),
                                  src[2 * t:2 * t + 2].rearrange("g c s -> c g s")).then_inc(once("cld"), 16)

            act.wait_ge(s_c, 16)
            a(scol[:, :], ccol[:, :], ACT.Silu).then_inc(s_silu, 1)
            act.wait_ge(s_ssmp, 16 * 12)
            a(dt_[:, :], dt_[:, :], ACT.Exp).then_inc(once("dt"), 1)
            for i in range(ST):
                act.wait_ge(s_x[i], 16)
                if i >= 1:
                    act.wait_ge(s_sq, i)
                a(junk[:, :], xs[:, i, :], ACT.Square, accum_out=ss[:, i:i + 1]).then_inc(s_sq, 1)
            act.wait_ge(s_var, 1)
            a(rs[:, :], ss[:, :], ACT.Sqrt).then_inc(s_sd, 1)
            for n in range(0, 16, 2):
                k, cc = divmod(n, 2)
                act.wait_ge(s_xtr, n + 1)
                a(xt[:, k, cc * HALF:(cc + 1) * HALF], bank[4 + n % 4]).then_inc(once("xta"), 1)
            for r in range(2):
                act.wait_ge(once("ctr"), 1)
                a(ct[r][:, :, :], bank[4][:, P * r:P * r + P].rearrange("p (t c) -> p t c", t=SSM_T))\
                    .then_inc(once("ctev"), 1)
            act.wait_ge(once("pw_arg"), 1)
            a(pw[:, 1, :, :], pw[:, 1, :, :], ACT.Exp).then_inc(once("pw_fn"), 1)
            a(pw[:, 2, :, :], pw[:, 0, :, :], ACT.Sin, scale=SIN_2PI / 2).then_inc(once("pw_fn"), 1)
            a(pw[:, 3, :, :], pw[:, 0, :, :], ACT.Sin, scale=SIN_2PI).then_inc(once("pw_fn"), 1)
            act.wait_ge(s_mod, 1)
            for j in range(0, 4, 2):
                a(mrow[0:1, j * HALF:(j + 1) * HALF], bank[j][0:1, :]).then_inc(once("mra"), 1)

            def split_w(w):
                n = CHUNKS[w][1]
                act.wait_ge(s_raw, 16 * (w + 1))
                if w >= 2:
                    act.wait_ge(s_unit, unit_no[(w - 1, 0)])
                a(whi[w % 2][:, :, 0:n], wraw[:, :, 0:n]).then_inc(s_whi, 1)

            def fill(n):
                act.wait_ge(s_tr, n + 1)
                return bank[n % 2]

            split_w(0)
            for k in range(KT):
                act.wait_ge(s_h32, k + 1)
                a(ht_hi[:, k, :], xt[:, k, :]).then_inc(s_hhi, 1)
            split_w(1)
            for i in range(ST):
                act.wait_ge(s_unit, ST)
                if i == 0:
                    act.wait_ge(s_hlo, KT)
                a(utok[:, :, i, :], unit_bank(i).rearrange("p (g c) -> p g c", g=SG)).then_inc(s_eva, 1)
            split_w(2)
            for q in range(4):
                r, th = divmod(q, 2)
                bk = fill(first["gt"] + q)
                a(gt[r][:, 4 * th:4 * th + 4, :], bk.rearrange("p (t s) -> p t s", t=4)).then_inc(s_trf, 1)
            for i in range(4):
                nb, cc = divmod(i, 2)
                n = unit_no[(ZS_, i)]
                act.wait_ge(s_unit, n + 1)
                if i == 0:
                    act.wait_ge(s_masks, 3)
                a(so[:, nb, cc * HALF:(cc + 1) * HALF], unit_bank(n), ACT.Silu).then_inc(s_eva, 1)
            split_w(3)
            kl = klag[:, :, :].rearrange("p (t g) s -> p g t s", g=2)
            for q in range(4):
                gp, th = divmod(q, 2)
                bk = fill(first["klag"] + q)
                a(kl[:, gp, 4 * th:4 * th + 4, :], bk[0:SC, :].rearrange("p (t s) -> p t s", t=4)).then_inc(s_trf, 1)
            for q in range(4):
                bk = fill(first["ut"] + q)
                if q == 0:
                    act.wait_ge(once("toep"), 16 * CH)
                a(ut[:, 4 * q:4 * q + 4, :], bk.rearrange("p (g s) -> p g s", g=4)).then_inc(s_trf, 1)
            act.wait_ge(once("eang"), 1)
            a(ecos[:, :, :], etmp[:, :, :], ACT.Sin, scale=SIN_2PI / 2).then_inc(once("efn"), 1)
            a(esin[:, :, :], etmp[:, :, :], ACT.Sin, scale=SIN_2PI).then_inc(once("efn"), 1)
            for q in range(4):
                r, th = divmod(q, 2)
                bk = fill(first["bu"] + q)
                dst = (b_r, b_i)[r]
                a(dst[:, 4 * th:4 * th + 4, 1:NCH], bk.rearrange("p (t s) -> p t s", t=4)[:, :, 0:NCH - 1])\
                    .then_inc(s_trf, 1)
            split_w(4)
            for q in range(4):
                bk = fill(first["y"] + q)
                if q == 0:
                    act.wait_ge(once("rot"), 1)
                gp, th = divmod(q, 2)
                yv = ytok[:, :, :].rearrange("p j (t g c) -> p g t j c", g=2, c=SC)
                a(yv[:, gp, 4 * th:4 * th + 4, :, :], bk.rearrange("p (t j c) -> p t j c", t=4, c=SC)).then_inc(s_trf, 1)
            split_w(5)
            for q in range(4):
                ctile, jh = divmod(q, 2)
                bk = fill(first["yt"] + q)
                if q == 0:
                    act.wait_ge(s_trf, first["y"] + 4)
                a(yt[:, ctile, :].rearrange("p (n j) -> p j n", j=CH)[:, 4 * jh:4 * jh + 4, :],
                  bk.rearrange("p (j n) -> p j n", j=4), ACT.Gelu_apprx_tanh).then_inc(s_trf, 1)
            def kc_values(i):
                n = unit_no[(KC_, i)]
                act.wait_ge(s_evd, read_count(reads_d, n + 1))
                if i >= 4:
                    act.wait_ge(s_tr, first["kc"] + 4)
                src = unit_bank(n)[:, P:2 * P].rearrange("p (g d) -> p g d", g=GROUPS)
                a(catc[i % 4][:, 1, :, :, :], src.unsqueeze(2).to_broadcast([P, GROUPS, 2, HD])).then_inc(s_eva, 1)

            def token_rows(hf):
                for q in range(4):
                    bk = fill(first["kc"] + 4 * hf + q)
                    r, g = divmod(q, 2)
                    a(t2[0:HD, r, g, hf * HALF:(hf + 1) * HALF], bk[0:HD, :]).then_inc(once("t2a"), 1)

            for i in range(4):
                kc_values(i)
            for n in range(4):
                act.wait_ge(once("glu"), 2 * n + 1)
                if n >= 1:
                    act.wait_ge(once("glugate"), n)
                a(sg[:, :], bank[0], ACT.Sigmoid).then_inc(once("glusig"), 1)
            act.wait_ge(once("gluo"), 4)
            token_rows(0)
            for i in range(4, ST):
                kc_values(i)
            token_rows(1)
            split_w(6)
            for w in (Z0_, Z1_):
                for i in range(ST):
                    n = unit_no[(w, i)]
                    act.wait_ge(s_unit, n + 1)
                    if w == Z0_:
                        act.wait_ge(s_evd, read_count(reads_d, n + 1))
                    if w == Z0_ and i == 0:
                        act.wait_ge(once("gluo"), 4)
                    o = NGATE if w == Z0_ else 0
                    c0 = 0 if w == Z0_ else 256
                    a(zs[:, i, c0:c0 + 256], unit_bank(n)[:, o:o + 256], ACT.Silu).then_inc(s_eva, 1)
                if w == Z0_:
                    split_w(7)
                    for r in range(2):
                        act.wait_ge(once("hid"), r + 1)
                        act.wait_ge(once("hbias"), r + 1)
                        a(hid[r][:, :], bank[r][:, 0:GROUPS * NCMP], ACT.Gelu_apprx_tanh, bias=hb[:, r:r + 1])\
                            .then_inc(once("hidev"), 1)
                else:
                    split_w(8)
            act.wait_ge(s_evd, read_count(reads_d, unit_no[(Z1_, 0)]))
            a(gates[:, :, :], gates[:, :, :], ACT.Sigmoid).then_inc(once("gates"), 1)
            for b, w in enumerate((KS_, KW_)):
                for i in range(ST):
                    n = unit_no[(w, i)]
                    m = ST * b + i
                    act.wait_ge(s_evd, read_count(reads_d, n + 1))
                    if m == 0:
                        act.wait_ge(once("cmpdone"), 1)
                    a(vv[b][:, i, :, 0:HD], unit_bank(n)[:, P:2 * P].rearrange("p (g d) -> p g d", g=GROUPS))\
                        .then_inc(s_eva, 1)
                    act.wait_ge(once("krot"), m + 1)
                    if m >= 2:
                        act.wait_ge(s_tr, first["ks"] + m - 1)
                    a(kcat[m % 2][:, :, 0, :], rt1[:, 0:P].rearrange("p (g d) -> p g d", g=GROUPS))\
                        .then_inc(once("khi"), 1)
                    bk = fill(first["ks"] + m)
                    a(k1[b][:, :, P * i:P * i + P], bk[:, 0:2 * P].rearrange("p (g s) -> p g s", g=GROUPS))\
                        .then_inc(once("k1"), 1)

            for step in plan:
                if step[0] == "MQ":
                    h = step[1]
                    if h == 0:
                        act.wait_ge(s_unit, len(unit_list))
                        act.wait_ge(once("qrot"), 2 * ST)
                    if h >= 1:
                        act.wait_ge(once("qt"), 2 * h)
                        act.wait_ge(once("qlo"), h)
                    v = qa[:, h // 2, :, HD * (h % 2):HD * (h % 2) + HD]
                    a(qc1[:, :, 0, :], v, scale=1.0 / math.sqrt(HD)).then_inc(once("qhi"), 1)
                    for hf in range(2):
                        act.wait_ge(once("qt"), 2 * h + hf + 1)
                        a(q1[h % 2][:, hf * HALF:(hf + 1) * HALF], bank[7]).then_inc(once("b7"), 1)
                elif step[0] == "MM":
                    h = step[1]
                    for hf in range(2):
                        act.wait_ge(once("mt"), 2 * h + hf + 1)
                        a(q2[h % 2][:, hf * HALF:(hf + 1) * HALF], bank[7]).then_inc(once("b7"), 1)
                elif step[0] == "S":
                    e = step[1]
                    br, cc, j, lo, hi_, dg, bd = units[e % NU]
                    rows = 64 if br == 0 else P
                    act.wait_ge(once("score"), e + 1)
                    if e >= NPT:
                        act.wait_ge(once("pv"), e - NPT + 1)
                    a(pt[e % NPT][0:rows, 0:hi_ - lo], bank[e % 2][0:rows, 0:hi_ - lo], ACT.Exp)\
                        .then_inc(once("exp"), 1)
                elif step[0] == "V":
                    e = step[1]
                    br, cc, j = units[e % NU][0:3]
                    if e % NU + 1 == NU or units[e % NU + 1][0:2] != (br, cc):
                        n = 6 * (e // NU) + 2 * br + cc
                        act.wait_ge(once("pv"), e + 1)
                        if n >= 2:
                            act.wait_ge(once("ot"), n - 1)
                        a(osb[n % 2][:, :], bank[6][0:HD + 1, :]).then_inc(once("osb"), 1)

            def split_d(n):
                rows = KT + (4 if n % 2 == 0 else 2)
                act.wait_ge(once(f"draw{n % 2}"), 32 * (n // 2 + 1))
                if n >= 2:
                    act.wait_ge(once("dgate"), 2 * (n - 1))
                a(dhi[n % 2][:, 0:rows, :], draw[n % 2][:, 0:rows, :]).then_inc(once("dhi"), 1)

            act.wait_ge(once("norm"), 4 * HEADS)
            for r in range(2):
                a(so_hi[:, r, :], so[:, r, :]).then_inc(once("sohi"), 1)
            split_d(0)
            for n in range(8):
                b, hf = divmod(n, 2)
                act.wait_ge(once("att"), n + 1)
                if n == 0:
                    act.wait_ge(once("az"), 4)
                a(at_hi[:, b, hf * HALF:(hf + 1) * HALF], bank[n]).then_inc(once("athi"), 1)
            split_d(1)
            for nb in range(KT):
                for kind in range(2):
                    for cc in range(NC_HALF):
                        m = 4 * nb + 2 * kind + cc
                        act.wait_ge(once("dgate"), m + 1)
                        if m >= 1:
                            act.wait_ge(once("dmul"), m)
                        a(dsig[:, :], bank[2 * (m % 4)], ACT.Sigmoid).then_inc(once("dsig"), 1)
                    if 2 * nb + kind + 2 < 2 * KT:
                        split_d(2 * nb + kind + 2)

            act.wait_ge(once("merged"), 2 * KT)
            for k in range(KT):
                act.wait_ge(once(f"oraw{k}"), 16)
                if k == 0:
                    act.wait_ge(once("dgate"), 4 * KT)
                a(ohi[:, k, :], oraw[:, k, :]).then_inc(once("ohi"), 1)
                if k == 0:
                    split_m = lambda i: a(mhi[i % 2][:, :, :], mt[:, :, P * i:P * i + P]).then_inc(once("mhi"), 1)
                    split_m(0)
            for i in range(ST):
                if i + 1 < ST:
                    if i >= 1:
                        act.wait_ge(once("ounit"), 2 * i)
                    split_m(i + 1)
                act.wait_ge(once("res"), i + 1)
                if i >= 1:
                    act.wait_ge(once("osq"), i)
                a(ojunk[:, :], yr[i % 2][:, :], ACT.Square, accum_out=oss[:, 0, i:i + 1]).then_inc(once("osq"), 1)
                act.wait_ge(once("ovar"), i + 1)
                a(oss[:, 2, i:i + 1], oss[:, 1, i:i + 1], ACT.Sqrt).then_inc(once("osd"), 1)

        @block.vector
        def _(dve):
            ch = Chain(dve, s_ch_d)
            V = nc.vector

            def tt(o, a, b, op):
                return V.tensor_tensor(o, a, b, op)

            dve.wait_ge(s_small, 16 * 8)
            V.tensor_copy(identb[:, :], ident[:, :]).then_inc(once("identb"), 1)
            V.tensor_copy(maskb[:, :, :], mload[:, :, :]).then_inc(s_masks, 1)
            V.tensor_copy(cmpq[:, :, :], cqload[:, :, :]).then_inc(s_masks, 1)
            V.tensor_copy(cmpt[:, :], ctload[:, :]).then_inc(s_masks, 1)
            V.memset(one11[0:1, 0:1], 1.0).then_inc(once("one11"), 1)
            dve.wait_ge(s_sq, ST)
            V.tensor_scalar(ss[:, :], ss[:, :], 1.0 / D_MODEL, EPS, ALU.mult, ALU.add).then_inc(s_var, 1)
            dve.wait_ge(s_sd, 1)
            V.reciprocal(rs[:, :], rs[:, :]).then_inc(s_rs, 1)
            dve.wait_ge(s_rs, 1)
            for i in range(ST):
                V.tensor_scalar(xs[:, i, :], xs[:, i, :], rs[:, i:i + 1], None, ALU.mult).then_inc(s_xn, 1)
            for n in range(1, 16, 2):
                k, cc = divmod(n, 2)
                dve.wait_ge(s_xtr, n + 1)
                V.tensor_copy(xt[:, k, cc * HALF:(cc + 1) * HALF], bank[4 + n % 4]).then_inc(once("xtd"), 1)
            dve.wait_ge(once("den"), 1)
            V.reciprocal(sm[:, 9, :], sm[:, 8, :]).then_inc(once("rden"), 1)
            dve.wait_ge(s_mod, 1)
            for j in range(1, 4, 2):
                V.tensor_copy(mrow[0:1, j * HALF:(j + 1) * HALF], bank[j][0:1, :]).then_inc(once("mrd"), 1)
            dve.wait_ge(s_mcol, 1)
            ch.link(tt(modc[:, :], bank[5][:, 0:2 * KT], bcol[:, :], ALU.add))
            ch.link(V.scalar_tensor_tensor(out=g1[:, :], in0=modc[:, KT:2 * KT], scalar=1.0, in1=gcol[:, :],
                                           op0=ALU.add, op1=ALU.mult))
            dve.wait_ge(once("xta"), 8)

            def h_lo(k):
                dve.wait_ge(s_hhi, k + 1)
                tt(ht_lo[:, k, :], xt[:, k, :], f(ht_hi[:, k, :]), ALU.subtract).then_inc(s_hlo, 1)

            def split_w(w):
                n = CHUNKS[w][1]
                dve.wait_ge(s_whi, w + 1)
                tt(wlo[w % 2][:, :, 0:n], wraw[:, :, 0:n], f(whi[w % 2][:, :, 0:n]), ALU.subtract).then_inc(s_wlo, 1)

            split_w(0)
            for k in range(KT):
                V.tensor_scalar(xt[:, k, :], xt[:, k, :], g1[:, k:k + 1], modc[:, k:k + 1], ALU.mult, ALU.add)\
                    .then_inc(s_h32, 1)
                if k >= 1:
                    h_lo(k - 1)
            h_lo(KT - 1)
            split_w(1)
            split_w(2)
            split_w(3)

            def rotate(src, i, width):
                hn = width // HD
                v = src[:, 0:width].rearrange("p (h a d) -> p h a d", h=hn, a=2)
                a1 = rt1[:, 0:width].rearrange("p (h a d) -> p h a d", h=hn, a=2)
                a2 = rt2[:, 0:width].rearrange("p (h a d) -> p h a d", h=hn, a=2)
                shp = [P, hn, 2, HD // 2]
                cv = rope[:, i, 0, :].rearrange("p (a d) -> p a d", a=2).unsqueeze(1).to_broadcast(shp)
                sv = rope[:, i, 1, :].rearrange("p (a d) -> p a d", a=2).unsqueeze(1).to_broadcast(shp)
                ch.mark(tt(a1, v, cv, ALU.mult))
                tt(a2, v[:, :, ::-1, :], sv, ALU.mult).then_inc(s_evd, 1)
            def q_chunk(w, between=iter(())):
                for i in range(ST):
                    n = unit_no[(w, i)]
                    dve.wait_ge(s_unit, n + 1)
                    if w == Q0_ and i == 0:
                        dve.wait_ge(s_tr, first["ut"] + 4)
                        dve.wait_ge(once("efn"), 2)
                    if (w, i) != (Q0_, 0):
                        dve.wait_ge(once("qrot"), ST * (w - Q0_) + i)
                    rotate(unit_bank(n), i, 256)
                    dve.wait_ge(s_evd, read_count(reads_d, n + 1))
                    dst = qa[:, 2 * (w - Q0_):2 * (w - Q0_) + 2, i, :]
                    ch.wait()
                    tt(dst, rt1[:, :].rearrange("p (b d) -> p b d", b=2), rt2[:, :].rearrange("p (b d) -> p b d", b=2),
                       ALU.add).then_inc(once("qrot"), 1)
                    for _ in range(3):
                        next(between, None)
                for _ in between:
                    pass

            def states():
                bR, bI, zR, zI, eC, eS = (t[:, :, :] for t in (b_r, b_i, zr, zi, ecos, esin))
                yield ch.mark(V.memset(b_r[:, :, 0:1], 0.0))
                yield ch.link(V.memset(b_i[:, :, 0:1], 0.0))
                yield ch.link(tt(zR, bR, eC, ALU.mult))
                yield ch.link(tt(zI, bI, eS, ALU.mult))
                yield ch.link(tt(zR, zR, zI, ALU.add))
                yield ch.link(tt(zI, bR, eS, ALU.mult))
                yield ch.link(tt(bI, bI, eC, ALU.mult))
                yield ch.link(tt(bI, bI, zI, ALU.subtract))
                for t in range(SSM_T):
                    d0 = sm[:, 4, t:t + 1].to_broadcast([P, NCH])
                    ch.mark(V.tensor_tensor_scan(b_r[:, t, :], d0, zr[:, t, :], 0.0, ALU.mult, ALU.add))
                    yield ch.mark(V.tensor_tensor_scan(zi[:, t, :], d0, b_i[:, t, :], 0.0, ALU.mult, ALU.add))
                ch.wait()
                yield ch.link(tt(zR, bR, eC, ALU.mult))
                yield ch.link(tt(bI, zI, eS, ALU.mult))
                yield ch.link(tt(zR, zR, bI, ALU.subtract))
                yield ch.link(tt(bI, bR, eS, ALU.mult))
                yield ch.link(tt(zI, zI, eC, ALU.mult))
                yield tt(zI, zI, bI, ALU.add).then_inc(once("rot"), 1)

            q_chunk(Q0_)
            split_w(4)
            dve.wait_ge(s_trf, first["bu"] + 4)
            dve.wait_ge(once("ecos"), 1)
            q_chunk(Q1_, states())
            split_w(5)

            def kc_keys(i):
                n = unit_no[(KC_, i)]
                dve.wait_ge(s_unit, n + 1)
                if i == 0:
                    dve.wait_ge(s_trf, first["yt"] + 4)
                if i >= 1:
                    dve.wait_ge(once("kcat"), i)
                else:
                    dve.wait_ge(once("qrot"), 2 * ST)
                rotate(unit_bank(n), i, P)
                dve.wait_ge(s_evd, read_count(reads_d, n + 1))
                if i >= 4:
                    dve.wait_ge(s_tr, first["kc"] + 4)
                shp = [P, GROUPS, 2, HD]
                ch.wait()
                tt(catc[i % 4][:, 0, :, :, :],
                   rt1[:, 0:P].rearrange("p (g d) -> p g d", g=GROUPS).unsqueeze(2).to_broadcast(shp),
                   rt2[:, 0:P].rearrange("p (g d) -> p g d", g=GROUPS).unsqueeze(2).to_broadcast(shp),
                   ALU.add).then_inc(once("kcat"), 1)

            def next_rows(hf):
                for q in range(4):
                    fl = first["kc"] + 4 * hf + q
                    r, g = divmod(q, 2)
                    dve.wait_ge(s_tr, fl + 1)
                    dve.wait_ge(once("t2a"), 4 * hf + q + 1)
                    lo = hf * HALF
                    s0 = 1 if hf == 0 else 0
                    V.tensor_copy(t2[HD:P, r, g, lo + s0 - 1:lo + HALF - 1], bank[fl % 2][HD:P, s0:HALF])\
                        .then_inc(s_trf, 1)

            for i in range(4):
                kc_keys(i)
            for n in range(4):
                nb, cc = divmod(n, 2)
                dve.wait_ge(once("glu"), 2 * n + 2)
                dve.wait_ge(once("glugate"), n + 1)
                v = so[:, nb, cc * HALF:(cc + 1) * HALF]
                tt(v, bank[1], v, ALU.mult).then_inc(once("gluo"), 1)
            next_rows(0)
            for i in range(4, ST):
                kc_keys(i)
            next_rows(1)
            split_w(6)
            for i in range(ST):
                n = unit_no[(Z0_, i)]
                dve.wait_ge(s_unit, n + 1)
                V.tensor_copy(gates[:, i, :], unit_bank(n)[:, 0:NGATE]).then_inc(s_evd, 1)
            split_w(7)
            for r in range(2):
                dve.wait_ge(once("pe"), 2)
                dve.wait_ge(once("cmpw"), 16 * 8)
                tt(hb[:, r:r + 1], bank[2][:, r:r + 1], b1c[r][:, :], ALU.add).then_inc(once("hbias"), 1)
            V.tensor_copy(w2d[:, :, :], w2[0][:, :].unsqueeze(1).to_broadcast([P, 2, HD])).then_inc(once("w2d"), 1)
            ch.mark(V.memset(f(k1c[:, :, :]), 0.0))
            ch.link(V.memset(f(k2c[:, :, :]), 0.0))
            dve.wait_ge(once("kcps"), 1)
            kp = bank[2][:, 2:2 + GROUPS * NCMP]
            kp3 = kp.rearrange("p (g n) -> p g n", g=GROUPS)
            ch.mark(V.tensor_copy(k1c[0:HD, :, 0:NCMP], kp3[0:HD]))
            ch.mark(V.tensor_copy(k2c[0:HD, :, 0:NCMP], kp3[0:HD]))
            ch.link(V.tensor_copy(kch[HD:P, :], kp[HD:P]))
            ch.link(tt(k1c[HD:P, :, 0:NCMP], kp3[HD:P], f(kch[HD:P, :]).rearrange("p (g n) -> p g n", g=GROUPS),
                       ALU.subtract))
            ch.link(V.tensor_copy(k2c[HD:P, :, :], aug[HD:P, 0:1].unsqueeze(1).to_broadcast([HD, GROUPS, 64])))
            dve.wait_ge(once("vcps"), 1)
            dve.wait_ge(once("vc0"), 2)
            for g in range(GROUPS):
                ch.mark(V.tensor_copy(vc[0:NCMP, g, 0:HD], bank[3][0:NCMP, HD * g:HD * g + HD]))
            V.memset(vc[:, :, HD:HD + 1], 1.0).then_inc(once("cmpdone"), 1)
            split_w(8)
            for b in range(2):
                ch.mark(V.memset(vv[b][:, :, :, HD:VW], 1.0))
                ch.mark(V.tensor_copy(k2[b][HD:P, :, :],
                                      aug[HD:P, b + 1:b + 2].unsqueeze(1).to_broadcast([HD, GROUPS, SEQ])))
            for b, w in enumerate((KS_, KW_)):
                for i in range(ST):
                    n = unit_no[(w, i)]
                    m = ST * b + i
                    dve.wait_ge(s_unit, n + 1)
                    if m >= 1:
                        dve.wait_ge(once("klo"), m)
                    rotate(unit_bank(n), i, P)
                    dve.wait_ge(s_evd, read_count(reads_d, n + 1))
                    ch.wait()
                    tt(rt1[:, 0:P], rt1[:, 0:P], rt2[:, 0:P], ALU.add).then_inc(once("krot"), 1)
                    dve.wait_ge(once("krot"), m + 1)
                    dve.wait_ge(once("khi"), m + 1)
                    kc_ = kcat[m % 2]
                    tt(kc_[:, :, 1, :], rt1[:, 0:P].rearrange("p (g d) -> p g d", g=GROUPS),
                       f(kc_[:, :, 0, :]), ALU.subtract).then_inc(once("klo"), 1)
                    fl = first["ks"] + m
                    dve.wait_ge(s_tr, fl + 1)
                    dve.wait_ge(once("k1"), m + 1)
                    V.tensor_copy(k2[b][0:HD, :, P * i:P * i + P],
                                  bank[fl % 2][0:HD, 0:2 * P].rearrange("p (g s) -> p g s", g=GROUPS))\
                        .then_inc(s_trf, 1)

            dve.wait_ge(s_unit, len(unit_list))
            ch.link(V.memset(qc2[:, :, :], 0.0))
            for step in plan:
                if step[0] == "MQ":
                    h = step[1]
                    dve.wait_ge(once("qhi"), h + 1)
                    if h >= 1:
                        dve.wait_ge(once("mt"), 2 * h)
                    v = qa[:, h // 2, :, HD * (h % 2):HD * (h % 2) + HD]
                    V.scalar_tensor_tensor(out=qc2[:, :, 0:HD], in0=v, scalar=1.0 / math.sqrt(HD),
                                           in1=f(qc1[:, :, 0, :]), op0=ALU.mult, op1=ALU.subtract)\
                        .then_inc(once("qlo"), 1)
                elif step[0] == "MX":
                    _, h, i = step
                    n = ST * h + i
                    m = mx[h % 2]
                    dve.wait_ge(once("ms"), n + 1)
                    V.tensor_reduce(m[:, i, 1:2], slc_max[:, 0:P * (i + 1)], AX.X, ALU.max).then_inc(once("msr"), 1)
                    dve.wait_ge(once("mw"), n + 1)
                    ch.mark(V.tensor_reduce(m[:, i, 0:1], win_max[:, 640:704], AX.X, ALU.max))
                    V.tensor_reduce(m[:, i, 2:3], win_max[:, 0:P * min(i + 1, WIN_TILES + 1)], AX.X, ALU.max)\
                        .then_inc(once("mwr"), 1)
                    if i == ST - 1:
                        dve.wait_ge(once("mwr"), n + 1)
                        ch.link(V.tensor_scalar(mneg[:, :, :], m[:, :, :], MAX_FLOOR, -1.0, ALU.max, ALU.mult))
                        q2v = qc2[:, :, HD:HD + 6].rearrange("p i (b a) -> p i b a", a=2)
                        ch.link(V.tensor_copy(mneg_hi[:, :, :], mneg[:, :, :]))
                        ch.link(V.tensor_copy(q2v[:, :, :, 0], f(mneg_hi[:, :, :])))
                        tt(q2v[:, :, :, 1], mneg[:, :, :], f(mneg_hi[:, :, :]), ALU.subtract).then_inc(once("mcat"), 1)
                        dve.wait_ge(once("mcat"), h + 1)
                elif step[0] == "N":
                    n = step[1]
                    h, r = divmod(n, 6)
                    br, cc = divmod(r, 2)
                    dve.wait_ge(once("ot"), n + 1)
                    if n == 0:
                        dve.wait_ge(once("gates"), 1)
                    o3 = bank[7][:, 0:4 * VW].rearrange("p (i d) -> p i d", i=4)
                    ch.link(V.tensor_scalar(lsum[:, :], o3[:, :, HD], TINY, None, ALU.max))
                    ch.link(V.reciprocal(lsum[:, :], lsum[:, :]))
                    ch.link(tt(wrow[:, :], lsum[:, :], gates[:, 4 * cc:4 * cc + 4, 3 * h + br], ALU.mult))
                    dst = qa[:, h // 2, 4 * cc:4 * cc + 4, HD * (h % 2):HD * (h % 2) + HD]
                    wb = wrow[:, :].unsqueeze(2).to_broadcast([P, 4, HD])
                    if br == 0:
                        tt(dst, o3[:, :, 0:HD], wb, ALU.mult).then_inc(once("b7"), 1)
                        dve.wait_ge(once("b7"), b7_after[step])
                    else:
                        tt(otmp[:, :, :], o3[:, :, 0:HD], wb, ALU.mult).then_inc(once("b7"), 1)
                        dve.wait_ge(once("b7"), b7_after[step])
                        tt(dst, dst, otmp[:, :, :], ALU.add).then_inc(once("norm"), 1)
                        dve.wait_ge(once("norm"), 4 * h + r - 1)

            def split_d(n):
                rows = KT + (4 if n % 2 == 0 else 2)
                dve.wait_ge(once("dhi"), n + 1)
                tt(dlo[n % 2][:, 0:rows, :], draw[n % 2][:, 0:rows, :], f(dhi[n % 2][:, 0:rows, :]), ALU.subtract)\
                    .then_inc(once("dlo"), 1)

            for r in range(2):
                dve.wait_ge(once("sohi"), r + 1)
                tt(so_lo[:, r, :], so[:, r, :], f(so_hi[:, r, :]), ALU.subtract).then_inc(once("sosplit"), 1)
            split_d(0)
            for n in range(8):
                b, hf = divmod(n, 2)
                dve.wait_ge(once("athi"), n + 1)
                dve.wait_ge(once("att"), 2 * b + 2)
                tt(at_lo[:, b, hf * HALF:(hf + 1) * HALF], bank[n],
                   f(at_hi[:, b, hf * HALF:(hf + 1) * HALF]), ALU.subtract).then_inc(once("atlo"), 1)
            split_d(1)
            for nb in range(KT):
                for kind in range(2):
                    for cc in range(NC_HALF):
                        m = 4 * nb + 2 * kind + cc
                        dve.wait_ge(once("dsig"), m + 1)
                        dve.wait_ge(once("dproj"), m + 1)
                        dst = mt[:, nb, cc * HALF:(cc + 1) * HALF]
                        if kind == 0:
                            tt(dst, bank[2 * (m % 4) + 1], dsig[:, :], ALU.mult).then_inc(once("dmul"), 1)
                        else:
                            tt(dtm[:, :], bank[2 * (m % 4) + 1], dsig[:, :], ALU.mult).then_inc(once("dmul"), 1)
                            dve.wait_ge(once("dmul"), m + 1)
                            tt(dst, dst, dtm[:, :], ALU.add).then_inc(once("merged"), 1)
                            dve.wait_ge(once("merged"), 2 * nb + cc + 1)
                    if 2 * nb + kind + 2 < 2 * KT:
                        split_d(2 * nb + kind + 2)

            for k in range(KT):
                dve.wait_ge(once("ohi"), k + 1)
                tt(olo[:, k, :], oraw[:, k, :], f(ohi[:, k, :]), ALU.subtract).then_inc(once("olo"), 1)
                if k == 0:
                    def split_m(i):
                        dve.wait_ge(once("mhi"), i + 1)
                        tt(mlo[i % 2][:, :, :], mt[:, :, P * i:P * i + P], f(mhi[i % 2][:, :, :]), ALU.subtract)\
                            .then_inc(once("mlo"), 1)
                    split_m(0)
            dve.wait_ge(once("gps"), 1)
            dve.wait_ge(once("gbias"), 16)
            for hf in range(2):
                s = slice(HALF * hf, HALF * hf + HALF)
                ch.mark(tt(gateb[:, s], bank[6 + hf], gbias[:, s], ALU.add))
            ch.wait()
            dve.wait_ge(once("fgb"), 16)
            for i in range(ST):
                if i + 1 < ST:
                    split_m(i + 1)
                dve.wait_ge(once(f"xr{i % 2}"), 16 * (i // 2 + 1))
                if i >= 2:
                    dve.wait_ge(once(f"out{i % 2}"), 16 * (i // 2))
                y = yr[i % 2]
                for hf in range(2):
                    s = slice(HALF * hf, HALF * hf + HALF)
                    dve.wait_ge(once("ounit"), 2 * i + hf + 1)
                    tt(y[:, s], bank[2 * (i % 2) + hf], gateb[:, s], ALU.mult).then_inc(once("oread"), 1)
                dve.wait_ge(once("oread"), 2 * i + 2)
                tt(y[:, :], y[:, :], xr[i % 2][:, :], ALU.add).then_inc(once("res"), 1)
                dve.wait_ge(once("osq"), i + 1)
                V.tensor_scalar(oss[:, 1, i:i + 1], oss[:, 0, i:i + 1], 1.0 / D_MODEL, EPS, ALU.mult, ALU.add)\
                    .then_inc(once("ovar"), 1)
                dve.wait_ge(once("osd"), i + 1)
                ch.link(V.reciprocal(oss[:, 2, i:i + 1], oss[:, 2, i:i + 1]))
                V.scalar_tensor_tensor(out=y[:, :], in0=y[:, :], scalar=oss[:, 2, i:i + 1], in1=fgb[:, :],
                                       op0=ALU.mult, op1=ALU.mult).then_inc(once("y"), 1)

        @block.tensor
        def _(pe):
            T = nc.tensor

            def mm(o, l, r, start, stop, **kw):
                return T.matmul(o, l, r, start=start, stop=stop, **kw)

            def tr(o, i, rows=P):
                return T.transpose(o, i, ident[0:rows, 0:rows])

            def three(o, parts, start=True, stop=True, **kw):
                n = 3 * len(parts)
                m = 0
                for lh, ll, rh, rl in parts:
                    for l, r in ((lh, rh), (lh, rl), (ll, rh)):
                        ins = mm(o, l, r, start and m == 0, stop and m == n - 1, **kw)
                        m += 1
                return ins

            def ada_mm(k):
                pe.wait_ge(s_ada[k], 16)
                for j in range(4):
                    ins = mm(bank[j][0:1, :], scol[:, k:k + 1], ada[:, k, j * HALF:(j + 1) * HALF],
                             k == 0, k == KT - 1)
                return ins
            pe.wait_ge(s_silu, 1)
            ada_mm(0)
            ada_mm(1)
            pe.wait_ge(s_small, 16 * 8)
            pe.wait_ge(s_xn, ST)
            for n in range(16):
                k, cc = divmod(n, 2)
                if n >= 4:
                    if n % 2 == 0:
                        pe.wait_ge(once("xta"), (n - 4) // 2 + 1)
                    else:
                        pe.wait_ge(once("xtd"), (n - 5) // 2 + 1)
                for q in range(4):
                    ins = tr(bank[4 + n % 4][:, P * q:P * q + P], xs[:, 4 * cc + q, P * k:P * k + P])
                ins.then_inc(s_xtr, 1)
            pe.wait_ge(once("cld"), 16 * 2 * SSM_T)
            pe.wait_ge(once("xta"), 7)
            for r in range(2):
                ins = tr(bank[4][:, P * r:P * r + P], cld[r][:, :])
            ins.then_inc(once("ctr"), 1)
            for k in range(2, KT):
                ins = ada_mm(k)
            ins.then_inc(s_mod, 1)
            pe.wait_ge(once("mra"), 2)
            pe.wait_ge(once("mrd"), 2)
            pe.wait_ge(once("one11"), 1)
            pe.wait_ge(once("xtd"), 8)
            for j in range(2 * KT):
                ins = mm(bank[5][:, j:j + 1], mrow[0:1, P * j:P * j + P], one11[0:1, 0:1], True, True)
            ins.then_inc(s_mcol, 1)

            def bank_free(n):
                m = n - 4
                if m < ST:
                    return
                if read_count(reads_d, m + 1):
                    pe.wait_ge(s_evd, read_count(reads_d, m + 1))
                pe.wait_ge(s_eva, read_count(reads_a, m + 1))

            def fill_free(n):
                if n >= 2:
                    pe.wait_ge(s_trf, n - 1)

            pe.wait_ge(s_whi, 1)
            pe.wait_ge(s_wlo, 1)
            for k in range(KT):
                pe.wait_ge(s_hlo, k + 1)
                for j in range(ST):
                    tok = slice(j, SEQ, CH)
                    parts = ((ht_hi, whi[0]), (ht_hi, wlo[0]), (ht_lo, whi[0]))
                    for m, (l, r) in enumerate(parts):
                        ins = mm(unit_bank(j), l[:, k, tok], r[:, k, 0:256],
                                 k == 0 and m == 0 and j % 2 == 0, k == KT - 1 and m == 2,
                                 skip_group_check=True)
            ins.then_inc(s_unit, ST)

            def project(w, tiles=range(ST)):
                pe.wait_ge(s_whi, w + 1)
                pe.wait_ge(s_wlo, w + 1)
                wh, wl = whi[w % 2], wlo[w % 2]
                for i in tiles:
                    n = unit_no[(w, i)]
                    bank_free(n)
                    if w == ZS_:
                        nb, cc = divmod(i, 2)
                        cs, ts = slice(P * nb, P * nb + P), slice(cc * HALF, (cc + 1) * HALF)
                        ins = three(unit_bank(n), [(wh[:, k, cs], wl[:, k, cs], ht_hi[:, k, ts], ht_lo[:, k, ts])
                                                   for k in range(KT)])
                    else:
                        width, ts = CHUNKS[w][1], slice(P * i, P * i + P)
                        ins = three(unit_bank(n)[:, 0:width],
                                    [(ht_hi[:, k, ts], ht_lo[:, k, ts], wh[:, k, 0:width], wl[:, k, 0:width])
                                     for k in range(KT)])
                    ins.then_inc(s_unit, 1)

            pe.wait_ge(once("gs"), 2)
            pe.wait_ge(s_eva, ST)
            for q in range(4):
                r, th = divmod(q, 2)
                n = first["gt"] + q
                fill_free(n)
                for t in range(4):
                    ins = tr(bank[n % 2][:, P * t:P * t + P],
                             gs[r][:, 4 * th + t, :, :].rearrange("p j c -> p (j c)"))
                ins.then_inc(s_tr, 1)
            project(ZS_, range(4))
            pe.wait_ge(once("cp"), 1)
            for q in range(4):
                gp, th = divmod(q, 2)
                n = first["klag"] + q
                fill_free(n)
                s = slice(SS * gp, SS * gp + SS)
                for m in range(4):
                    t = 4 * th + m
                    for r in range(2):
                        ins = mm(bank[n % 2][0:SC, P * m:P * m + P], bbar[r][s, t, :],
                                 cp[r][s, t, 0:CH, :].rearrange("p j c -> p (j c)"), r == 0, r == 1)
                ins.then_inc(s_tr, 1)
            for q in range(4):
                n = first["ut"] + q
                fill_free(n)
                for m in range(4):
                    ins = tr(bank[n % 2][:, P * m:P * m + P],
                             utok[:, 4 * q + m, :, :].rearrange("p j c -> p (j c)"))
                ins.then_inc(s_tr, 1)
            project(Q0_)
            pe.wait_ge(s_trf, first["ut"] + 4)
            for q in range(4):
                r, th = divmod(q, 2)
                n = first["bu"] + q
                fill_free(n)
                for m in range(4):
                    t = 4 * th + m
                    for gp in range(2):
                        ins = mm(bank[n % 2][SS * gp:SS * gp + SS, P * m:P * m + P],
                                 gt[r][:, t, SS * gp:SS * gp + SS], ut[:, 2 * t + gp, :], True, True)
                ins.then_inc(s_tr, 1)
            project(Q1_)
            pe.wait_ge(once("rot"), 1)
            pe.wait_ge(once("toep"), 16 * CH)
            for q in range(4):
                n = first["y"] + q
                fill_free(n)
                gp, th = divmod(q, 2)
                s = slice(SS * gp, SS * gp + SS)
                for m in range(4):
                    t = 4 * th + m
                    g = 2 * t + gp
                    o = bank[n % 2][:, P * m:P * m + P]
                    for r, st in enumerate((zr, zi)):
                        mm(o, st[s, t, :], cp[r][s, t, 1:9, :].rearrange("p j c -> p (j c)"), r == 0, False)
                    ins = mm(o, ut[:, g, :], toep[:, g, :], False, True)
                ins.then_inc(s_tr, 1)
            project(KC_, range(4))
            pe.wait_ge(s_trf, first["y"] + 4)
            for q in range(4):
                ctile, jh = divmod(q, 2)
                n = first["yt"] + q
                fill_free(n)
                for m in range(4):
                    ins = tr(bank[n % 2][:, P * m:P * m + P], ytok[:, 4 * jh + m, P * ctile:P * ctile + P])
                ins.then_inc(s_tr, 1)
            project(KC_, range(4, ST))
            pe.wait_ge(once("wglu"), 16)
            pe.wait_ge(s_trf, first["yt"] + 4)
            for n in range(4):
                nb, cc = divmod(n, 2)
                for part in range(2):
                    if n >= 1:
                        pe.wait_ge(once("glusig" if part == 0 else "gluo"), n)
                    col = P * (nb + 2 * (1 - part))
                    for k in range(2):
                        ins = mm(bank[part], wglu[:, k, col:col + P], yt[:, k, cc * HALF:(cc + 1) * HALF],
                                 k == 0, k == 1)
                    ins.then_inc(once("glu"), 1)
            pe.wait_ge(once("gluo"), 4)
            pe.wait_ge(once("glusig"), 4)
            for hf in range(2):
                pe.wait_ge(once("kcat"), 4 * (hf + 1))
                pe.wait_ge(s_eva, read_count(reads_a, unit_no[(KC_, 4 * hf + 3)] + 1))
                for q in range(4):
                    r, g = divmod(q, 2)
                    n = first["kc"] + 4 * hf + q
                    if 4 * hf + q >= 2:
                        fill_free(n)
                    for m in range(4):
                        ins = tr(bank[n % 2][:, P * m:P * m + P],
                                 catc[m][:, r, g, :, :].rearrange("p a d -> p (a d)"))
                    ins.then_inc(s_tr, 1)
                project(Z0_, range(3) if hf == 0 else range(3, ST))
            pe.wait_ge(once("cmpw"), 16 * 8)
            pe.wait_ge(s_trf, first["kc"] + 8)
            for r in range(2):
                o = bank[r][:, 0:GROUPS * NCMP].rearrange("p (g n) -> p g n", g=GROUPS)
                for m in range(PAIRS):
                    ins = mm(o, w1[r][:, m, :], t2[:, r, :, 2 * m:2 * m + CMP_STRIDE * (NCMP - 1) + 1:CMP_STRIDE],
                             m == 0, m == PAIRS - 1)
                ins.then_inc(once("hid"), 1)
                for m in range(PAIRS):
                    ins = mm(bank[2][:, r:r + 1], w1[r][:, m, :], pec[r][:, m:m + 1], m == 0, m == PAIRS - 1)
                ins.then_inc(once("pe"), 1)
            pe.wait_ge(once("hbias"), 2)
            pe.wait_ge(once("w2d"), 1)
            pe.wait_ge(once("hidev"), 1)
            mm(bank[2][:, 2:2 + GROUPS * NCMP], w2d[:, :, :].rearrange("p a d -> p (a d)"), hid[0][:, :],
               True, True).then_inc(once("kcps"), 1)
            pe.wait_ge(once("hidev"), 2)
            for g in range(GROUPS):
                ins = mm(bank[3][0:NCMP, HD * g:HD * g + HD], hid[1][:, NCMP * g:NCMP * g + NCMP], w2[1][:, :],
                         True, True)
            ins.then_inc(once("vcps"), 1)
            project(Z1_)

            def project_keys(b, w):
                pe.wait_ge(s_whi, w + 1)
                pe.wait_ge(s_wlo, w + 1)
                wh, wl = whi[w % 2], wlo[w % 2]
                for i in range(ST + 1):
                    if i < ST:
                        n = unit_no[(w, i)]
                        bank_free(n)
                        ts = slice(P * i, P * i + P)
                        three(unit_bank(n)[:, 0:256],
                              [(ht_hi[:, k, ts], ht_lo[:, k, ts], wh[:, k, 0:256], wl[:, k, 0:256])
                               for k in range(KT)]).then_inc(s_unit, 1)
                    if i >= 1:
                        m = ST * b + i - 1
                        n = first["ks"] + m
                        pe.wait_ge(once("klo"), m + 1)
                        fill_free(n)
                        for g in range(GROUPS):
                            ins = tr(bank[n % 2][:, P * g:P * g + P],
                                     f(kcat[m % 2][:, g, :, :]).rearrange("p a d -> p (a d)"))
                        ins.then_inc(s_tr, 1)
            project_keys(0, KS_)
            project_keys(1, KW_)

            K1 = lambda br, g, s: k1c[:, g, :] if br == 0 else k1[br - 1][:, g, s]
            K2 = lambda br, g, s: k2c[:, g, :] if br == 0 else k2[br - 1][:, g, s]
            b7 = 0
            pe.wait_ge(s_trf, first["kw"] + 8)
            pe.wait_ge(once("k1"), 2 * ST)
            pe.wait_ge(s_eva, read_count(reads_a, len(unit_list)))
            pe.wait_ge(s_evd, read_count(reads_d, len(unit_list)))
            pe.wait_ge(s_masks, 3)
            for step in plan:
                if step[0] == "MQ":
                    h = step[1]
                    pe.wait_ge(once("qdup"), h + 1)
                    for hf in range(2):
                        if b7:
                            pe.wait_ge(once("b7"), b7)
                        for q in range(4):
                            ins = tr(bank[7][:, P * q:P * q + P],
                                     f(qc1[:, 4 * hf + q, :, :]).rearrange("p a d -> p (a d)"))
                        ins.then_inc(once("qt"), 1)
                        b7 += 1
                    q1_ready = b7
                elif step[0] == "MX":
                    _, h, i = step
                    n, g = ST * h + i, h // HPG
                    if i == 0:
                        pe.wait_ge(once("b7"), q1_ready)
                    lhs = q1[h % 2][:, P * i:P * i + P]
                    if n >= 1:
                        pe.wait_ge(once("msr"), n)
                    for s0 in range(0, i + 1, 4):
                        s1 = min(s0 + 4, i + 1)
                        mm(slc_max[:, P * s0:P * s1], lhs, k1[0][:, g, P * s0:P * s1], True, s1 != i + 1)
                    mm(slc_max[:, P * i:P * i + P], identb[:, :], maskb[:, 0, :], False, True).then_inc(once("ms"), 1)
                    if n >= 1:
                        pe.wait_ge(once("mwr"), n)
                    j0 = max(0, i - WIN_TILES)
                    cnt = i + 1 - j0
                    for s0 in range(0, cnt, 4):
                        s1 = min(s0 + 4, cnt)
                        mm(win_max[:, P * s0:P * s1], lhs, k1[1][:, g, P * (j0 + s0):P * (j0 + s1)], True, False)
                    if i >= WIN_TILES:
                        mm(win_max[:, 0:P], identb[:, :], maskb[:, 1, :], False, True)
                    mm(win_max[:, P * (cnt - 1):P * cnt], identb[:, :], maskb[:, 0, :], False, True)
                    mm(win_max[:, 640:704], lhs, k1c[:, g, :], True, False)
                    mm(win_max[:, 640:704], identb[:, :], cmpq[:, i, :], False, True)\
                        .then_inc(once("mw"), 1)
                elif step[0] == "MM":
                    h = step[1]
                    pe.wait_ge(once("mcat"), h + 1)
                    pe.wait_ge(once("qlo"), h + 1)
                    for hf in range(2):
                        pe.wait_ge(once("b7"), b7)
                        for q in range(4):
                            ins = tr(bank[7][:, P * q:P * q + P], qc2[:, 4 * hf + q, :])
                        ins.then_inc(once("mt"), 1)
                        b7 += 1
                    q2_ready = b7
                elif step[0] == "S":
                    e = step[1]
                    h, u = divmod(e, NU)
                    g = h // HPG
                    br, cc, j, lo, hi_, dg, bd = units[u]
                    if u == 0:
                        pe.wait_ge(once("b7"), q2_ready)
                    if e >= 2:
                        pe.wait_ge(once("exp"), e - 1)
                    rows, n = (64 if br == 0 else P), hi_ - lo
                    o = bank[e % 2][0:rows, 0:n]
                    ks = slice(P * j, P * j + P)
                    mm(o, K1(br, g, ks), q1[h % 2][:, lo:hi_], True, False)
                    ins = mm(o, K2(br, g, ks), q2[h % 2][:, lo:hi_], False, not (dg or bd or br == 0))
                    if br == 0:
                        ins = mm(o, identb[0:64, 0:64], cmpt[:, lo:hi_], False, True)
                    if dg:
                        ins = mm(o[:, 0:P], maskb[:, 0, :], identb[:, :], False, not bd)
                    if bd:
                        ins = mm(o[:, n - P:n], maskb[:, 1, :], identb[:, :], False, True)
                    ins.then_inc(once("score"), 1)
                elif step[0] == "V":
                    e = step[1]
                    h, u = divmod(e, NU)
                    g = h // HPG
                    br, cc, j, lo, hi_, dg, bd = units[u]
                    is_first = u == 0 or units[u - 1][0:2] != (br, cc)
                    is_last = u == NU - 1 or units[u + 1][0:2] != (br, cc)
                    n = 6 * h + 2 * br + cc
                    if is_first and n >= 1:
                        pe.wait_ge(once("osb"), n)
                    pe.wait_ge(once("exp"), e + 1)
                    rows = 64 if br == 0 else P
                    v = vc[:, g, 0:HD + 1] if br == 0 else vv[br - 1][:, j, g, 0:HD + 1]
                    mm(bank[6][0:HD + 1, lo - HALF * cc:hi_ - HALF * cc], v, pt[e % NPT][0:rows, 0:hi_ - lo],
                       is_first, is_last).then_inc(once("pv"), 1)
                else:
                    n = step[1]
                    pe.wait_ge(once("osb"), n + 1)
                    pe.wait_ge(once("b7"), b7)
                    for q in range(4):
                        ins = tr(bank[7][:, VW * q:VW * q + HD + 1], osb[n % 2][:, P * q:P * q + P], HD + 1)
                    ins.then_inc(once("ot"), 1)
                    b7 += 1

            pe.wait_ge(once("b7"), b7)
            pe.wait_ge(once("az"), 4)
            pe.wait_ge(once("mwr"), ST * HEADS)
            for n in range(8):
                b, hf = divmod(n, 2)
                for q in range(4):
                    ins = tr(bank[n][:, P * q:P * q + P], qa[:, b, 4 * hf + q, :])
                ins.then_inc(once("att"), 1)
            pe.wait_ge(once("sosplit"), 2)
            for nb in range(KT):
                for kind in range(2):
                    n = 2 * nb + kind
                    wh, wl = dhi[n % 2], dlo[n % 2]
                    pe.wait_ge(once("dhi"), n + 1)
                    pe.wait_ge(once("dlo"), n + 1)
                    bh, bl, kp = (at_hi, at_lo, 4) if kind == 0 else (so_hi, so_lo, 2)
                    for cc in range(NC_HALF):
                        m = 2 * n + cc
                        ts = slice(cc * HALF, (cc + 1) * HALF)
                        if n == 0 and cc == 0:
                            pe.wait_ge(once("atlo"), 8)
                        if m >= 4:
                            pe.wait_ge(once("dmul"), m - 3)
                        three(bank[2 * (m % 4) + 1],
                              [(wh[:, KT + k, :], wl[:, KT + k, :], bh[:, k, ts], bl[:, k, ts])
                               for k in range(kp)]).then_inc(once("dproj"), 1)
                    for cc in range(NC_HALF):
                        m = 2 * n + cc
                        ts = slice(cc * HALF, (cc + 1) * HALF)
                        three(bank[2 * (m % 4)],
                              [(wh[:, k, :], wl[:, k, :], ht_hi[:, k, ts], ht_lo[:, k, ts])
                               for k in range(KT)]).then_inc(once("dgate"), 1)

            pe.wait_ge(once("merged"), 2 * KT)
            pe.wait_ge(once("gacc"), 1)
            for hf in range(2):
                ins = mm(bank[6 + hf], onesq[:, :], gacc[:, HALF * hf:HALF * hf + HALF], True, True)
            ins.then_inc(once("gps"), 1)
            for i in range(ST):
                pe.wait_ge(once("mhi"), i + 1)
                pe.wait_ge(once("mlo"), i + 1)
                if i >= 2:
                    pe.wait_ge(once("oread"), 2 * i - 2)
                m0 = 0
                for k in range(KT):
                    if i == 0:
                        pe.wait_ge(once("ohi"), k + 1)
                        pe.wait_ge(once("olo"), k + 1)
                    for hf in range(2):
                        s = slice(HALF * hf, HALF * hf + HALF)
                        o = bank[2 * (i % 2) + hf]
                        mh, ml = mhi[i % 2][:, k, :], mlo[i % 2][:, k, :]
                        for q, (l, r) in enumerate(((mh, ohi), (mh, olo), (ml, ohi))):
                            ins = mm(o, l, r[:, k, s], k == 0 and q == 0, k == KT - 1 and q == 2)
                        if k == KT - 1:
                            ins.then_inc(once("ounit"), 1)


_INS = ["x", "c", "w_ada", "b_ada", "norm_gain", "w_in", "pe_cmp_k", "w_cmp_k1", "b_cmp_k1", "w_cmp_k2",
        "pe_cmp_v", "w_cmp_v1", "b_cmp_v1", "w_cmp_v2", "lam_re", "lam_im", "log_dt", "b_re", "b_im",
        "c_re", "c_im", "d_skip", "w_glu", "w_proj_attn", "w_proj_ssm", "w_out", "final_gain"]


def kernel(**inputs):
    import concourse.bacc as bacc
    from concourse.bass_utils import run_bass_kernel_spmd

    nc = bacc.Bacc("TRN2", target_bir_lowering=False, num_devices=1)
    arrays, args = {}, {}
    for name, a in list(((n, inputs[n]) for n in _INS)) + list(shape_tables().items()):
        a = np.ascontiguousarray(a)
        arrays[f"in_{name}"] = a
        args[name] = nc.dram_tensor(f"in_{name}", a.shape, mybir.dt.from_np(a.dtype), kind="ExternalInput").ap()
    out = nc.dram_tensor("out", (1, SEQ, D_MODEL), mybir.dt.float32, kind="ExternalOutput").ap()
    build(nc, out=out, **args)
    r = run_bass_kernel_spmd(nc, [arrays], core_ids=[0])
    return np.asarray(r.results[0]["out"])
```

```python
import math
import numpy as np
import concourse.bass as bass
from concourse import mybir

P = 128
SEQ = 1024
D_MODEL = 1024
KT = D_MODEL // P
ST = SEQ // P
HALF = 512
NC_HALF = SEQ // HALF
HEADS, GROUPS, HD = 8, 2, 64
HPG = HEADS // GROUPS
CMP_BLOCK, CMP_STRIDE = 32, 16
NCMP = (SEQ - CMP_BLOCK) // CMP_STRIDE + 1
PAIRS = CMP_BLOCK // 2
CMP_HIDDEN = 2 * HD
WIN_TILES = 512 // P
EPS = 1e-6
MASK = -1.0e30
MAX_FLOOR = -1.0e29
TINY = 1.0e-30
SG, SC, SS = 16, 16, 64
SW = SG * SC
SSM_T = SG // 2
CH = 8
NCH = SEQ // CH
IN_W = 4376
COL_Q, COL_KV, COL_GATE, COL_U, COL_ZS, COL_MA, COL_MS = 0, 512, 1280, 1816, 2072, 2328, 3352
NGATE = 3 * HEADS
ROUND = 1.5 * 2.0 ** 23
TWO_PI_1, TWO_PI_2, TWO_PI_3 = 6.28125, 0.0019350051879882812, 3.019915981956753e-07
SIN_2PI = 6.2831845
VW = HD + 2

CHUNKS = [(COL_U, 256), (COL_ZS, 256), (COL_Q, 256), (COL_Q + 256, 256), (COL_KV, 256),
          (COL_GATE, 280), (COL_GATE + 280, 256), (COL_KV + 256, 256), (COL_KV + 512, 256)]
U_, ZS_, Q0_, Q1_, KC_, Z0_, Z1_, KS_, KW_ = range(9)
CW = 280

R_H = 16544
R_K = R_H + 65536
R_V = R_K + 32768
R_Q = R_V + 8448
R_Z = R_Q + 16384
R_O = R_Z + 16384
R_W = R_O + 8192
R_C = R_W + 5 * CW * 4 * KT


def shape_tables():
    f32 = np.float32
    half = HD // 2
    inv = (f32(10000.0) ** (-np.arange(half, dtype=f32) / f32(half))).astype(f32)
    ang = (np.arange(SEQ, dtype=f32)[:, None] * inv[None, :]).astype(f32)
    cos, sin = np.cos(ang).astype(f32), np.sin(ang).astype(f32)
    rope = np.concatenate([cos, cos, -sin, sin], axis=1)
    ident = np.eye(P, dtype=f32)
    p, f = np.arange(P)[:, None], np.arange(P)[None, :]
    causal = np.where(f <= p, 0.0, MASK).astype(f32)
    band = np.where(f > p, 0.0, MASK).astype(f32)
    q, n = np.arange(SEQ)[:, None], np.arange(64)[None, :]
    cmp_q = np.where((CMP_STRIDE * n + CMP_BLOCK - 1 <= q) & (n < NCMP), 0.0, MASK).astype(f32)
    ramp = np.zeros((1, 160), f32)
    ramp[0, 0:NCH] = np.arange(NCH) - 1
    ramp[0, NCH:NCH + 16] = np.arange(16)
    aug = np.zeros((P, 4), f32)
    for b in range(3):
        aug[HD + 2 * b:HD + 2 * b + 2, b] = 1.0
    return {"t_rope": rope, "t_ident": ident, "t_masks": np.concatenate([causal, band], 1),
            "t_cmpq": cmp_q, "t_cmpt": np.concatenate([cmp_q.T, cmp_q.T], 0), "t_ramp": ramp, "t_aug": aug}


class Chain:

    def __init__(self, eng, sem):
        self.eng, self.sem, self.n = eng, sem, 0

    def mark(self, ins):
        self.n += 1
        ins.then_inc(self.sem, 1)

    def wait(self):
        self.eng.wait_ge(self.sem, self.n)

    def link(self, ins):
        self.mark(ins)
        self.wait()


def head_units():
    units = []
    for c in range(NC_HALF):
        units.append((0, c, 0, c * HALF, (c + 1) * HALF, False, False))
    for c in range(NC_HALF):
        for j in range(4 * c + 4):
            q0 = max(P * j, HALF * c)
            units.append((1, c, j, q0, HALF * (c + 1), P * j >= HALF * c, False))
    for c in range(NC_HALF):
        order = range(4) if c == 0 else (3, 0, 1, 2, 4, 5, 6, 7)
        for j in order:
            q0, q1 = max(P * j, HALF * c), min(P * (j + WIN_TILES + 1), HALF * (c + 1))
            last = j + WIN_TILES
            units.append((2, c, j, q0, q1, P * j >= HALF * c, HALF * c <= P * last < HALF * (c + 1)))
    return units


LAG = 3


def attention_plan():
    units = head_units()
    nu = len(units)
    plan = [("MW", 0, i) for i in range(1, ST)]
    plan += [("MC", 0, p) for p in range(4)] + [("MM", 0, 0), ("MM", 0, 1), ("PQ", 1)]
    last_of = {}
    for u, t in enumerate(units):
        last_of[(t[0], t[1])] = u
    closes = {u: k for k, u in enumerate(sorted(last_of.values()))}
    pending = []
    total = HEADS * nu
    for e in range(total + LAG + 4):
        h, u = divmod(e, nu)
        more = h + 1 < HEADS and e < total
        if e < total:
            plan.append(("S", e))
        if more and 3 <= u < 3 + 2 * ST and u % 2 == 1:
            i = (u - 3) // 2
            plan += [("MX", h + 1, i), ("MW", h + 1, i)]
        v = e - LAG
        if 0 <= v < total:
            plan.append(("V", v))
            if v % nu in closes:
                k = closes[v % nu]
                pending.append((e + {0: 3, 1: 4}.get(k, 2), 6 * (v // nu) + k))
        if more and u in (0, 1):
            plan.append(("MQ", h + 1, u))
        if more and u in (20, 21):
            plan.append(("MM", h + 1, u - 20))
        norm = [n for t, n in pending if t == e]
        plan += [("N", n) for n in norm]
        parts = [[("ND", n, 0), ("ND", n, 1)] for n in norm]
        parts += [[("ND", n, 2), ("ND", n, 3)] for t, n in pending if t == e - 1]
        if more and u in (18, 19):
            parts += [[("MC", h + 1, 2 * (u - 18)), ("MC", h + 1, 2 * (u - 18) + 1)]]
        for group in zip(*parts):
            plan += group
        if more and u == 21 and h + 2 < HEADS:
            plan.append(("PQ", h + 2))
    assert pending[-1][0] + 1 < total + LAG + 4 and len(pending) == 6 * HEADS
    b7_after, n = {}, 0
    for step in plan:
        n += step[0] in ("MQ", "MM") or (step[0] == "ND" and step[2] == 3)
        b7_after[step] = n
    return units, plan, b7_after


def build(nc, x, c, w_ada, b_ada, norm_gain, w_in, pe_cmp_k, w_cmp_k1, b_cmp_k1, w_cmp_k2,
          pe_cmp_v, w_cmp_v1, b_cmp_v1, w_cmp_v2, lam_re, lam_im, log_dt, b_re, b_im,
          c_re, c_im, d_skip, w_glu, w_proj_attn, w_proj_ssm, w_out, final_gain,
          t_rope, t_ident, t_masks, t_cmpq, t_cmpt, t_ramp, t_aug, out, stop_after=None):
    F, R, B = mybir.dt.float32, mybir.dt.float32r, mybir.dt.bfloat16
    ALU, ACT, AX = mybir.AluOpType, mybir.ActivationFunctionType, mybir.AxisListType

    def at(name, shape, dt, offset):
        return nc.alloc_sbuf_tensor_at(name, shape, dt, offset=offset)

    def f(ap):
        return ap.bitcast(F)

    ada = at("ada", [P, KT, 2048], F, R_H)
    ht_hi = at("ht_hi", [P, KT, SEQ], R, R_H)
    ht_lo = at("ht_lo", [P, KT, SEQ], R, R_H + 32768)
    xs = at("xs", [P, ST, D_MODEL], F, R_K)
    xt = at("xt", [P, KT, SEQ], F, R_Q)
    k1 = [at(f"k1_{b}", [P, GROUPS, SEQ], R, R_K + 16384 * (b - 1)) for b in (1, 2)]
    k2 = [at(f"k2_{b}", [P, GROUPS, SEQ], R, R_K + 16384 * (b - 1) + 8192) for b in (1, 2)]
    vhi = [at(f"vhi_{b}", [P, ST, GROUPS, VW], R, R_V + 4224 * (b - 1)) for b in (1, 2)]
    vlo = [at(f"vlo_{b}", [P, ST, GROUPS, HD], R, R_W + 4096 * (b - 1)) for b in (1, 2)]
    qa = at("qa", [P, 4, ST, P], F, R_Q)
    zs = at("zs", [P, ST, 512], F, R_Z)
    so = at("so", [P, 2, SEQ], F, R_O)
    wraw = at("wraw", [P, KT, CW], F, R_W)
    whi = [at(f"whi{s}", [P, KT, CW], R, R_W + KT * CW * 4 * (1 + s)) for s in range(2)]
    wlo = [at(f"wlo{s}", [P, KT, CW], R, R_W + KT * CW * 4 * (3 + s)) for s in range(2)]
    mrow = at("mrow", [P, HALF], F, R_W + KT * CW * 4 * 2)
    junk = at("junk", [P, D_MODEL], F, R_W + KT * CW * 4 * 4)

    top = [R_C]

    def const(name, shape, dt, size=4):
        n = size * int(np.prod(shape[1:]))
        t = at(name, shape, dt, top[0])
        top[0] += (n + 31) // 32 * 32
        return t

    rope = const("rope", [P, ST, 2, HD], F)
    rt1 = const("rt1", [P, 256], F)
    rt2 = const("rt2", [P, 256], F)
    kcat = [const(f"kcat{s}", [P, GROUPS, 2, HD], R) for s in range(2)]
    r_used = top[0]
    ident = const("ident", [P, P], F)
    identb = const("identb", [P, P], B, 2)
    maskb = const("maskb", [P, 2, P], B, 2)
    cmpq = const("cmpq", [P, ST, 64], B, 2)
    cmpt = const("cmpt", [P, SEQ], B, 2)
    gates = const("gates", [P, ST, NGATE], F)
    aug = const("aug", [P, 4], F)
    k1c = const("k1c", [P, GROUPS, 2, 64], R)
    k2c = const("k2c", [P, GROUPS, 2, 64], R)
    vchi = const("vchi", [P, GROUPS, VW], R)
    vclo = const("vclo", [P, GROUPS, VW], R)
    ccol = const("ccol", [P, KT], F)
    scol = const("scol", [P, KT], F)
    bcol = const("bcol", [P, 2 * KT], F)
    modc = const("modc", [P, 2 * KT], F)
    gcol = const("gcol", [P, KT], F)
    g1 = const("g1", [P, KT], F)
    ss = const("ss", [P, ST], F)
    rs = const("rs", [P, ST], F)
    mx = [const(f"mx{s}", [P, ST, 3], F) for s in range(2)]
    mneg = const("mneg", [P, ST, 3], F)
    mneg_hi = const("mneg_hi", [P, ST, 3], R)
    onesq = const("onesq", [P, P], F)
    lsum = const("lsum", [P, 4], F)
    wrow = const("wrow", [P, 4], F)
    lr = const("lr", [P, SSM_T], F)
    li = const("li", [P, SSM_T], F)
    dt_ = const("dt_", [P, SSM_T], F)
    sm = const("sm", [P, 12, SSM_T], F)
    ramp = const("ramp", [P, 160], F)
    dcol = const("dcol", [SC, SG], F)
    assert top[0] <= nc.sbuf_usable_end, top[0]
    mload = at("mload", [P, 2, P], F, R_O)
    cqload = at("cqload", [P, ST, 64], F, R_O + 1024)
    ctload = at("ctload", [P, SEQ], F, R_O + 3072)

    cld = [at(f"cld{r}", [P, P], F, R_V + 512 * r) for r in range(2)]
    ct = [at(f"ct{r}", [P, SSM_T, SC], F, R_V + 1024 + 512 * r) for r in range(2)]
    bb = [at(f"bb{r}", [P, SSM_T, SC], F, R_V + 2048 + 512 * r) for r in range(2)]
    bbar = [at(f"bbar{r}", [P, SSM_T, SC], F, R_V + 3072 + 512 * r) for r in range(2)]
    pw = at("pw", [P, 6, SSM_T, 9], F, R_V + 4096)
    cp = [at(f"cp{r}", [P, SSM_T, 9, SC], F, R_K + 4608 * r) for r in range(2)]
    gt = [at(f"gt{r}", [P, SSM_T, P], F, R_K + 9216 + 4096 * r) for r in range(2)]
    toep = at("toep", [P, SG, P], F, R_K + 17408)
    b_r = at("b_r", [P, SSM_T, NCH], F, R_K + 25600)
    gs = [at(f"gs{r}", [P, SSM_T, CH, SC], F, R_K + 17408 + 4096 * r) for r in range(2)]
    klag = at("klag", [SC, SG, CH * SC], F, R_Z)
    b_i = at("b_i", [P, SSM_T, NCH], F, R_Z)
    zi = at("zi", [P, SSM_T, NCH], F, R_Z + 4096)
    zr = at("zr", [P, SSM_T, NCH], F, R_K + 9216)
    utok = at("utok", [P, SG, CH, SC], F, R_Q)
    ut = at("ut", [P, SG, NCH], F, R_Z + 8192)
    ecos = at("ecos", [P, SSM_T, NCH], F, R_V)
    esin = at("esin", [P, SSM_T, NCH], F, R_V + 4096)
    etmp = at("etmp", [P, SSM_T, NCH], F, R_Q + 8192)
    etmp2 = at("etmp2", [P, SSM_T, NCH], F, R_Q + 12288)
    ytok = at("ytok", [P, CH, SW], F, R_V)
    yt = at("yt", [P, 2, SEQ], F, R_Z)
    wglu = at("wglu", [P, 2, 512], F, R_K + 13312)
    sg = at("sg", [P, HALF], F, R_K + 29696)
    catc = [at(f"catc{s}", [P, 2, GROUPS, 2, HD], F, R_V + 2048 * s) for s in range(4)]
    t2 = at("t2", [P, 2, GROUPS, SEQ], F, R_K)
    w1 = [at(f"w1_{r}", [P, PAIRS, CMP_HIDDEN], F, R_K + 16384 + 8192 * r) for r in range(2)]
    hid = [at(f"hid{r}", [P, GROUPS * NCMP], F, R_V + 512 * r) for r in range(2)]
    w2 = [at(f"w2_{r}", [P, HD], F, R_V + 1024 + 256 * r) for r in range(2)]
    w2d = at("w2d", [P, 2, HD], F, R_V + 1536)
    pec = [at(f"pec{r}", [P, PAIRS], F, R_V + 2048 + 64 * r) for r in range(2)]
    b1c = [at(f"b1c{r}", [P, 1], F, R_V + 2176 + 32 * r) for r in range(2)]
    hb = at("hb", [P, 2], F, R_V + 2240)
    kch = at("kch", [P, GROUPS * NCMP], R, R_V + 2304)

    q1 = [at(f"q1_{s}", [P, SEQ], R, R_W + (17920, 26112)[s]) for s in range(2)]
    q2 = [at(f"q2_{s}", [P, SEQ], R, R_W + 30208 + 4096 * s) for s in range(2)]
    qc1 = at("qc1", [P, ST, 2, HD], R, R_W + 22016)
    NQ2 = HD + 6
    qc2 = at("qc2", [P, ST, NQ2], F, R_W + 38400)
    NPT = 4
    pt = [at(f"pt{s}", [P, HALF], F, R_W + 40640 + 2048 * s) for s in range(NPT)]
    plo = [at(f"plo{s}", [P, HALF], R, R_W + 40640 + 2048 * s) for s in range(NPT)]
    phi = [at(f"phi{s}", [P, HALF], R, R_W + 8192 + 2048 * s) for s in range(NPT)]
    osb = [at(f"osb{s}", [HD + 1, HALF], F, R_W + 48832 + 2048 * s) for s in range(2)]
    otmp = at("otmp", [P, 4, HD], F, R_W + 16384)
    assert R_W + 52928 <= r_used

    NW = 12
    mt = at("mt", [P, KT, SEQ], F, R_K)
    at_hi = at("at_hi", [P, 4, SEQ], R, R_Z)
    at_lo = at("at_lo", [P, 4, SEQ], R, R_Q)
    so_hi = at("so_hi", [P, 2, SEQ], R, R_V)
    so_lo = at("so_lo", [P, 2, SEQ], R, R_O)
    draw = [at(f"draw{s}", [P, NW, P], F, R_W + (17920, 36352)[s]) for s in range(2)]
    dhi = [at(f"dhi{s}", [P, NW, P], R, R_W + 6144 * s) for s in range(2)]
    dlo = [at(f"dlo{s}", [P, NW, P], R, R_W + 24064 + 6144 * s) for s in range(2)]
    dsig = at("dsig", [P, HALF], F, R_W + 42496)
    dtm = at("dtm", [P, HALF], F, R_W + 14336)
    gstage = at("gstage", [P, HALF], F, R_W + 12288)
    gacc = at("gacc", [P, D_MODEL], F, R_C)

    ohi = at("ohi", [P, KT, D_MODEL], R, R_H)
    olo = at("olo", [P, KT, D_MODEL], R, R_H + 32768)
    oraw = at("oraw", [P, KT, D_MODEL], F, R_Q)
    mhi = [at(f"mhi{s}", [P, KT, P], R, R_W + 4096 * s) for s in range(2)]
    mlo = [at(f"mlo{s}", [P, KT, P], R, R_W + 8192 + 4096 * s) for s in range(2)]
    xr = [at(f"xr{s}", [P, D_MODEL], F, R_W + 16384 + 4096 * s) for s in range(2)]
    yr = [at(f"yr{s}", [P, D_MODEL], F, R_W + 24576 + 4096 * s) for s in range(2)]
    gateb = at("gateb", [P, D_MODEL], F, R_W + 32768)
    fgb = at("fgb", [P, D_MODEL], F, R_W + 36864)
    gbias = at("gbias", [P, D_MODEL], F, R_V)
    oss = at("oss", [P, 3, ST], F, R_W + 40960)
    ojunk = at("ojunk", [P, D_MODEL], F, R_O)

    bank = [nc.alloc_psum_tensor(f"bank{i}", [P, HALF], F) for i in range(2)]
    slc_max = nc.alloc_psum_tensor("slc_max", [P, SEQ], F)
    win_max = nc.alloc_psum_tensor("win_max", [P, SEQ], F)
    bank += [slc_max[:, 0:HALF], slc_max[:, HALF:SEQ], win_max[:, 0:HALF], win_max[:, HALF:SEQ]]
    bank += [nc.alloc_psum_tensor(f"bank{i}", [P, HALF], F) for i in (6, 7)]
    bank = [b[:, :] for b in bank]

    def max_no(h, i):
        return ST * h + i

    def other_max(h, i):
        return slc_max if h == 0 and i % 2 else win_max

    names = {}

    def sem(name):
        names[name] = nc.alloc_semaphore(name)
        return names[name]

    units, plan, b7_after = attention_plan()
    NU = len(units)

    s_small, s_c, s_id, s_mod_in = sem("s_small"), sem("s_c"), sem("s_id"), sem("s_mod_in")
    s_ssmp = sem("s_ssmp")
    s_x = [sem(f"s_x{i}") for i in range(ST)]
    s_ada = [sem(f"s_ada{k}") for k in range(KT)]
    s_raw = sem("s_raw")
    s_silu, s_sq, s_var, s_sd, s_rs, s_xn = (sem(n) for n in
        ("s_silu", "s_sq", "s_var", "s_sd", "s_rs", "s_xn"))
    s_xtr, s_mod = sem("s_xtr"), sem("s_mod")
    s_h32, s_hhi, s_hlo = sem("s_h32"), sem("s_hhi"), sem("s_hlo")
    s_whi, s_wlo = sem("s_whi"), sem("s_wlo")
    s_unit = sem("s_unit")
    s_evd, s_eva = sem("s_evd"), sem("s_eva")
    s_tr, s_trf = sem("s_tr"), sem("s_trf")
    s_ch_d, s_ch_a, s_ch_p = sem("s_ch_d"), sem("s_ch_a"), sem("s_ch_p")
    s_masks = sem("s_masks")
    s_one = {}

    def once(name):
        if name not in s_one:
            s_one[name] = sem("s_" + name)
        return s_one[name]

    unit_list = [(w, i) for w in range(9) for i in range(4 if w == ZS_ else ST)]
    unit_no = {u: n for n, u in enumerate(unit_list)}
    reads_d = {U_: False, ZS_: False, Q0_: True, Q1_: True, KC_: True, Z0_: True, Z1_: False,
               KS_: True, KW_: True}
    reads_a = {U_: True, ZS_: True, Q0_: False, Q1_: False, KC_: True, Z0_: True, Z1_: True,
               KS_: False, KW_: False}

    def read_count(table, n):
        return sum(1 for w, _ in unit_list[:n] if table[w])

    def unit_bank(n):
        w, i = unit_list[n]
        if w == U_:
            return bank[i // 2][:, (i % 2) * 256:(i % 2) * 256 + 256]
        return bank[4 + (n - ST) % 4]

    FILLS = (["gt"] * 4 + ["klag"] * 4 + ["ut"] * 4 + ["bu"] * 4 + ["y"] * 4 + ["yt"] * 4
             + ["kc"] * 8 + ["ks"] * 8 + ["q"] * 2 + ["kw"] * 8)
    EARLY = ST + 2
    first = {}
    for n, name in enumerate(FILLS):
        first.setdefault(name, n)

    def key_fill(m):
        return first["ks"] + m if m < ST else first["kw"] + m - ST

    C_RE, C_IM = c_re[0], c_im[0]

    with nc.Block() as block:

        @block.sync
        def _(sp):
            def load_ada(k):
                sp.dma_start(ada[:, k, :], w_ada[0, P * k:P * k + P, 0:2048]).then_inc(s_ada[k], 16)
            def load_x(i):
                sp.dma_start(xs[:, i, :], x[0, P * i:P * i + P, :]).then_inc(s_x[i], 16)
            for i in range(4):
                load_x(i)
            load_ada(0)
            load_ada(1)
            for i in range(4, ST):
                load_x(i)
            for k in range(2, KT):
                load_ada(k)
            w_view = w_in[0].rearrange("(k p) n -> p k n", p=P)
            for w, (c0, n) in enumerate(CHUNKS):
                if w >= 1:
                    sp.wait_ge(s_whi, w)
                    sp.wait_ge(s_wlo, w)
                sp.dma_start(wraw[:, :, 0:n], w_view[:, :, c0:c0 + n]).then_inc(s_raw, 16)
                if w == Q1_:
                    sp.wait_ge(once("lags"), 1)
                    for i in range(CH):
                        sp.dma_start(toep[SC * i:SC * i + SC, :, SC * i:CH * SC], klag[:, :, 0:(CH - i) * SC])\
                          .then_inc(once("toep"), 16)
                    sp.wait_ge(s_tr, first["bu"] + 4)
                    sp.dma_start(wglu[:, :, :], w_glu[0].rearrange("(k p) n -> p k n", p=P))\
                      .then_inc(once("wglu"), 16)
                if w == Z1_:
                    sp.wait_ge(once("gluo"), 4)
                    for r, (a, b, pe) in enumerate(((w_cmp_k1, w_cmp_k2, pe_cmp_k),
                                                    (w_cmp_v1, w_cmp_v2, pe_cmp_v))):
                        sp.dma_start(w1[r][:, :, :], a[0].rearrange("(m p) n -> p m n", p=P))\
                          .then_inc(once("cmpw"), 16)
                    sp.wait_ge(s_tr, first["kc"] + 8)
                    for r, (b, pe, b1) in enumerate(((w_cmp_k2, pe_cmp_k, b_cmp_k1),
                                                     (w_cmp_v2, pe_cmp_v, b_cmp_v1))):
                        sp.dma_start(w2[r][:, :], b[0]).then_inc(once("cmpw"), 16)
                        sp.dma_start(pec[r][:, :], pe[0].rearrange("(m l) d -> (l d) m", l=2),
                                     allow_slow_non_contiguous=True).then_inc(once("cmpw"), 16)
                        sp.dma_start(b1c[r][:, :], b1[0].rearrange("(p a) -> p a", a=1),
                                     allow_slow_non_contiguous=True).then_inc(once("cmpw"), 16)

            def slot_parts(n):
                nb, kind = divmod(n, 2)
                gate = COL_MA if kind == 0 else COL_MS
                proj = w_proj_attn if kind == 0 else w_proj_ssm
                kp = 4 if kind == 0 else 2
                return nb, gate, proj, kp
            for n in range(2 * KT):
                nb, gate, proj, kp = slot_parts(n)
                if n == 0:
                    sp.wait_ge(once("score"), (HEADS - 1) * NU)
                    sp.wait_ge(once("qt"), 2 * HEADS - 2)
                    sp.wait_ge(once("qlo"), HEADS)
                elif n == 1:
                    sp.wait_ge(once("norm"), 4 * HEADS)
                else:
                    sp.wait_ge(once("dhi"), n - 1)
                    sp.wait_ge(once("dlo"), n - 1)
                sp.dma_start(draw[n % 2][:, 0:KT, :], w_view[:, :, gate + P * nb:gate + P * nb + P])\
                  .then_inc(once(f"draw{n % 2}"), 16)
                sp.dma_start(draw[n % 2][:, KT:KT + kp, :],
                             proj[0].rearrange("(k p) n -> p k n", p=P)[:, :, P * nb:P * nb + P])\
                  .then_inc(once(f"draw{n % 2}"), 16)
            sp.wait_ge(once("dproj"), 4 * (KT - 1) + 2)
            for k in range(KT):
                sp.dma_start(oraw[:, k, :], w_out[0, P * k:P * k + P, :]).then_inc(once(f"oraw{k}"), 16)
            sp.wait_ge(once("merged"), 2 * KT)
            sp.wait_ge(once("dgate"), 4 * KT)
            sp.dma_start(gbias[:, :], b_ada[0:1, 2048:3072].to_broadcast([P, D_MODEL])).then_inc(once("gbias"), 16)
            sp.dma_start(fgb[:, :], final_gain.rearrange("(a n) -> a n", a=1).to_broadcast([P, D_MODEL]))\
              .then_inc(once("fgb"), 16)
            for i in range(ST):
                if i >= 2:
                    sp.wait_ge(once("res"), i - 1)
                sp.dma_start(xr[i % 2][:, :], x[0, P * i:P * i + P, :]).then_inc(once(f"xr{i % 2}"), 16)
                if i >= 1:
                    sp.wait_ge(once("y"), i)
                    sp.dma_start(out[0, P * (i - 1):P * i, :], yr[(i - 1) % 2][:, :])\
                      .then_inc(once(f"out{(i - 1) % 2}"), 16)
            sp.wait_ge(once("y"), ST)
            sp.dma_start(out[0, P * (ST - 1):P * ST, :], yr[(ST - 1) % 2][:, :]).then_inc(once("out1"), 16)
            sp.wait_ge(once("out0"), 16 * (ST // 2))
            sp.wait_ge(once("out1"), 16 * (ST // 2))

        @block.gpsimd
        def _(pool):
            ch = Chain(pool, s_ch_p)

            def tt(o, a, b, op):
                return nc.gpsimd.tensor_tensor(o, a, b, op)

            nc.gpsimd.memset(onesq[:, :], 1.0).then_inc(once("vc0"), 1)
            nc.gpsimd.memset(f(vchi[:, :, :]), 0.0).then_inc(once("vc0"), 1)
            nc.gpsimd.memset(f(vclo[:, :, :]), 0.0).then_inc(once("vc0"), 1)
            z_re, ph, fr, ta, tb, nr, cr, ci, den, tc = (sm[:, i, :] for i in range(10))
            pool.wait_ge(s_ssmp, 16 * 12)
            pool.wait_ge(once("dt"), 1)
            ch.link(tt(z_re, lr[:, :], dt_[:, :], ALU.mult))
            ch.link(tt(ph, li[:, :], dt_[:, :], ALU.mult))
            ch.link(nc.gpsimd.tensor_scalar(ta, ph, 1.0 / (2 * math.pi), ROUND, ALU.mult, ALU.add))
            ch.link(nc.gpsimd.tensor_scalar(ta, ta, -ROUND, None, ALU.add))
            for part in (TWO_PI_1, TWO_PI_2, TWO_PI_3):
                ch.link(nc.gpsimd.tensor_scalar(tb, ta, part, None, ALU.mult))
                ch.link(tt(ph, ph, tb, ALU.subtract))
            ch.link(nc.gpsimd.tensor_scalar(fr, ph, 1.0 / (2 * math.pi), None, ALU.mult))
            J = [P, SSM_T, 9]
            turns, mag, cs, sn, pr, pi = (pw[:, i, :, :] for i in range(6))
            jr = ramp[:, NCH:NCH + 9].unsqueeze(1).to_broadcast(J)
            ch.link(tt(turns, fr.unsqueeze(2).to_broadcast(J), jr, ALU.mult))
            ch.link(nc.gpsimd.tensor_scalar(cs, turns, ROUND, -ROUND, ALU.add, ALU.add))
            ch.link(tt(turns, turns, cs, ALU.subtract))
            tt(mag, z_re.unsqueeze(2).to_broadcast(J), jr, ALU.mult).then_inc(once("pw_arg"), 1)
            pool.wait_ge(once("pw_fn"), 3)
            ch.link(tt(cs, cs, cs, ALU.mult))
            ch.link(nc.gpsimd.tensor_scalar(cs, cs, -2.0, 1.0, ALU.mult, ALU.add))
            ch.link(tt(pr, mag, cs, ALU.mult))
            ch.link(tt(pi, mag, sn, ALU.mult))
            ar, ai = pw[:, 4, :, 1], pw[:, 5, :, 1]
            ch.link(nc.gpsimd.tensor_scalar(nr, ar, -1.0, None, ALU.add))
            ch.link(tt(den, lr[:, :], lr[:, :], ALU.mult))
            ch.link(tt(ta, li[:, :], li[:, :], ALU.mult))
            ch.link(tt(den, den, ta, ALU.add))
            ch.link(tt(cr, nr, lr[:, :], ALU.mult))
            ch.link(tt(ta, ai, li[:, :], ALU.mult))
            ch.link(tt(cr, cr, ta, ALU.add))
            ch.link(tt(ci, ai, lr[:, :], ALU.mult))
            ch.link(tt(ta, nr, li[:, :], ALU.mult))
            tt(ci, ci, ta, ALU.subtract).then_inc(once("den"), 1)
            pool.wait_ge(once("rden"), 1)
            ch.link(tt(cr, cr, tc, ALU.mult))
            ch.link(tt(ci, ci, tc, ALU.mult))
            S3 = [P, SSM_T, SC]
            crb, cib = cr.unsqueeze(2).to_broadcast(S3), ci.unsqueeze(2).to_broadcast(S3)
            tmp3 = at("tmp3", S3, F, R_V + 5824)[:, :, :]
            for r, (a, b, op) in enumerate(((0, 1, ALU.subtract), (1, 0, ALU.add))):
                ch.link(tt(bbar[r][:, :, :], crb, bb[a][:, :, :], ALU.mult))
                ch.link(tt(tmp3, cib, bb[b][:, :, :], ALU.mult))
                ch.link(tt(bbar[r][:, :, :], bbar[r][:, :, :], tmp3, op))
            G4 = [P, SSM_T, CH, SC]

            def pw_rev(q):
                return pw[:, q, :, 7::-1].unsqueeze(3).to_broadcast(G4)

            def bb4(q):
                return bbar[q][:, :, :].unsqueeze(2).to_broadcast(G4)
            pool.wait_ge(s_xtr, 16)
            gtmp = b_r[:, :, :].rearrange("p t (j c) -> p t j c", c=SC)
            for r, (a, b, op) in enumerate(((0, 1, ALU.subtract), (1, 0, ALU.add))):
                ch.link(tt(gs[r][:, :, :, :], pw_rev(4), bb4(a), ALU.mult))
                ch.link(tt(gtmp, pw_rev(5), bb4(b), ALU.mult))
                tt(gs[r][:, :, :, :], gs[r][:, :, :, :], gtmp, op).then_inc(once("gs"), 1)
                pool.wait_ge(once("gs"), r + 1)
            pool.wait_ge(once("ctev"), 2)
            C4 = [P, SSM_T, 9, SC]
            ctmp = at("ctmp", [P, SSM_T, 9, SC], F, R_K + 25600)

            def pw9(q):
                return pw[:, q, :, :].unsqueeze(3).to_broadcast(C4)

            def ct4(q):
                return ct[q][:, :, :].unsqueeze(2).to_broadcast(C4)
            ch.link(tt(cp[0][:, :, :, :], pw9(4), ct4(0), ALU.mult))
            ch.link(tt(ctmp[:, :, :, :], pw9(5), ct4(1), ALU.mult))
            ch.link(tt(cp[0][:, :, :, :], cp[0][:, :, :, :], ctmp[:, :, :, :], ALU.subtract))
            ch.link(tt(cp[1][:, :, :, :], pw9(5), ct4(0), ALU.mult))
            ch.link(tt(ctmp[:, :, :, :], pw9(4), ct4(1), ALU.mult))
            ch.link(tt(cp[1][:, :, :, :], cp[1][:, :, :, :], ctmp[:, :, :, :], ALU.add))
            nc.gpsimd.tensor_scalar(cp[1][:, :, :, :], cp[1][:, :, :, :], -1.0, None, ALU.mult)\
                .then_inc(once("cp"), 1)
            pool.wait_ge(s_tr, first["gt"] + 4)
            ch.link(nc.gpsimd.memset(toep[:, :, :], 0.0))
            ch.link(nc.gpsimd.tensor_copy(tb, pw[:, 1, :, 8]))
            ch.link(nc.gpsimd.tensor_copy(ta, pw[:, 0, :, 8]))
            E3 = [P, SSM_T, NCH]
            pool.wait_ge(s_hlo, KT)
            ch.link(tt(etmp[:, :, :], ta.unsqueeze(2).to_broadcast(E3),
                       ramp[:, 0:NCH].unsqueeze(1).to_broadcast(E3), ALU.mult))
            ch.link(nc.gpsimd.tensor_scalar(etmp2[:, :, :], etmp[:, :, :], ROUND, -ROUND, ALU.add, ALU.add))
            tt(etmp[:, :, :], etmp[:, :, :], etmp2[:, :, :], ALU.subtract).then_inc(once("eang"), 1)
            pool.wait_ge(once("eang"), 1)
            pool.wait_ge(s_trf, first["klag"] + 4)
            dtmp = at("dtmp", [SC, SG, SC], F, R_K + 30208)
            ch.link(tt(dtmp[:, :, :], ident[0:SC, 0:SC].unsqueeze(1).to_broadcast([SC, SG, SC]),
                       dcol[:, :].unsqueeze(2).to_broadcast([SC, SG, SC]), ALU.mult))
            tt(klag[:, :, 0:SC], klag[:, :, 0:SC], dtmp[:, :, :], ALU.add).then_inc(once("lags"), 1)
            pool.wait_ge(once("lags"), 1)
            pool.wait_ge(once("efn"), 2)
            ch.link(tt(ecos[:, :, :], ecos[:, :, :], ecos[:, :, :], ALU.mult))
            nc.gpsimd.tensor_scalar(ecos[:, :, :], ecos[:, :, :], -2.0, 1.0, ALU.mult, ALU.add)\
                .then_inc(once("ecos"), 1)
            def split_w(w):
                n = CHUNKS[w][1]
                pool.wait_ge(s_whi, w + 1)
                tt(wlo[w % 2][:, :, 0:n], wraw[:, :, 0:n], f(whi[w % 2][:, :, 0:n]), ALU.subtract).then_inc(s_wlo, 1)
            split_w(4)
            split_w(5)
            for n in range(4):
                nb, cc = divmod(n, 2)
                pool.wait_ge(once("glusig"), n + 1)
                v = so[:, nb, cc * HALF:(cc + 1) * HALF]
                tt(v, v, sg[:, :], ALU.mult).then_inc(once("glugate"), 1)
            split_w(6)
            split_w(7)
            pool.wait_ge(once("cmpdone"), GROUPS)
            for b in range(2):
                ch.link(nc.gpsimd.memset(f(vhi[b][:, :, :, HD:VW]), 1.0))
                nc.gpsimd.tensor_copy(k2[b][HD:P, :, :],
                                      aug[HD:P, b + 1:b + 2].unsqueeze(1).to_broadcast([HD, GROUPS, SEQ]))\
                    .then_inc(once("k2aug"), 1)
                pool.wait_ge(once("k2aug"), b + 1)
            n_dup = n_low = n_sum = 0
            for step in [("PQ", 0)] + plan:
                if step[0] == "PQ":
                    if n_low:
                        pool.wait_ge(once("plo_cmp"), n_low)
                    if n_sum:
                        pool.wait_ge(once("norm"), n_sum)
                    n_dup += 1
                    pool.wait_ge(once("qhi"), step[1] + 1)
                    nc.gpsimd.tensor_copy(qc1[:, :, 1, :], f(qc1[:, :, 0, :])).then_inc(once("qdup"), 1)
                elif step[0] == "S" and units[step[1] % NU][0] == 0:
                    e = step[1]
                    pool.wait_ge(once("qdup"), n_dup)
                    if n_low:
                        pool.wait_ge(once("plo_cmp"), n_low)
                    if n_sum:
                        pool.wait_ge(once("norm"), n_sum)
                    n_low += 1
                    pool.wait_ge(once("exp"), 2 * e + 2)
                    tt(phi[e % NPT][HD:P, :], pt[e % NPT][HD:P, :], f(phi[e % NPT][HD:P, :]), ALU.subtract)\
                        .then_inc(once("plo_cmp"), 1)
                elif step[0] == "ND" and step[2] == 3 and step[1] % 6 >= 2:
                    n = step[1]
                    h, r = divmod(n, 6)
                    cc = r % 2
                    pool.wait_ge(once("b7"), b7_after[step])
                    pool.wait_ge(once("qdup"), n_dup)
                    pool.wait_ge(once("plo_cmp"), n_low)
                    if n_sum:
                        pool.wait_ge(once("norm"), n_sum)
                    n_sum += 1
                    dst = qa[:, h // 2, 4 * cc:4 * cc + 4, HD * (h % 2):HD * (h % 2) + HD]
                    tt(dst, dst, otmp[:, :, :], ALU.add).then_inc(once("norm"), 1)
                    if n_sum % 8 == 0 and n_sum < 4 * HEADS:
                        pool.wait_ge(once("norm"), n_sum)
                        b = n_sum // 8 - 1
                        tt(qa[:, b, :, :], qa[:, b, :, :], zs[:, :, P * b:P * b + P], ALU.mult).then_inc(once("az"), 1)
                        pool.wait_ge(once("az"), b + 1)
            pool.wait_ge(once("norm"), 4 * HEADS)
            for n in range(2 * KT):
                k, hf = divmod(n, 2)
                dst = gacc[:, HALF * hf:HALF * hf + HALF]
                if n > 0:
                    ch.wait()
                pool.dma_start(gstage[:, :], w_ada[0, P * k:P * k + P, 2048 + HALF * hf:2560 + HALF * hf])\
                    .then_inc(once("gst"), 16)
                pool.wait_ge(once("gst"), 16 * (n + 1))
                if k == 0:
                    ch.mark(nc.gpsimd.tensor_scalar(dst, gstage[:, :], scol[:, k:k + 1], None, ALU.mult))
                else:
                    ch.link(nc.gpsimd.tensor_scalar(gstage[:, :], gstage[:, :], scol[:, k:k + 1], None,
                                                    ALU.mult))
                    ins = tt(dst, dst, gstage[:, :], ALU.add)
                    if n < 2 * KT - 1:
                        ch.mark(ins)
            ins.then_inc(once("gacc"), 1)

        @block.scalar
        def _(act):
            ch = Chain(act, s_ch_a)

            def a(o, i, fn=ACT.Copy, **kw):
                return nc.scalar.activation(o, i, fn, **kw)

            sl = dict(allow_slow_non_contiguous=True)
            act.dma_start(ccol[:, :], c[0].rearrange("(k p) -> p k", p=P), **sl).then_inc(s_c, 16)
            act.dma_start(ident[:, :], t_ident).then_inc(s_id, 16)

            def small_loads():
                yield act.dma_start(bcol[:, :], b_ada[0, 0:2048].rearrange("(k p) -> p k", p=P), **sl)\
                    .then_inc(s_mod_in, 16)
                yield act.dma_start(gcol[:, :], norm_gain[0].rearrange("(k p) -> p k", p=P), **sl)\
                    .then_inc(s_mod_in, 16)
                for gp in range(2):
                    half = slice(SS * gp, SS * gp + SS)
                    for dst, src in ((lr, lam_re), (li, lam_im)):
                        yield act.dma_start(dst[half, :], src[0].rearrange("(t g) s -> g s t", g=2)[gp], **sl)\
                            .then_inc(s_ssmp, 16)
                    yield act.dma_start(dt_[half, :], log_dt[0].rearrange("(t g) -> g t", g=2)[gp:gp + 1, :]
                                        .to_broadcast([SS, SSM_T]), **sl).then_inc(s_ssmp, 16)
                    for dst, src in ((bb[0], b_re), (bb[1], b_im)):
                        yield act.dma_start(dst[half, :, :], src[0].rearrange("(t g) s c -> g s t c", g=2)[gp], **sl)\
                            .then_inc(s_ssmp, 16)
                yield act.dma_start(ramp[:, :], t_ramp.to_broadcast([P, 160])).then_inc(s_ssmp, 16)
                yield act.dma_start(dcol[:, :], d_skip[0].rearrange("(g c) -> c g", g=SG), **sl).then_inc(s_ssmp, 16)
                for r, src in enumerate((C_RE, C_IM)):
                    for t in range(SSM_T):
                        yield act.dma_start(cld[r][SC * t:SC * t + SC, :].rearrange("c (g s) -> c g s", g=2),
                                            src[2 * t:2 * t + 2].rearrange("g c s -> c g s")).then_inc(once("cld"), 16)
                yield act.dma_start(mload[:, :, :], t_masks.rearrange("p (a f) -> p a f", a=2)).then_inc(s_small, 16)
                yield act.dma_start(cqload[:, :, :], t_cmpq.rearrange("(i p) n -> p i n", p=P)).then_inc(s_small, 16)
                yield act.dma_start(ctload[:, :], t_cmpt).then_inc(s_small, 16)
                yield act.dma_start(rope[:, :, :, :], t_rope.rearrange("(i p) (a d) -> p i a d", p=P, a=2))\
                    .then_inc(s_small, 16)
                yield act.dma_start(aug[:, :], t_aug).then_inc(s_small, 16)

            act.wait_ge(s_c, 16)
            a(scol[:, :], ccol[:, :], ACT.Silu).then_inc(s_silu, 1)
            loads = small_loads()
            for i in range(ST):
                for _ in range(1 if i < 4 else 2):
                    next(loads, None)
                act.wait_ge(s_x[i], 16)
                if i >= 1:
                    act.wait_ge(s_sq, i)
                a(junk[:, :], xs[:, i, :], ACT.Square, accum_out=ss[:, i:i + 1]).then_inc(s_sq, 1)
                if i % 4 == 3:
                    cc = i // 4
                    act.wait_ge(s_var, cc + 1)
                    a(rs[:, i - 3:i + 1], ss[:, i - 3:i + 1], ACT.Sqrt).then_inc(s_sd, 1)
                    for k in range(0, KT, 2):
                        n = KT * cc + k
                        act.wait_ge(s_xtr, n + 1)
                        a(xt[:, k, cc * HALF:(cc + 1) * HALF], bank[4 + n % 4]).then_inc(once("xta"), 1)
            for _ in loads:
                pass
            act.wait_ge(s_ssmp, 16 * 12)
            a(dt_[:, :], dt_[:, :], ACT.Exp).then_inc(once("dt"), 1)
            act.wait_ge(once("pw_arg"), 1)
            a(pw[:, 1, :, :], pw[:, 1, :, :], ACT.Exp).then_inc(once("pw_fn"), 1)
            a(pw[:, 2, :, :], pw[:, 0, :, :], ACT.Sin, scale=SIN_2PI / 2).then_inc(once("pw_fn"), 1)
            a(pw[:, 3, :, :], pw[:, 0, :, :], ACT.Sin, scale=SIN_2PI).then_inc(once("pw_fn"), 1)

            def split_w(w):
                n = CHUNKS[w][1]
                act.wait_ge(s_raw, 16 * (w + 1))
                if w >= 2:
                    act.wait_ge(s_unit, unit_no[(w - 1, 0)])
                a(whi[w % 2][:, :, 0:n], wraw[:, :, 0:n]).then_inc(s_whi, 1)

            split_w(0)
            act.wait_ge(s_mod, 1)
            act.wait_ge(once("mrow"), 1)
            for j in range(0, 4, 2):
                a(mrow[32 * j:32 * j + 1, :], bank[j][0:1, :]).then_inc(once("mrow"), 1)

            for r in range(2):
                act.wait_ge(once("ctr"), 1)
                a(ct[r][:, :, :], bank[4][:, P * r:P * r + P].rearrange("p (t c) -> p t c", t=SSM_T))\
                    .then_inc(once("ctev"), 1)

            def fill(n):
                act.wait_ge(s_tr, n + 1)
                return bank[n % 2]

            for k in range(KT):
                act.wait_ge(s_h32, k + 1)
                a(ht_hi[:, k, :], xt[:, k, :]).then_inc(s_hhi, 1)
            split_w(1)
            for i in range(ST):
                act.wait_ge(s_unit, ST)
                if i == 0:
                    act.wait_ge(s_hlo, KT)
                a(utok[:, :, i, :], unit_bank(i).rearrange("p (g c) -> p g c", g=SG)).then_inc(s_eva, 1)
            split_w(2)
            for i in range(4):
                nb, cc = divmod(i, 2)
                n = unit_no[(ZS_, i)]
                act.wait_ge(s_unit, n + 1)
                if i == 0:
                    act.wait_ge(s_masks, 3)
                a(so[:, nb, cc * HALF:(cc + 1) * HALF], unit_bank(n), ACT.Silu).then_inc(s_eva, 1)
            for q in range(4):
                r, th = divmod(q, 2)
                bk = fill(first["gt"] + q)
                a(gt[r][:, 4 * th:4 * th + 4, :], bk.rearrange("p (t s) -> p t s", t=4)).then_inc(s_trf, 1)
            split_w(3)
            kl = klag[:, :, :].rearrange("p (t g) s -> p g t s", g=2)
            for q in range(4):
                gp, th = divmod(q, 2)
                bk = fill(first["klag"] + q)
                a(kl[:, gp, 4 * th:4 * th + 4, :], bk[0:SC, :].rearrange("p (t s) -> p t s", t=4)).then_inc(s_trf, 1)
            for q in range(4):
                bk = fill(first["ut"] + q)
                a(ut[:, 4 * q:4 * q + 4, :], bk.rearrange("p (g s) -> p g s", g=4)).then_inc(s_trf, 1)
            act.wait_ge(once("eang"), 1)
            a(ecos[:, :, :], etmp[:, :, :], ACT.Sin, scale=SIN_2PI / 2).then_inc(once("efn"), 1)
            a(esin[:, :, :], etmp[:, :, :], ACT.Sin, scale=SIN_2PI).then_inc(once("efn"), 1)
            for q in range(4):
                r, th = divmod(q, 2)
                bk = fill(first["bu"] + q)
                dst = (b_r, b_i)[r]
                if q == 2:
                    act.wait_ge(once("toep"), 16 * CH)
                a(dst[:, 4 * th:4 * th + 4, 1:NCH], bk.rearrange("p (t s) -> p t s", t=4)[:, :, 0:NCH - 1])\
                    .then_inc(s_trf, 1)
            split_w(4)
            for q in range(4):
                bk = fill(first["y"] + q)
                if q == 0:
                    act.wait_ge(once("rot"), 1)
                gp, th = divmod(q, 2)
                yv = ytok[:, :, :].rearrange("p j (t g c) -> p g t j c", g=2, c=SC)
                a(yv[:, gp, 4 * th:4 * th + 4, :, :], bk.rearrange("p (t j c) -> p t j c", t=4, c=SC)).then_inc(s_trf, 1)
            split_w(5)
            for q in range(4):
                ctile, jh = divmod(q, 2)
                bk = fill(first["yt"] + q)
                if q == 0:
                    act.wait_ge(s_trf, first["y"] + 4)
                a(yt[:, ctile, :].rearrange("p (n j) -> p j n", j=CH)[:, 4 * jh:4 * jh + 4, :],
                  bk.rearrange("p (j n) -> p j n", j=4), ACT.Gelu_apprx_tanh).then_inc(s_trf, 1)
            def kc_values(i):
                n = unit_no[(KC_, i)]
                act.wait_ge(s_evd, read_count(reads_d, n + 1))
                if i >= 4:
                    act.wait_ge(s_tr, first["kc"] + 4)
                src = unit_bank(n)[:, P:2 * P].rearrange("p (g d) -> p g d", g=GROUPS)
                a(catc[i % 4][:, 1, :, :, :], src.unsqueeze(2).to_broadcast([P, GROUPS, 2, HD])).then_inc(s_eva, 1)

            def token_rows(hf):
                for q in range(4):
                    bk = fill(first["kc"] + 4 * hf + q)
                    r, g = divmod(q, 2)
                    a(t2[0:HD, r, g, hf * HALF:(hf + 1) * HALF], bk[0:HD, :]).then_inc(once("t2a"), 1)

            for i in range(4):
                kc_values(i)
            for n in range(4):
                act.wait_ge(once("glu"), 2 * n + 1)
                if n >= 1:
                    act.wait_ge(once("glugate"), n)
                a(sg[:, :], bank[0], ACT.Sigmoid).then_inc(once("glusig"), 1)
            act.wait_ge(once("gluo"), 4)
            token_rows(0)
            for i in range(4, ST):
                kc_values(i)
            for w in (Z0_, Z1_):
                for i in range(ST):
                    if w == Z0_ and i == 3:
                        token_rows(1)
                    if w == Z0_ and i == 5:
                        split_w(6)
                    n = unit_no[(w, i)]
                    act.wait_ge(s_unit, n + 1)
                    if w == Z0_:
                        act.wait_ge(s_evd, read_count(reads_d, n + 1))
                    if w == Z0_ and i == 0:
                        act.wait_ge(once("gluo"), 4)
                    o = NGATE if w == Z0_ else 0
                    c0 = 0 if w == Z0_ else 256
                    a(zs[:, i, c0:c0 + 256], unit_bank(n)[:, o:o + 256], ACT.Silu).then_inc(s_eva, 1)
                if w == Z0_:
                    split_w(7)
                    for r in range(2):
                        act.wait_ge(once("hid"), r + 1)
                        act.wait_ge(once("hbias"), r + 1)
                        a(hid[r][:, :], bank[r][:, 0:GROUPS * NCMP], ACT.Gelu_apprx_tanh, bias=hb[:, r:r + 1])\
                            .then_inc(once("hidev"), 1)
                else:
                    split_w(8)
            act.wait_ge(s_evd, read_count(reads_d, unit_no[(Z1_, 0)]))
            a(gates[:, :, :], gates[:, :, :], ACT.Sigmoid).then_inc(once("gates"), 1)
            def attention_step(step):
                if step[0] == "PQ":
                    h = step[1]
                    if h == 0:
                        act.wait_ge(s_unit, unit_no[(KW_, 0)])
                        act.wait_ge(once("qrot"), 2 * ST)
                    if h == 1:
                        act.wait_ge(s_tr, first["q"] + 2)
                    if h >= 2:
                        act.wait_ge(once("qt"), 2 * h - 2)
                    if h >= 1:
                        act.wait_ge(once("qlo"), h)
                    v = qa[:, h // 2, :, HD * (h % 2):HD * (h % 2) + HD]
                    a(qc1[:, :, 0, :], v, scale=1.0 / math.sqrt(HD)).then_inc(once("qhi"), 1)
                elif step[0] == "MQ":
                    h, hf = step[1:]
                    act.wait_ge(once("qt"), 2 * h + hf - 1)
                    a(q1[h % 2][:, hf * HALF:(hf + 1) * HALF], bank[7]).then_inc(once("b7"), 1)
                elif step[0] == "MM":
                    h, hf = step[1:]
                    act.wait_ge(once("mt"), 2 * h + hf + 1)
                    a(q2[h % 2][0:NQ2, hf * HALF:(hf + 1) * HALF], bank[7][0:NQ2, :]).then_inc(once("b7"), 1)
                elif step[0] == "S":
                    e = step[1]
                    br, cc, j, lo, hi_, dg, bd = units[e % NU]
                    act.wait_ge(once("score"), e + 1)
                    if e >= NPT:
                        act.wait_ge(once("pv"), e - NPT + 1)
                    a(pt[e % NPT][:, 0:hi_ - lo], bank[e % 2][:, 0:hi_ - lo], ACT.Exp).then_inc(once("exp"), 1)
                    a(phi[e % NPT][:, 0:hi_ - lo], bank[e % 2][:, 0:hi_ - lo], ACT.Exp).then_inc(once("exp"), 1)
                elif step[0] == "V":
                    e = step[1]
                    br, cc, j = units[e % NU][0:3]
                    if e % NU + 1 == NU or units[e % NU + 1][0:2] != (br, cc):
                        n = 6 * (e // NU) + 2 * br + cc
                        act.wait_ge(once("pv"), e + 1)
                        if n >= 2:
                            act.wait_ge(once("ot"), n - 1)
                        a(osb[n % 2][:, :], bank[6][0:HD + 1, :]).then_inc(once("osb"), 1)

            for m in range(2 * ST + 1):
                if m < 2 * ST:
                    if m == ST:
                        attention_step(("PQ", 0))
                    act.wait_ge(once("krot"), m + 1)
                    if m >= 2:
                        act.wait_ge(s_tr, key_fill(m - 2) + 1)
                    a(kcat[m % 2][:, :, 0, :], rt1[:, 0:P].rearrange("p (g d) -> p g d", g=GROUPS))\
                        .then_inc(once("khi"), 1)
                if m == ST + 1:
                    for hf in range(2):
                        bk = fill(first["q"] + hf)
                        act.wait_ge(s_trf, first["q"] + hf)
                        a(q1[0][:, hf * HALF:(hf + 1) * HALF], bk).then_inc(s_trf, 1)
                if m >= 1:
                    b, i = divmod(m - 1, ST)
                    bk = fill(key_fill(m - 1))
                    a(k1[b][:, :, P * i:P * i + P], bk[:, 0:2 * P].rearrange("p (g s) -> p g s", g=GROUPS))\
                        .then_inc(once("k1"), 1)

            for step in plan:
                attention_step(step)

            def split_d(n):
                rows = KT + (4 if n % 2 == 0 else 2)
                act.wait_ge(once(f"draw{n % 2}"), 32 * (n // 2 + 1))
                if n >= 2:
                    act.wait_ge(once("dgate"), 2 * (n - 1))
                    act.wait_ge(once("dproj"), 2 * (n - 1))
                a(dhi[n % 2][:, 0:rows, :], draw[n % 2][:, 0:rows, :]).then_inc(once("dhi"), 1)

            act.wait_ge(once("norm"), 4 * HEADS)
            split_d(0)
            for n in range(8):
                b, hf = divmod(n, 2)
                act.wait_ge(once("att"), n + 1)
                if n == 0:
                    act.wait_ge(once("azl"), 2)
                a(at_hi[:, b, hf * HALF:(hf + 1) * HALF], bank[n]).then_inc(once("athi"), 1)
            for r in range(2):
                a(so_hi[:, r, :], so[:, r, :]).then_inc(once("sohi"), 1)
            split_d(1)
            for nb in range(KT):
                for kind in range(2):
                    for cc in range(NC_HALF):
                        m = 4 * nb + 2 * kind + cc
                        act.wait_ge(once("dgate"), m + 1)
                        if m >= 1:
                            act.wait_ge(once("dmul"), m)
                        a(dsig[:, :], bank[2 * (m % 4)], ACT.Sigmoid).then_inc(once("dsig"), 1)
                    if 2 * nb + kind + 2 < 2 * KT:
                        split_d(2 * nb + kind + 2)

            split_m = lambda i: a(mhi[i % 2][:, :, :], mt[:, :, P * i:P * i + P]).then_inc(once("mhi"), 1)
            act.wait_ge(once("dgate"), 4 * KT)
            for k in range(KT):
                act.wait_ge(once(f"oraw{k}"), 16)
                a(ohi[:, k, :], oraw[:, k, :]).then_inc(once("ohi"), 1)
                if k == 1:
                    act.wait_ge(once("merged"), 2 * KT)
                    split_m(0)
            for i in range(ST):
                if i + 1 < ST:
                    if i >= 1:
                        act.wait_ge(once("ounit"), 2 * i)
                    split_m(i + 1)
                act.wait_ge(once("res"), i + 1)
                if i >= 1:
                    act.wait_ge(once("osq"), i)
                a(ojunk[:, :], yr[i % 2][:, :], ACT.Square, accum_out=oss[:, 0, i:i + 1]).then_inc(once("osq"), 1)
                act.wait_ge(once("ovar"), i + 1)
                a(oss[:, 2, i:i + 1], oss[:, 1, i:i + 1], ACT.Sqrt).then_inc(once("osd"), 1)

        @block.vector
        def _(dve):
            ch = Chain(dve, s_ch_d)
            V = nc.vector

            def tt(o, a, b, op):
                return V.tensor_tensor(o, a, b, op)

            for b in range(2):
                four = slice(4 * b, 4 * b + 4)
                dve.wait_ge(s_sq, 4 * b + 4)
                V.tensor_scalar(ss[:, four], ss[:, four], 1.0 / D_MODEL, EPS, ALU.mult, ALU.add).then_inc(s_var, 1)
                dve.wait_ge(s_sd, b + 1)
                V.reciprocal(rs[:, four], rs[:, four]).then_inc(s_rs, 1)
                dve.wait_ge(s_rs, b + 1)
                for i in range(4 * b, 4 * b + 4):
                    V.tensor_scalar(xs[:, i, :], xs[:, i, :], rs[:, i:i + 1], None, ALU.mult).then_inc(s_xn, 1)
                for k in range(1, KT, 2):
                    n = KT * b + k
                    dve.wait_ge(s_xtr, n + 1)
                    V.tensor_copy(xt[:, k, b * HALF:(b + 1) * HALF], bank[4 + n % 4]).then_inc(once("xtd"), 1)
            dve.wait_ge(s_id, 16)
            V.tensor_copy(identb[:, :], ident[:, :]).then_inc(once("identb"), 1)
            dve.wait_ge(once("den"), 1)
            V.reciprocal(sm[:, 9, :], sm[:, 8, :]).then_inc(once("rden"), 1)
            V.memset(mrow[:, :], 0.0).then_inc(once("mrow"), 1)
            dve.wait_ge(s_whi, 1)
            tt(wlo[0][:, :, 0:256], wraw[:, :, 0:256], f(whi[0][:, :, 0:256]), ALU.subtract).then_inc(s_wlo, 1)
            dve.wait_ge(s_mod, 1)
            dve.wait_ge(once("mrow"), 1)
            for j in range(1, 4, 2):
                V.tensor_copy(mrow[32 * j:32 * j + 1, :], bank[j][0:1, :]).then_inc(once("mrow"), 1)
            dve.wait_ge(s_mod_in, 32)
            dve.wait_ge(once("mcol"), 1)
            mcol = bank[5].rearrange("p (q r) -> p r q", q=4)[:, ::32, :]
            ch.link(tt(modc[:, :].rearrange("p (b q) -> p b q", b=4), mcol,
                       bcol[:, :].rearrange("p (b q) -> p b q", b=4), ALU.add))
            ch.link(V.scalar_tensor_tensor(out=g1[:, :], in0=modc[:, KT:2 * KT], scalar=1.0, in1=gcol[:, :],
                                           op0=ALU.add, op1=ALU.mult))
            dve.wait_ge(once("xta"), 8)

            def h_lo(k):
                dve.wait_ge(s_hhi, k + 1)
                tt(ht_lo[:, k, :], xt[:, k, :], f(ht_hi[:, k, :]), ALU.subtract).then_inc(s_hlo, 1)

            def split_w(w):
                n = CHUNKS[w][1]
                dve.wait_ge(s_whi, w + 1)
                tt(wlo[w % 2][:, :, 0:n], wraw[:, :, 0:n], f(whi[w % 2][:, :, 0:n]), ALU.subtract).then_inc(s_wlo, 1)

            for k in range(KT):
                V.tensor_scalar(xt[:, k, :], xt[:, k, :], g1[:, k:k + 1], modc[:, k:k + 1], ALU.mult, ALU.add)\
                    .then_inc(s_h32, 1)
                if k >= 1:
                    h_lo(k - 1)
            h_lo(KT - 1)
            split_w(1)
            dve.wait_ge(s_small, 16 * 5)
            V.tensor_copy(maskb[:, :, :], mload[:, :, :]).then_inc(s_masks, 1)
            V.tensor_copy(cmpq[:, :, :], cqload[:, :, :]).then_inc(s_masks, 1)
            V.tensor_copy(cmpt[:, :], ctload[:, :]).then_inc(s_masks, 1)
            split_w(2)
            split_w(3)

            def rotate(src, i, width, last_read=True):
                hn = width // HD
                v = src[:, 0:width].rearrange("p (h a d) -> p h a d", h=hn, a=2)
                a1 = rt1[:, 0:width].rearrange("p (h a d) -> p h a d", h=hn, a=2)
                a2 = rt2[:, 0:width].rearrange("p (h a d) -> p h a d", h=hn, a=2)
                shp = [P, hn, 2, HD // 2]
                cv = rope[:, i, 0, :].rearrange("p (a d) -> p a d", a=2).unsqueeze(1).to_broadcast(shp)
                sv = rope[:, i, 1, :].rearrange("p (a d) -> p a d", a=2).unsqueeze(1).to_broadcast(shp)
                ch.mark(tt(a1, v, cv, ALU.mult))
                ins = tt(a2, v[:, :, ::-1, :], sv, ALU.mult)
                if last_read:
                    ins.then_inc(s_evd, 1)
                else:
                    ch.mark(ins)
            def q_chunk(w, between=iter(())):
                for _ in range(8):
                    next(between, None)
                for i in range(ST):
                    n = unit_no[(w, i)]
                    dve.wait_ge(s_unit, n + 1)
                    if w == Q0_ and i == 0:
                        dve.wait_ge(s_tr, first["ut"] + 4)
                    if w == Q1_ and i == 0:
                        dve.wait_ge(once("efn"), 2)
                    if (w, i) != (Q0_, 0):
                        dve.wait_ge(once("qrot"), ST * (w - Q0_) + i)
                    rotate(unit_bank(n), i, 256)
                    dve.wait_ge(s_evd, read_count(reads_d, n + 1))
                    dst = qa[:, 2 * (w - Q0_):2 * (w - Q0_) + 2, i, :]
                    ch.wait()
                    tt(dst, rt1[:, :].rearrange("p (b d) -> p b d", b=2), rt2[:, :].rearrange("p (b d) -> p b d", b=2),
                       ALU.add).then_inc(once("qrot"), 1)
                    for _ in range(4):
                        next(between, None)
                for _ in between:
                    pass

            def states():
                bR, bI, zR, zI, eC, eS = (t[:, :, :] for t in (b_r, b_i, zr, zi, ecos, esin))
                yield ch.mark(V.memset(b_r[:, :, 0:1], 0.0))
                yield ch.link(V.memset(b_i[:, :, 0:1], 0.0))
                yield ch.link(tt(zR, bR, eC, ALU.mult))
                yield ch.link(tt(zI, bI, eS, ALU.mult))
                yield ch.link(tt(zR, zR, zI, ALU.add))
                yield ch.link(tt(zI, bR, eS, ALU.mult))
                yield ch.link(tt(bI, bI, eC, ALU.mult))
                yield ch.link(tt(bI, bI, zI, ALU.subtract))
                for t in range(SSM_T):
                    d0 = sm[:, 4, t:t + 1].to_broadcast([P, NCH])
                    ch.mark(V.tensor_tensor_scan(b_r[:, t, :], d0, zr[:, t, :], 0.0, ALU.mult, ALU.add))
                    yield ch.mark(V.tensor_tensor_scan(zi[:, t, :], d0, b_i[:, t, :], 0.0, ALU.mult, ALU.add))
                ch.wait()
                yield ch.link(tt(zR, bR, eC, ALU.mult))
                yield ch.link(tt(bI, zI, eS, ALU.mult))
                yield ch.link(tt(zR, zR, bI, ALU.subtract))
                yield ch.link(tt(bI, bR, eS, ALU.mult))
                yield ch.link(tt(zI, zI, eC, ALU.mult))
                yield tt(zI, zI, bI, ALU.add).then_inc(once("rot"), 1)

            q_chunk(Q0_)
            dve.wait_ge(s_trf, first["bu"] + 4)
            dve.wait_ge(once("ecos"), 1)
            q_chunk(Q1_, states())

            def kc_keys(i):
                n = unit_no[(KC_, i)]
                dve.wait_ge(s_unit, n + 1)
                if i == 0:
                    dve.wait_ge(s_trf, first["yt"] + 4)
                if i >= 1:
                    dve.wait_ge(once("kcat"), i)
                else:
                    dve.wait_ge(once("qrot"), 2 * ST)
                rotate(unit_bank(n), i, P)
                dve.wait_ge(s_evd, read_count(reads_d, n + 1))
                if i >= 4:
                    dve.wait_ge(s_tr, first["kc"] + 4)
                shp = [P, GROUPS, 2, HD]
                ch.wait()
                tt(catc[i % 4][:, 0, :, :, :],
                   rt1[:, 0:P].rearrange("p (g d) -> p g d", g=GROUPS).unsqueeze(2).to_broadcast(shp),
                   rt2[:, 0:P].rearrange("p (g d) -> p g d", g=GROUPS).unsqueeze(2).to_broadcast(shp),
                   ALU.add).then_inc(once("kcat"), 1)

            def next_rows(hf):
                for q in range(4):
                    fl = first["kc"] + 4 * hf + q
                    r, g = divmod(q, 2)
                    dve.wait_ge(s_tr, fl + 1)
                    dve.wait_ge(once("t2a"), 4 * hf + q + 1)
                    lo = hf * HALF
                    s0 = 1 if hf == 0 else 0
                    V.tensor_copy(t2[HD:P, r, g, lo + s0 - 1:lo + HALF - 1], bank[fl % 2][HD:P, s0:HALF])\
                        .then_inc(s_trf, 1)

            for i in range(4):
                kc_keys(i)
            for n in range(4):
                nb, cc = divmod(n, 2)
                dve.wait_ge(once("glu"), 2 * n + 2)
                dve.wait_ge(once("glugate"), n + 1)
                v = so[:, nb, cc * HALF:(cc + 1) * HALF]
                tt(v, bank[1], v, ALU.mult).then_inc(once("gluo"), 1)
            next_rows(0)
            for i in range(4, ST):
                kc_keys(i)
            for i in range(ST):
                if i == 3:
                    next_rows(1)
                n = unit_no[(Z0_, i)]
                dve.wait_ge(s_unit, n + 1)
                V.tensor_copy(gates[:, i, :], unit_bank(n)[:, 0:NGATE]).then_inc(s_evd, 1)
            for r in range(2):
                dve.wait_ge(once("pe"), 2)
                dve.wait_ge(once("cmpw"), 16 * 8)
                tt(hb[:, r:r + 1], bank[2][:, r:r + 1], b1c[r][:, :], ALU.add).then_inc(once("hbias"), 1)
            V.tensor_copy(w2d[:, :, :], w2[0][:, :].unsqueeze(1).to_broadcast([P, 2, HD])).then_inc(once("w2d"), 1)
            ch.mark(V.memset(f(k1c[:, :, :]), 0.0))
            ch.link(V.memset(f(k2c[:, :, :]), 0.0))
            dve.wait_ge(once("kcps"), 1)
            kp = bank[2][:, 2:2 + GROUPS * NCMP]
            kp3 = kp.rearrange("p (g n) -> p g n", g=GROUPS)
            for a_ in range(2):
                ch.mark(V.tensor_copy(k1c[0:HD, :, a_, 0:NCMP], kp3[0:HD]))
                ch.mark(V.tensor_copy(k2c[0:HD, :, a_, 0:NCMP], kp3[0:HD]))
            ch.link(V.tensor_copy(kch[HD:P, :], kp[HD:P]))
            for a_ in range(2):
                ch.mark(tt(k1c[HD:P, :, a_, 0:NCMP], kp3[HD:P],
                           f(kch[HD:P, :]).rearrange("p (g n) -> p g n", g=GROUPS), ALU.subtract))
                ch.mark(V.tensor_copy(k2c[HD:P, :, a_, :],
                                      aug[HD:P, 0:1].unsqueeze(1).to_broadcast([HD, GROUPS, 64])))
            dve.wait_ge(once("vcps"), 1)
            dve.wait_ge(once("vc0"), 3)
            for r0 in (0, HD):
                rows = slice(r0, r0 + NCMP)
                for g in range(GROUPS):
                    ch.mark(V.tensor_copy(vchi[rows, g, 0:HD], bank[3][rows, HD * g:HD * g + HD]))
            ch.mark(V.memset(f(vchi[:, :, HD:HD + 1]), 1.0))
            ch.wait()
            for g in range(GROUPS):
                tt(vclo[0:NCMP, g, 0:HD], bank[3][0:NCMP, HD * g:HD * g + HD],
                   f(vchi[0:NCMP, g, 0:HD]), ALU.subtract).then_inc(once("cmpdone"), 1)
            def weights_low(e):
                br, n = units[e % NU][0], units[e % NU][4] - units[e % NU][3]
                w, wh = pt[e % NPT], phi[e % NPT]
                if br == 0:
                    return
                dve.wait_ge(once("exp"), 2 * e + 2)
                tt(plo[e % NPT][:, 0:n], w[:, 0:n], f(wh[:, 0:n]), ALU.subtract).then_inc(once("plo"), 1)

            def attention_step(step):
                if step[0] == "PQ":
                    h = step[1]
                    dve.wait_ge(once("qhi"), h + 1)
                    dve.wait_ge(once("qrot"), 2 * ST)
                    if h >= 1:
                        dve.wait_ge(once("mt"), 2 * h)
                    v = qa[:, h // 2, :, HD * (h % 2):HD * (h % 2) + HD]
                    V.scalar_tensor_tensor(out=qc2[:, :, 0:HD], in0=v, scalar=1.0 / math.sqrt(HD),
                                           in1=f(qc1[:, :, 0, :]), op0=ALU.mult, op1=ALU.subtract)\
                        .then_inc(once("qlo"), 1)
                elif step[0] == "S" and step[1] >= 1:
                    weights_low(step[1] - 1)
                elif step[0] == "V" and step[1] == HEADS * NU - LAG:
                    weights_low(HEADS * NU - 1)
                elif step[0] == "MX":
                    _, h, i = step
                    n = max_no(h, i)
                    m = mx[h % 2]
                    dve.wait_ge(once("ms"), n + 1)
                    V.tensor_reduce(m[:, i, 1:2], slc_max[:, 0:P * (i + 1)], AX.X, ALU.max).then_inc(once("msr"), 1)
                elif step[0] == "MW":
                    _, h, i = step
                    n = max_no(h, i)
                    m = mx[h % 2]
                    dve.wait_ge(once("mw"), n + 1)
                    buf = other_max(h, i)
                    ch.mark(V.tensor_reduce(m[:, i, 0:1], buf[:, 640:704], AX.X, ALU.max))
                    V.tensor_reduce(m[:, i, 2:3], buf[:, 0:P * min(i + 1, WIN_TILES + 1)], AX.X, ALU.max)\
                        .then_inc(once("mwr"), 1)
                elif step[0] == "MC":
                    _, h, part = step
                    q2v = qc2[:, :, HD:HD + 6].rearrange("p i (b a) -> p i b a", a=2)
                    if part == 0:
                        dve.wait_ge(once("mwr"), ST * (h + 1))
                        V.tensor_scalar(mneg[:, :, :], mx[h % 2][:, :, :], MAX_FLOOR, -1.0, ALU.max, ALU.mult)\
                            .then_inc(once("mneg"), 1)
                    elif part == 1:
                        dve.wait_ge(once("mneg"), h + 1)
                        V.tensor_copy(mneg_hi[:, :, :], mneg[:, :, :]).then_inc(once("mneghi"), 1)
                    elif part == 2:
                        dve.wait_ge(once("mneghi"), h + 1)
                        V.tensor_copy(q2v[:, :, :, 0], f(mneg_hi[:, :, :])).then_inc(once("mcat"), 1)
                    else:
                        tt(q2v[:, :, :, 1], mneg[:, :, :], f(mneg_hi[:, :, :]), ALU.subtract).then_inc(once("mcat"), 1)
                elif step[0] == "ND":
                    _, n, part = step
                    h, r = divmod(n, 6)
                    br, cc = divmod(r, 2)
                    o3 = bank[7][:, 0:4 * VW].rearrange("p (i d) -> p i d", i=4)
                    if part == 0:
                        dve.wait_ge(once("ot"), n + 1)
                        V.tensor_scalar(lsum[:, :], o3[:, :, HD], TINY, None, ALU.max).then_inc(once("lsum"), 1)
                    elif part == 1:
                        dve.wait_ge(once("lsum"), n + 1)
                        V.reciprocal(lsum[:, :], lsum[:, :]).then_inc(once("lrec"), 1)
                    elif part == 2:
                        dve.wait_ge(once("lrec"), n + 1)
                        if n == 0:
                            dve.wait_ge(once("gates"), 1)
                        tt(wrow[:, :], lsum[:, :], gates[:, 4 * cc:4 * cc + 4, 3 * h + br], ALU.mult)\
                            .then_inc(once("wrow"), 1)
                    else:
                        dve.wait_ge(once("wrow"), n + 1)
                        wb = wrow[:, :].unsqueeze(2).to_broadcast([P, 4, HD])
                        if br == 0:
                            dst = qa[:, h // 2, 4 * cc:4 * cc + 4, HD * (h % 2):HD * (h % 2) + HD]
                        else:
                            dst = otmp[:, :, :]
                            if 4 * h + r - 2 >= 1:
                                dve.wait_ge(once("norm"), 4 * h + r - 2)
                        tt(dst, o3[:, :, 0:HD], wb, ALU.mult).then_inc(once("b7"), 1)

            split_w(8)

            def key_rows(m):
                b, i = divmod(m, ST)
                fl = key_fill(m)
                dve.wait_ge(s_tr, fl + 1)
                dve.wait_ge(once("k1"), m + 1)
                V.tensor_copy(k2[b][0:HD, :, P * i:P * i + P],
                              bank[fl % 2][0:HD, 0:2 * P].rearrange("p (g s) -> p g s", g=GROUPS))\
                    .then_inc(s_trf, 1)

            for m in range(2 * ST):
                b, i = divmod(m, ST)
                n = unit_no[((KS_, KW_)[b], i)]
                if m >= EARLY:
                    attention_step(("MX", 0, m - EARLY))
                dve.wait_ge(s_unit, n + 1)
                if m == 0:
                    dve.wait_ge(s_whi, len(CHUNKS))
                    dve.wait_ge(s_wlo, len(CHUNKS))
                if m >= 1:
                    dve.wait_ge(once("klo"), m)
                rotate(unit_bank(n), i, P, last_read=False)
                vsrc = unit_bank(n)[:, P:2 * P].rearrange("p (g d) -> p g d", g=GROUPS)
                ch.link(V.tensor_copy(vhi[b][:, i, :, 0:HD], vsrc))
                tt(rt1[:, 0:P], rt1[:, 0:P], rt2[:, 0:P], ALU.add).then_inc(once("krot"), 1)
                tt(vlo[b][:, i, :, :], vsrc, f(vhi[b][:, i, :, 0:HD]), ALU.subtract).then_inc(s_evd, 1)
                dve.wait_ge(once("krot"), m + 1)
                dve.wait_ge(once("khi"), m + 1)
                kc_ = kcat[m % 2]
                tt(kc_[:, :, 1, :], rt1[:, 0:P].rearrange("p (g d) -> p g d", g=GROUPS),
                   f(kc_[:, :, 0, :]), ALU.subtract).then_inc(once("klo"), 1)
                if m == ST:
                    attention_step(("PQ", 0))
                if m >= 1:
                    key_rows(m - 1)
            attention_step(("MX", 0, ST - 2))
            attention_step(("MW", 0, 0))
            key_rows(2 * ST - 1)
            attention_step(("MX", 0, ST - 1))

            for step in plan:
                attention_step(step)

            def split_d(n):
                rows = KT + (4 if n % 2 == 0 else 2)
                dve.wait_ge(once("dhi"), n + 1)
                tt(dlo[n % 2][:, 0:rows, :], draw[n % 2][:, 0:rows, :], f(dhi[n % 2][:, 0:rows, :]), ALU.subtract)\
                    .then_inc(once("dlo"), 1)

            dve.wait_ge(once("norm"), 4 * HEADS)
            for hf in range(2):
                v = qa[:, 3, 4 * hf:4 * hf + 4, :]
                tt(v, v, zs[:, 4 * hf:4 * hf + 4, 3 * P:4 * P], ALU.mult).then_inc(once("azl"), 1)
            split_d(0)
            for n in range(8):
                b, hf = divmod(n, 2)
                dve.wait_ge(once("athi"), n + 1)
                dve.wait_ge(once("att"), 2 * b + 2)
                tt(at_lo[:, b, hf * HALF:(hf + 1) * HALF], bank[n],
                   f(at_hi[:, b, hf * HALF:(hf + 1) * HALF]), ALU.subtract).then_inc(once("atlo"), 1)
            for r in range(2):
                dve.wait_ge(once("sohi"), r + 1)
                tt(so_lo[:, r, :], so[:, r, :], f(so_hi[:, r, :]), ALU.subtract).then_inc(once("sosplit"), 1)
            split_d(1)
            for nb in range(KT):
                for kind in range(2):
                    for cc in range(NC_HALF):
                        m = 4 * nb + 2 * kind + cc
                        dve.wait_ge(once("dsig"), m + 1)
                        dve.wait_ge(once("dproj"), m + 1)
                        dst = mt[:, nb, cc * HALF:(cc + 1) * HALF]
                        if kind == 0:
                            tt(dst, bank[2 * (m % 4) + 1], dsig[:, :], ALU.mult).then_inc(once("dmul"), 1)
                        else:
                            tt(dtm[:, :], bank[2 * (m % 4) + 1], dsig[:, :], ALU.mult).then_inc(once("dmul"), 1)
                            dve.wait_ge(once("dmul"), m + 1)
                            tt(dst, dst, dtm[:, :], ALU.add).then_inc(once("merged"), 1)
                            dve.wait_ge(once("merged"), 2 * nb + cc + 1)
                    if 2 * nb + kind + 2 < 2 * KT:
                        split_d(2 * nb + kind + 2)

            def split_m(i):
                dve.wait_ge(once("mhi"), i + 1)
                tt(mlo[i % 2][:, :, :], mt[:, :, P * i:P * i + P], f(mhi[i % 2][:, :, :]), ALU.subtract)\
                    .then_inc(once("mlo"), 1)
            for k in range(KT):
                dve.wait_ge(once("ohi"), k + 1)
                tt(olo[:, k, :], oraw[:, k, :], f(ohi[:, k, :]), ALU.subtract).then_inc(once("olo"), 1)
                if k == 0:
                    split_m(0)
            dve.wait_ge(once("gps"), 1)
            dve.wait_ge(once("gbias"), 16)
            for hf in range(2):
                s = slice(HALF * hf, HALF * hf + HALF)
                ch.mark(tt(gateb[:, s], bank[4 + hf], gbias[:, s], ALU.add))
            ch.wait()
            dve.wait_ge(once("fgb"), 16)
            for i in range(ST):
                if i + 1 < ST:
                    split_m(i + 1)
                dve.wait_ge(once(f"xr{i % 2}"), 16 * (i // 2 + 1))
                if i >= 2:
                    dve.wait_ge(once(f"out{i % 2}"), 16 * (i // 2))
                y = yr[i % 2]
                for hf in range(2):
                    s = slice(HALF * hf, HALF * hf + HALF)
                    dve.wait_ge(once("ounit"), 2 * i + hf + 1)
                    tt(y[:, s], bank[2 * (i % 2) + hf], gateb[:, s], ALU.mult).then_inc(once("oread"), 1)
                dve.wait_ge(once("oread"), 2 * i + 2)
                tt(y[:, :], y[:, :], xr[i % 2][:, :], ALU.add).then_inc(once("res"), 1)
                dve.wait_ge(once("osq"), i + 1)
                V.tensor_scalar(oss[:, 1, i:i + 1], oss[:, 0, i:i + 1], 1.0 / D_MODEL, EPS, ALU.mult, ALU.add)\
                    .then_inc(once("ovar"), 1)
                dve.wait_ge(once("osd"), i + 1)
                ch.link(V.reciprocal(oss[:, 2, i:i + 1], oss[:, 2, i:i + 1]))
                V.scalar_tensor_tensor(out=y[:, :], in0=y[:, :], scalar=oss[:, 2, i:i + 1], in1=fgb[:, :],
                                       op0=ALU.mult, op1=ALU.mult).then_inc(once("y"), 1)

        @block.tensor
        def _(pe):
            T = nc.tensor

            def mm(o, l, r, start, stop, **kw):
                return T.matmul(o, l, r, start=start, stop=stop, **kw)

            def tr(o, i, rows=P):
                return T.transpose(o, i, ident[0:rows, 0:rows])

            def three(o, parts, start=True, stop=True, **kw):
                n = 3 * len(parts)
                m = 0
                for lh, ll, rh, rl in parts:
                    for l, r in ((lh, rh), (lh, rl), (ll, rh)):
                        ins = mm(o, l, r, start and m == 0, stop and m == n - 1, **kw)
                        m += 1
                return ins

            def ada_mm(k):
                pe.wait_ge(s_ada[k], 16)
                for j in range(4):
                    ins = mm(bank[j][0:1, :], scol[:, k:k + 1], ada[:, k, j * HALF:(j + 1) * HALF],
                             k == 0, k == KT - 1)
                return ins
            pe.wait_ge(s_id, 16)
            for n in range(16):
                cc, k = divmod(n, KT)
                if k == 0:
                    pe.wait_ge(s_xn, 4 * cc + 4)
                if n >= 4:
                    if n % 2 == 0:
                        pe.wait_ge(once("xta"), (n - 4) // 2 + 1)
                    else:
                        pe.wait_ge(once("xtd"), (n - 5) // 2 + 1)
                for q in range(4):
                    ins = tr(bank[4 + n % 4][:, P * q:P * q + P], xs[:, 4 * cc + q, P * k:P * k + P])
                ins.then_inc(s_xtr, 1)
                if n == KT - 1:
                    pe.wait_ge(s_silu, 1)
                    ada_mm(0)
                    ada_mm(1)
            for k in range(2, KT):
                ins = ada_mm(k)
            ins.then_inc(s_mod, 1)
            pe.wait_ge(once("cld"), 16 * 2 * SSM_T)
            pe.wait_ge(once("xta"), 7)
            for r in range(2):
                ins = tr(bank[4][:, P * r:P * r + P], cld[r][:, :])
            ins.then_inc(once("ctr"), 1)
            pe.wait_ge(once("xtd"), 8)
            pe.wait_ge(once("mrow"), 5)
            for q in range(4):
                ins = tr(bank[5][:, P * q:P * q + P], mrow[:, P * q:P * q + P])
            ins.then_inc(once("mcol"), 1)

            def bank_free(n):
                m = n - 4
                if m < ST:
                    return
                if read_count(reads_d, m + 1):
                    pe.wait_ge(s_evd, read_count(reads_d, m + 1))
                pe.wait_ge(s_eva, read_count(reads_a, m + 1))

            def fill_free(n):
                if n >= 2:
                    pe.wait_ge(s_trf, n - 1)

            pe.wait_ge(s_whi, 1)
            pe.wait_ge(s_wlo, 1)
            for k in range(KT):
                pe.wait_ge(s_hlo, k + 1)
                for j in range(ST):
                    tok = slice(j, SEQ, CH)
                    parts = ((ht_hi, whi[0]), (ht_hi, wlo[0]), (ht_lo, whi[0]))
                    for m, (l, r) in enumerate(parts):
                        ins = mm(unit_bank(j), l[:, k, tok], r[:, k, 0:256],
                                 k == 0 and m == 0 and j % 2 == 0, k == KT - 1 and m == 2,
                                 skip_group_check=True)
            ins.then_inc(s_unit, ST)

            def project(w, tiles=range(ST)):
                pe.wait_ge(s_whi, w + 1)
                pe.wait_ge(s_wlo, w + 1)
                wh, wl = whi[w % 2], wlo[w % 2]
                for i in tiles:
                    n = unit_no[(w, i)]
                    bank_free(n)
                    if w == ZS_:
                        nb, cc = divmod(i, 2)
                        cs, ts = slice(P * nb, P * nb + P), slice(cc * HALF, (cc + 1) * HALF)
                        ins = three(unit_bank(n), [(wh[:, k, cs], wl[:, k, cs], ht_hi[:, k, ts], ht_lo[:, k, ts])
                                                   for k in range(KT)])
                    else:
                        width, ts = CHUNKS[w][1], slice(P * i, P * i + P)
                        ins = three(unit_bank(n)[:, 0:width],
                                    [(ht_hi[:, k, ts], ht_lo[:, k, ts], wh[:, k, 0:width], wl[:, k, 0:width])
                                     for k in range(KT)])
                    ins.then_inc(s_unit, 1)

            project(ZS_, range(4))
            pe.wait_ge(once("gs"), 2)
            pe.wait_ge(s_eva, ST)
            for q in range(4):
                r, th = divmod(q, 2)
                n = first["gt"] + q
                fill_free(n)
                for t in range(4):
                    ins = tr(bank[n % 2][:, P * t:P * t + P],
                             gs[r][:, 4 * th + t, :, :].rearrange("p j c -> p (j c)"))
                ins.then_inc(s_tr, 1)
            pe.wait_ge(once("cp"), 1)
            for q in range(4):
                gp, th = divmod(q, 2)
                n = first["klag"] + q
                fill_free(n)
                s = slice(SS * gp, SS * gp + SS)
                for m in range(4):
                    t = 4 * th + m
                    for r in range(2):
                        ins = mm(bank[n % 2][0:SC, P * m:P * m + P], bbar[r][s, t, :],
                                 cp[r][s, t, 0:CH, :].rearrange("p j c -> p (j c)"), r == 0, r == 1)
                ins.then_inc(s_tr, 1)
            for q in range(4):
                n = first["ut"] + q
                fill_free(n)
                for m in range(4):
                    ins = tr(bank[n % 2][:, P * m:P * m + P],
                             utok[:, 4 * q + m, :, :].rearrange("p j c -> p (j c)"))
                ins.then_inc(s_tr, 1)
            project(Q0_)
            pe.wait_ge(s_trf, first["ut"] + 4)
            for q in range(4):
                r, th = divmod(q, 2)
                n = first["bu"] + q
                fill_free(n)
                for m in range(4):
                    t = 4 * th + m
                    for gp in range(2):
                        ins = mm(bank[n % 2][SS * gp:SS * gp + SS, P * m:P * m + P],
                                 gt[r][:, t, SS * gp:SS * gp + SS], ut[:, 2 * t + gp, :], True, True)
                ins.then_inc(s_tr, 1)
            project(Q1_)
            pe.wait_ge(once("rot"), 1)
            pe.wait_ge(once("toep"), 16 * CH)
            for q in range(4):
                n = first["y"] + q
                fill_free(n)
                gp, th = divmod(q, 2)
                s = slice(SS * gp, SS * gp + SS)
                for m in range(4):
                    t = 4 * th + m
                    g = 2 * t + gp
                    o = bank[n % 2][:, P * m:P * m + P]
                    for r, st in enumerate((zr, zi)):
                        mm(o, st[s, t, :], cp[r][s, t, 1:9, :].rearrange("p j c -> p (j c)"), r == 0, False)
                    ins = mm(o, ut[:, g, :], toep[:, g, :], False, True)
                ins.then_inc(s_tr, 1)
            project(KC_, range(4))
            pe.wait_ge(s_trf, first["y"] + 4)
            for q in range(4):
                ctile, jh = divmod(q, 2)
                n = first["yt"] + q
                fill_free(n)
                for m in range(4):
                    ins = tr(bank[n % 2][:, P * m:P * m + P], ytok[:, 4 * jh + m, P * ctile:P * ctile + P])
                ins.then_inc(s_tr, 1)
            project(KC_, range(4, ST))
            pe.wait_ge(once("wglu"), 16)
            pe.wait_ge(s_trf, first["yt"] + 4)
            for n in range(4):
                nb, cc = divmod(n, 2)
                for part in range(2):
                    if n >= 1:
                        pe.wait_ge(once("glusig" if part == 0 else "gluo"), n)
                    col = P * (nb + 2 * (1 - part))
                    for k in range(2):
                        ins = mm(bank[part], wglu[:, k, col:col + P], yt[:, k, cc * HALF:(cc + 1) * HALF],
                                 k == 0, k == 1)
                    ins.then_inc(once("glu"), 1)
            pe.wait_ge(once("gluo"), 4)
            pe.wait_ge(once("glusig"), 4)
            for hf in range(2):
                pe.wait_ge(once("kcat"), 4 * (hf + 1))
                pe.wait_ge(s_eva, read_count(reads_a, unit_no[(KC_, 4 * hf + 3)] + 1))
                for q in range(4):
                    r, g = divmod(q, 2)
                    n = first["kc"] + 4 * hf + q
                    if 4 * hf + q >= 2:
                        fill_free(n)
                    for m in range(4):
                        ins = tr(bank[n % 2][:, P * m:P * m + P],
                                 catc[m][:, r, g, :, :].rearrange("p a d -> p (a d)"))
                    ins.then_inc(s_tr, 1)
                project(Z0_, range(3) if hf == 0 else range(3, ST))
            pe.wait_ge(once("cmpw"), 16 * 8)
            pe.wait_ge(s_trf, first["kc"] + 8)
            for r in range(2):
                o = bank[r][:, 0:GROUPS * NCMP].rearrange("p (g n) -> p g n", g=GROUPS)
                for m in range(PAIRS):
                    ins = mm(o, w1[r][:, m, :], t2[:, r, :, 2 * m:2 * m + CMP_STRIDE * (NCMP - 1) + 1:CMP_STRIDE],
                             m == 0, m == PAIRS - 1)
                ins.then_inc(once("hid"), 1)
                for m in range(PAIRS):
                    ins = mm(bank[2][:, r:r + 1], w1[r][:, m, :], pec[r][:, m:m + 1], m == 0, m == PAIRS - 1)
                ins.then_inc(once("pe"), 1)
            pe.wait_ge(once("hbias"), 2)
            pe.wait_ge(once("w2d"), 1)
            pe.wait_ge(once("hidev"), 1)
            mm(bank[2][:, 2:2 + GROUPS * NCMP], w2d[:, :, :].rearrange("p a d -> p (a d)"), hid[0][:, :],
               True, True).then_inc(once("kcps"), 1)
            pe.wait_ge(once("hidev"), 2)
            for r0 in (0, HD):
                for g in range(GROUPS):
                    ins = mm(bank[3][r0:r0 + NCMP, HD * g:HD * g + HD], hid[1][:, NCMP * g:NCMP * g + NCMP],
                             w2[1][:, :], True, True)
            ins.then_inc(once("vcps"), 1)
            project(Z1_)

            K1 = lambda br, g, s: k1c[:, g, :, :].rearrange("p a n -> p (a n)") if br == 0 else k1[br - 1][:, g, s]
            K2 = lambda br, g, s: (k2c[:, g, :, :].rearrange("p a n -> p (a n)") if br == 0 else k2[br - 1][:, g, s])[0:NQ2]
            b7 = q1_ready = q2_ready = 0

            def attention_step(step):
                nonlocal b7, q1_ready, q2_ready
                if step[0] == "MQ":
                    h, hf = step[1:]
                    pe.wait_ge(once("qdup"), h + 1)
                    if h == 0:
                        n = first["q"] + hf
                        fill_free(n)
                    elif b7:
                        pe.wait_ge(once("b7"), b7)
                    o = bank[n % 2] if h == 0 else bank[7]
                    for q in range(4):
                        ins = tr(o[:, P * q:P * q + P],
                                 f(qc1[:, 4 * hf + q, :, :]).rearrange("p a d -> p (a d)"))
                    if h == 0:
                        ins.then_inc(s_tr, 1)
                    else:
                        ins.then_inc(once("qt"), 1)
                        b7 += 1
                        q1_ready = b7
                elif step[0] == "MX":
                    _, h, i = step
                    n, g = max_no(h, i), h // HPG
                    if n == 0:
                        pe.wait_ge(s_trf, first["q"] + 2)
                        pe.wait_ge(once("k1"), ST)
                        pe.wait_ge(once("cmpdone"), GROUPS)
                        pe.wait_ge(s_masks, 3)
                    elif n % ST == 0:
                        pe.wait_ge(once("b7"), q1_ready)
                    lhs = q1[h % 2][:, P * i:P * i + P]
                    if n >= 1:
                        pe.wait_ge(once("msr"), n)
                    for s0 in range(0, i + 1, 4):
                        s1 = min(s0 + 4, i + 1)
                        mm(slc_max[:, P * s0:P * s1], lhs, k1[0][:, g, P * s0:P * s1], True, s1 != i + 1)
                    mm(slc_max[:, P * i:P * i + P], identb[:, :], maskb[:, 0, :], False, True).then_inc(once("ms"), 1)
                elif step[0] == "MW":
                    _, h, i = step
                    n, g = max_no(h, i), h // HPG
                    lhs = q1[h % 2][:, P * i:P * i + P]
                    buf = other_max(h, i)
                    if h == 0:
                        pe.wait_ge(once("k1"), ST + i + 1)
                        if i == 0:
                            pe.wait_ge(s_evd, read_count(reads_d, len(unit_list) - 2))
                        if i >= 2:
                            pe.wait_ge(once("mwr"), i - 1)
                        elif i == 1:
                            pe.wait_ge(once("msr"), ST)
                    else:
                        pe.wait_ge(once("mwr"), n)
                    j0 = max(0, i - WIN_TILES)
                    cnt = i + 1 - j0
                    for s0 in range(0, cnt, 4):
                        s1 = min(s0 + 4, cnt)
                        mm(buf[:, P * s0:P * s1], lhs, k1[1][:, g, P * (j0 + s0):P * (j0 + s1)], True, False)
                    if i >= WIN_TILES:
                        mm(buf[:, 0:P], identb[:, :], maskb[:, 1, :], False, True)
                    mm(buf[:, P * (cnt - 1):P * cnt], identb[:, :], maskb[:, 0, :], False, True)
                    mm(buf[:, 640:704], lhs, k1c[:, g, 0, :], True, False)
                    mm(buf[:, 640:704], identb[:, :], cmpq[:, i, :], False, True).then_inc(once("mw"), 1)
                elif step[0] == "MM":
                    h, hf = step[1:]
                    pe.wait_ge(once("mcat"), 2 * (h + 1))
                    pe.wait_ge(once("qlo"), h + 1)
                    pe.wait_ge(once("b7"), b7)
                    for q in range(4):
                        ins = tr(bank[7][0:NQ2, P * q:P * q + P], qc2[:, 4 * hf + q, :])
                    ins.then_inc(once("mt"), 1)
                    b7 += 1
                    q2_ready = b7
                elif step[0] == "S":
                    e = step[1]
                    h, u = divmod(e, NU)
                    g = h // HPG
                    br, cc, j, lo, hi_, dg, bd = units[u]
                    if u == 0:
                        pe.wait_ge(once("b7"), q2_ready)
                    if e >= 2:
                        pe.wait_ge(once("exp"), 2 * (e - 1))
                    n = hi_ - lo
                    o = bank[e % 2][:, 0:n]
                    ks = slice(P * j, P * j + P)
                    mm(o, K1(br, g, ks), q1[h % 2][:, lo:hi_], True, False)
                    ins = mm(o, K2(br, g, ks), q2[h % 2][0:NQ2, lo:hi_], False, not (dg or bd or br == 0))
                    if br == 0:
                        ins = mm(o, identb[:, :], cmpt[:, lo:hi_], False, True)
                    if dg:
                        ins = mm(o[:, 0:P], maskb[:, 0, :], identb[:, :], False, not bd)
                    if bd:
                        ins = mm(o[:, n - P:n], maskb[:, 1, :], identb[:, :], False, True)
                    ins.then_inc(once("score"), 1)
                elif step[0] == "V":
                    e = step[1]
                    h, u = divmod(e, NU)
                    g = h // HPG
                    br, cc, j, lo, hi_, dg, bd = units[u]
                    is_first = u == 0 or units[u - 1][0:2] != (br, cc)
                    is_last = u == NU - 1 or units[u + 1][0:2] != (br, cc)
                    n = 6 * h + 2 * br + cc
                    if is_first and n >= 1:
                        pe.wait_ge(once("osb"), n)
                    if br == 0:
                        pe.wait_ge(once("plo_cmp"), 2 * h + u + 1)
                    else:
                        pe.wait_ge(once("plo"), (NU - 2) * h + u - 1)
                    out_t = lambda rows: bank[6][0:rows, lo - HALF * cc:hi_ - HALF * cc]
                    w = phi[e % NPT][:, 0:hi_ - lo]
                    if br == 0:
                        mm(out_t(HD + 1), vchi[:, g, 0:HD + 1], w, True, False)
                        ins = mm(out_t(HD + 1), vclo[:, g, 0:HD + 1], w, False, True)
                    else:
                        v = vhi[br - 1][:, j, g, 0:HD + 1]
                        mm(out_t(HD + 1), v, w, is_first, False)
                        mm(out_t(HD), vlo[br - 1][:, j, g, :], w, False, False)
                        ins = mm(out_t(HD + 1), v, plo[e % NPT][:, 0:hi_ - lo], False, is_last)
                    ins.then_inc(once("pv"), 1)
                elif step[0] == "N":
                    n = step[1]
                    pe.wait_ge(once("osb"), n + 1)
                    pe.wait_ge(once("b7"), b7)
                    for q in range(4):
                        ins = tr(bank[7][:, VW * q:VW * q + HD + 1], osb[n % 2][:, P * q:P * q + P], HD + 1)
                    ins.then_inc(once("ot"), 1)
                    b7 += 1

            for m in range(2 * ST + 1):
                b, i = divmod(m, ST)
                if m >= EARLY:
                    attention_step(("MX", 0, m - EARLY))
                if m == 2 * ST:
                    attention_step(("MW", 0, 0))
                if m < 2 * ST:
                    w = (KS_, KW_)[b]
                    if i == 0:
                        pe.wait_ge(s_whi, w + 1)
                        pe.wait_ge(s_wlo, w + 1)
                    wh, wl = whi[w % 2], wlo[w % 2]
                    n = unit_no[(w, i)]
                    bank_free(n)
                    ts = slice(P * i, P * i + P)
                    three(unit_bank(n)[:, 0:256],
                          [(ht_hi[:, k, ts], ht_lo[:, k, ts], wh[:, k, 0:256], wl[:, k, 0:256])
                           for k in range(KT)]).then_inc(s_unit, 1)
                if m == ST + 1:
                    attention_step(("MQ", 0, 0))
                    attention_step(("MQ", 0, 1))
                if m >= 1:
                    n = key_fill(m - 1)
                    pe.wait_ge(once("klo"), m)
                    fill_free(n)
                    for g in range(GROUPS):
                        ins = tr(bank[n % 2][:, P * g:P * g + P],
                                 f(kcat[(m - 1) % 2][:, g, :, :]).rearrange("p a d -> p (a d)"))
                    ins.then_inc(s_tr, 1)
            attention_step(("MX", 0, ST - 1))

            pe.wait_ge(s_evd, read_count(reads_d, len(unit_list)))
            pe.wait_ge(s_eva, read_count(reads_a, len(unit_list)))
            for step in plan:
                if step == ("MM", 0, 0):
                    pe.wait_ge(s_trf, first["kw"] + ST)
                    pe.wait_ge(once("k2aug"), 2)
                if step == ("N", 6 * HEADS - 1):
                    pe.wait_ge(once("mwr"), ST * HEADS)
                    pe.wait_ge(once("exp"), 2 * HEADS * NU)
                    for n in range(6):
                        b, hf = divmod(n, 2)
                        pe.wait_ge(once("az"), b + 1)
                        for q in range(4):
                            ins = tr(bank[n][:, P * q:P * q + P], qa[:, b, 4 * hf + q, :])
                        ins.then_inc(once("att"), 1)
                attention_step(step)

            pe.wait_ge(once("b7"), b7)
            for n in range(6, 8):
                b, hf = divmod(n, 2)
                pe.wait_ge(once("azl"), hf + 1)
                for q in range(4):
                    ins = tr(bank[n][:, P * q:P * q + P], qa[:, b, 4 * hf + q, :])
                ins.then_inc(once("att"), 1)
            for nb in range(KT):
                for kind in range(2):
                    n = 2 * nb + kind
                    wh, wl = dhi[n % 2], dlo[n % 2]
                    pe.wait_ge(once("dhi"), n + 1)
                    pe.wait_ge(once("dlo"), n + 1)
                    bh, bl, kp = (at_hi, at_lo, 4) if kind == 0 else (so_hi, so_lo, 2)

                    def project_part():
                        for cc in range(NC_HALF):
                            m = 2 * n + cc
                            ts = slice(cc * HALF, (cc + 1) * HALF)
                            if m >= 4:
                                pe.wait_ge(once("dmul"), m - 3)
                            three(bank[2 * (m % 4) + 1],
                                  [(wh[:, KT + k, :], wl[:, KT + k, :], bh[:, k, ts], bl[:, k, ts])
                                   for k in range(kp)]).then_inc(once("dproj"), 1)

                    def gate_part():
                        for cc in range(NC_HALF):
                            m = 2 * n + cc
                            ts = slice(cc * HALF, (cc + 1) * HALF)
                            three(bank[2 * (m % 4)],
                                  [(wh[:, k, :], wl[:, k, :], ht_hi[:, k, ts], ht_lo[:, k, ts])
                                   for k in range(KT)]).then_inc(once("dgate"), 1)

                    if n == 0:
                        pe.wait_ge(once("atlo"), 3)
                        gate_part()
                        pe.wait_ge(once("atlo"), 8)
                        project_part()
                    else:
                        if n == 1:
                            pe.wait_ge(once("sosplit"), 2)
                        project_part()
                        gate_part()

            pe.wait_ge(once("gacc"), 1)
            pe.wait_ge(once("dmul"), 4 * KT - 1)
            for hf in range(2):
                ins = mm(bank[4 + hf], onesq[:, :], gacc[:, HALF * hf:HALF * hf + HALF], True, True)
            ins.then_inc(once("gps"), 1)
            for i in range(ST):
                pe.wait_ge(once("mhi"), i + 1)
                pe.wait_ge(once("mlo"), i + 1)
                if i >= 2:
                    pe.wait_ge(once("oread"), 2 * i - 2)
                m0 = 0
                for k in range(KT):
                    if i == 0:
                        pe.wait_ge(once("ohi"), k + 1)
                        pe.wait_ge(once("olo"), k + 1)
                    for hf in range(2):
                        s = slice(HALF * hf, HALF * hf + HALF)
                        o = bank[2 * (i % 2) + hf]
                        mh, ml = mhi[i % 2][:, k, :], mlo[i % 2][:, k, :]
                        for q, (l, r) in enumerate(((mh, ohi), (mh, olo), (ml, ohi))):
                            ins = mm(o, l, r[:, k, s], k == 0 and q == 0, k == KT - 1 and q == 2)
                        if k == KT - 1:
                            ins.then_inc(once("ounit"), 1)


_INS = ["x", "c", "w_ada", "b_ada", "norm_gain", "w_in", "pe_cmp_k", "w_cmp_k1", "b_cmp_k1", "w_cmp_k2",
        "pe_cmp_v", "w_cmp_v1", "b_cmp_v1", "w_cmp_v2", "lam_re", "lam_im", "log_dt", "b_re", "b_im",
        "c_re", "c_im", "d_skip", "w_glu", "w_proj_attn", "w_proj_ssm", "w_out", "final_gain"]


def kernel(**inputs):
    import concourse.bacc as bacc
    from concourse.bass_utils import run_bass_kernel_spmd

    nc = bacc.Bacc("TRN2", target_bir_lowering=False, num_devices=1)
    arrays, args = {}, {}
    for name, a in list(((n, inputs[n]) for n in _INS)) + list(shape_tables().items()):
        a = np.ascontiguousarray(a)
        arrays[f"in_{name}"] = a
        args[name] = nc.dram_tensor(f"in_{name}", a.shape, mybir.dt.from_np(a.dtype), kind="ExternalInput").ap()
    out = nc.dram_tensor("out", (1, SEQ, D_MODEL), mybir.dt.float32, kind="ExternalOutput").ap()
    build(nc, out=out, **args)
    r = run_bass_kernel_spmd(nc, [arrays], core_ids=[0])
    return np.asarray(r.results[0]["out"])
```
